# Optimizing a Trainium2 kernel written in Bass

```python
import math
import jax
import jax.numpy as jnp
from jax import lax
import numpy as np

D_MODEL = 1024
BATCH = 1
SEQ = 256
DEPTH = 2

N_MEM = 256
BLOCK_Q = 128
EPS = 1e-6
ROPE_THETA = 10000.0

DA_HEADS = 4
DA_DIM = 64
DA_QK = DA_HEADS * 2 * DA_DIM
DA_V = DA_HEADS * 2 * DA_DIM
SB_HEADS = 4
SB_DIM = 128
SB_W = SB_HEADS * SB_DIM
GD_HEADS = 4
GD_DIM = 128
GD_W = GD_HEADS * GD_DIM
GD_CONV = 4
GD_CHUNK = 64
N_BRANCH = 3
IN_SPLITS = (DA_QK, DA_QK, DA_V, SB_W, SB_W, SB_W, GD_W, GD_W, GD_W, GD_W, GD_HEADS, GD_HEADS, N_BRANCH * D_MODEL)
D_IN = 2 * DA_QK + DA_V + 3 * SB_W + 4 * GD_W + 2 * GD_HEADS + N_BRANCH * D_MODEL
X_HEADS = 4
X_DIM = 128
X_W = X_HEADS * X_DIM
D_FF_DENSE = 2816
N_EXPERTS = 8
TOP_K = 2
D_FF_EXPERT = 3584
N_DENSE_LAYERS = (DEPTH + 1) // 2
N_MOE_LAYERS = DEPTH // 2

kernel_name = 'hybrid_diff_stickbreak_deltanet_moe'

def rmsnorm(x, g):
    xf = x.astype(jnp.float32)
    y = xf * lax.rsqrt(jnp.mean(xf * xf, axis=-1, keepdims=True) + EPS)
    return (y * g.astype(jnp.float32)).astype(x.dtype)

def l2norm(x):
    return x * lax.rsqrt(jnp.sum(x * x, axis=-1, keepdims=True) + EPS)

def rope_tables(seq, dim):
    inv_freq = 1.0 / (ROPE_THETA ** (jnp.arange(0, dim, 2, dtype=jnp.float32) / dim))
    ang = jnp.arange(seq, dtype=jnp.float32)[:, None] * inv_freq[None, :]
    return jnp.cos(ang), jnp.sin(ang)

def apply_rope(t, cos, sin):
    t1, t2 = jnp.split(t, 2, axis=-1)
    c, s = cos.astype(t.dtype), sin.astype(t.dtype)
    return jnp.concatenate([t1 * c - t2 * s, t2 * c + t1 * s], axis=-1)

def to_heads(t, n_heads):
    b, s, w = t.shape
    return t.reshape(b, s, n_heads, w // n_heads).transpose(0, 2, 1, 3)

def from_heads(t):
    b, h, s, d = t.shape
    return t.transpose(0, 2, 1, 3).reshape(b, s, h * d)

def causal_depthwise_conv(t, w):
    ch = t.shape[-1]
    return lax.conv_general_dilated(t, w[:, None, :].astype(t.dtype), window_strides=(1,),
                                    padding=[(GD_CONV - 1, 0)],
                                    dimension_numbers=('NWC', 'WIO', 'NWC'),
                                    feature_group_count=ch)

def swiglu(h, w_gate, w_up, w_down):
    return (jax.nn.silu(h @ w_gate) * (h @ w_up)) @ w_down

def diff_attention(q, k, v, lam, subln, lam_init, cos, sin):
    b, s, _ = q.shape
    q = q.reshape(b, s, DA_HEADS, 2, DA_DIM).transpose(0, 2, 3, 1, 4)
    k = k.reshape(b, s, DA_HEADS, 2, DA_DIM).transpose(0, 2, 3, 1, 4)
    q = apply_rope(q, cos, sin) * DA_DIM ** -0.5
    k = apply_rope(k, cos, sin)
    v = to_heads(v, DA_HEADS)
    outs = []
    for i in range(s // BLOCK_Q):
        lo, hi = i * BLOCK_Q, (i + 1) * BLOCK_Q
        sc = jnp.einsum('bhcqd,bhckd->bhcqk', q[:, :, :, lo:hi], k[:, :, :, :hi]).astype(jnp.float32)
        causal = jnp.arange(hi)[None, :] <= jnp.arange(lo, hi)[:, None]
        p = jax.nn.softmax(jnp.where(causal, sc, -jnp.inf), axis=-1)
        attn = (p[:, :, 0] - lam * p[:, :, 1]).astype(v.dtype)
        outs.append(jnp.einsum('bhqk,bhkd->bhqd', attn, v[:, :, :hi]))
    o = rmsnorm(jnp.concatenate(outs, axis=2), subln) * (1.0 - lam_init)
    return from_heads(o)

def stick_breaking_attention(q, k, v):
    q = to_heads(q, SB_HEADS) * SB_DIM ** -0.5
    k = to_heads(k, SB_HEADS)
    v = to_heads(v, SB_HEADS)
    s = q.shape[2]
    outs = []
    for i in range(s // BLOCK_Q):
        lo, hi = i * BLOCK_Q, (i + 1) * BLOCK_Q
        z = jnp.einsum('bhqd,bhkd->bhqk', q[:, :, lo:hi], k[:, :, :hi]).astype(jnp.float32)
        strict = jnp.arange(hi)[None, :] < jnp.arange(lo, hi)[:, None]
        log_fail = jnp.where(strict, jax.nn.log_sigmoid(-z), 0.0)
        log_remain = lax.cumsum(log_fail, axis=3, reverse=True) - log_fail
        attn = jnp.where(strict, jnp.exp(jax.nn.log_sigmoid(z) + log_remain), 0.0)
        outs.append(jnp.einsum('bhqk,bhkd->bhqd', attn.astype(v.dtype), v[:, :, :hi]))
    return from_heads(jnp.concatenate(outs, axis=2))

def gated_deltanet(q, k, v, z, a, bg, conv_w, a_log, dt_bias, norm_g):
    dtype = q.dtype
    f32 = jnp.float32
    qkv = jax.nn.silu(causal_depthwise_conv(jnp.concatenate([q, k, v], axis=-1), conv_w))
    q, k, v = jnp.split(qkv, 3, axis=-1)
    q = l2norm(to_heads(q, GD_HEADS).astype(f32)) * GD_DIM ** -0.5
    k = l2norm(to_heads(k, GD_HEADS).astype(f32))
    v = to_heads(v, GD_HEADS).astype(f32)
    g = -jnp.exp(a_log.astype(f32))[:, None] * jax.nn.softplus(a.astype(f32).transpose(0, 2, 1) + dt_bias.astype(f32)[:, None])
    beta = jax.nn.sigmoid(bg.astype(f32)).transpose(0, 2, 1)
    b, h, s, d = q.shape
    nc = s // GD_CHUNK

    def chunk(t):
        return t.reshape(b, h, nc, GD_CHUNK, *t.shape[3:])

    qc, kc, vc, bc = chunk(q), chunk(k), chunk(v), chunk(beta)
    gc = lax.cumsum(chunk(g), axis=3)
    tril = jnp.tril(jnp.ones((GD_CHUNK, GD_CHUNK), dtype=bool))
    strict = jnp.tril(jnp.ones((GD_CHUNK, GD_CHUNK), dtype=bool), k=-1)
    diff = gc[..., :, None] - gc[..., None, :]
    decay = jnp.where(tril, jnp.exp(jnp.where(tril, diff, 0.0)), 0.0)
    kb = kc * bc[..., None]
    vb = vc * bc[..., None]
    lmat = jnp.where(strict, jnp.einsum('bhnid,bhnjd->bhnij', kb, kc) * decay, 0.0)
    eye = jnp.eye(GD_CHUNK, dtype=f32)
    tmat = lax.linalg.triangular_solve(eye + lmat, jnp.broadcast_to(eye, lmat.shape),
                                       left_side=True, lower=True, unit_diagonal=True)
    u = tmat @ vb
    w = tmat @ (kb * jnp.exp(gc)[..., None])
    intra = jnp.where(tril, jnp.einsum('bhnid,bhnjd->bhnij', qc, kc) * decay, 0.0)

    def step(state, xs):
        qi, ki, ui, wi, ai, gi = xs
        v_new = ui - wi @ state
        out = (qi * jnp.exp(gi)[..., None]) @ state + ai @ v_new
        g_last = gi[..., -1]
        state = state * jnp.exp(g_last)[..., None, None] + jnp.einsum(
            'bhcd,bhce->bhde', ki * jnp.exp(g_last[..., None] - gi)[..., None], v_new)
        return state, out

    xs = tuple(jnp.moveaxis(t, 2, 0) for t in (qc, kc, u, w, intra, gc))
    _, o = lax.scan(step, jnp.zeros((b, h, d, d), f32), xs)
    o = jnp.moveaxis(o, 0, 2).reshape(b, h, s, d)
    o = rmsnorm(o, norm_g) * jax.nn.silu(to_heads(z, GD_HEADS).astype(f32))
    return from_heads(o).astype(dtype)

def hybrid_mixer(h, w_in, gd_conv, lam_q1, lam_k1, lam_q2, lam_k2, da_subln, gd_a_log, gd_dt_bias,
                 gd_norm, w_br_a, w_br_b, w_br_c, w_out, lam_init, cos, sin):
    cuts = [int(c) for c in np.cumsum(IN_SPLITS)[:-1]]
    (da_q, da_k, da_v, sb_q, sb_k, sb_v, gd_q, gd_k, gd_v, gd_z, gd_a, gd_b, gates) = jnp.split(h @ w_in, cuts, axis=-1)
    f32 = jnp.float32
    lam = (jnp.exp(jnp.sum(lam_q1.astype(f32) * lam_k1.astype(f32)))
           - jnp.exp(jnp.sum(lam_q2.astype(f32) * lam_k2.astype(f32))) + lam_init)
    o_a = diff_attention(da_q, da_k, da_v, lam, da_subln, lam_init, cos, sin)
    o_b = stick_breaking_attention(sb_q, sb_k, sb_v)
    o_c = gated_deltanet(gd_q, gd_k, gd_v, gd_z, gd_a, gd_b, gd_conv, gd_a_log, gd_dt_bias, gd_norm)
    g_a, g_b, g_c = jnp.split(jax.nn.sigmoid(gates), 3, axis=-1)
    merged = g_a * (o_a @ w_br_a) + g_b * (o_b @ w_br_b) + g_c * (o_c @ w_br_c)
    return merged @ w_out

def memory_cross_attention(h, mem_n, w_q, w_kv, w_o):
    q = to_heads(h @ w_q, X_HEADS) * X_DIM ** -0.5
    k, v = jnp.split(mem_n @ w_kv, 2, axis=-1)
    k, v = to_heads(k, X_HEADS), to_heads(v, X_HEADS)
    b, nh, s, d = q.shape
    qb = q.reshape(b, nh, s // BLOCK_Q, BLOCK_Q, d).transpose(2, 0, 1, 3, 4)

    def block(qi):
        p = jax.nn.softmax(jnp.einsum('bhqd,bhmd->bhqm', qi, k).astype(jnp.float32), axis=-1)
        return jnp.einsum('bhqm,bhmd->bhqd', p.astype(v.dtype), v)

    o = lax.map(block, qb).transpose(1, 2, 0, 3, 4).reshape(b, nh, s, d)
    return from_heads(o) @ w_o

def moe_swiglu(h, w_router, w_gate, w_up, w_down):
    b, s, d = h.shape
    t = h.reshape(b * s, d)
    logits = (t @ w_router).astype(jnp.float32)
    top_val, top_idx = lax.top_k(logits, TOP_K)
    top_w = jax.nn.softmax(top_val, axis=-1)
    combine = jnp.sum(jax.nn.one_hot(top_idx, N_EXPERTS, dtype=jnp.float32) * top_w[..., None], axis=1)
    y = jnp.zeros_like(t)
    for e in range(N_EXPERTS):
        y = y + combine[:, e:e + 1].astype(t.dtype) * swiglu(t, w_gate[e], w_up[e], w_down[e])
    return y.reshape(b, s, d)

def setup_inputs(seed: int = 0) -> dict:
    key = jax.random.key(seed)
    counter = [0]

    def nk():
        counter[0] += 1
        return jax.random.fold_in(key, counter[0])

    def nrm(shape, scale):
        return jax.random.normal(nk(), shape, jnp.float32) * scale

    def gain(shape):
        return 1.0 + 0.01 * jax.random.normal(nk(), shape, jnp.float32)

    dt = jnp.exp(jax.random.uniform(nk(), (DEPTH, GD_HEADS), jnp.float32, math.log(0.001), math.log(0.1)))
    return {
        'x': nrm((BATCH, SEQ, D_MODEL), 1.0),
        'mem': nrm((BATCH, N_MEM, D_MODEL), 1.0),
        'norm_mix': gain((DEPTH, D_MODEL)),
        'w_in': nrm((DEPTH, D_MODEL, D_IN), D_MODEL ** -0.5),
        'gd_conv': nrm((DEPTH, GD_CONV, 3 * GD_W), GD_CONV ** -0.5),
        'lam_q1': nrm((DEPTH, DA_DIM), 0.1),
        'lam_k1': nrm((DEPTH, DA_DIM), 0.1),
        'lam_q2': nrm((DEPTH, DA_DIM), 0.1),
        'lam_k2': nrm((DEPTH, DA_DIM), 0.1),
        'da_subln': gain((DEPTH, 2 * DA_DIM)),
        'gd_a_log': jnp.log(jax.random.uniform(nk(), (DEPTH, GD_HEADS), jnp.float32, 1.0, 16.0)),
        'gd_dt_bias': dt + jnp.log(-jnp.expm1(-dt)),
        'gd_norm': gain((DEPTH, GD_DIM)),
        'w_br_a': nrm((DEPTH, DA_V, D_MODEL), DA_V ** -0.5),
        'w_br_b': nrm((DEPTH, SB_W, D_MODEL), SB_W ** -0.5),
        'w_br_c': nrm((DEPTH, GD_W, D_MODEL), GD_W ** -0.5),
        'w_out': nrm((DEPTH, D_MODEL, D_MODEL), D_MODEL ** -0.5),
        'norm_x': gain((DEPTH, D_MODEL)),
        'norm_mem': gain((DEPTH, D_MODEL)),
        'w_q_x': nrm((DEPTH, D_MODEL, X_W), D_MODEL ** -0.5),
        'w_kv_x': nrm((DEPTH, D_MODEL, 2 * X_W), D_MODEL ** -0.5),
        'w_o_x': nrm((DEPTH, X_W, D_MODEL), X_W ** -0.5),
        'norm_ffn': gain((DEPTH, D_MODEL)),
        'w_gate_dense': nrm((N_DENSE_LAYERS, D_MODEL, D_FF_DENSE), D_MODEL ** -0.5),
        'w_up_dense': nrm((N_DENSE_LAYERS, D_MODEL, D_FF_DENSE), D_MODEL ** -0.5),
        'w_down_dense': nrm((N_DENSE_LAYERS, D_FF_DENSE, D_MODEL), D_FF_DENSE ** -0.5),
        'w_router': nrm((N_MOE_LAYERS, D_MODEL, N_EXPERTS), D_MODEL ** -0.5),
        'w_gate_exp': nrm((N_MOE_LAYERS, N_EXPERTS, D_MODEL, D_FF_EXPERT), D_MODEL ** -0.5),
        'w_up_exp': nrm((N_MOE_LAYERS, N_EXPERTS, D_MODEL, D_FF_EXPERT), D_MODEL ** -0.5),
        'w_down_exp': nrm((N_MOE_LAYERS, N_EXPERTS, D_FF_EXPERT, D_MODEL), D_FF_EXPERT ** -0.5),
        'norm_final': gain((D_MODEL,)),
    }

def reference(x, mem, norm_mix, w_in, gd_conv, lam_q1, lam_k1, lam_q2, lam_k2, da_subln, gd_a_log,
              gd_dt_bias, gd_norm, w_br_a, w_br_b, w_br_c, w_out, norm_x, norm_mem, w_q_x, w_kv_x,
              w_o_x, norm_ffn, w_gate_dense, w_up_dense, w_down_dense, w_router, w_gate_exp,
              w_up_exp, w_down_exp, norm_final):
    cos, sin = rope_tables(x.shape[1], DA_DIM)
    for l in range(DEPTH):
        lam_init = 0.8 - 0.6 * math.exp(-0.3 * l)
        x = x + hybrid_mixer(rmsnorm(x, norm_mix[l]), w_in[l], gd_conv[l], lam_q1[l], lam_k1[l],
                             lam_q2[l], lam_k2[l], da_subln[l], gd_a_log[l], gd_dt_bias[l], gd_norm[l],
                             w_br_a[l], w_br_b[l], w_br_c[l], w_out[l], lam_init, cos, sin)
        x = x + memory_cross_attention(rmsnorm(x, norm_x[l]), rmsnorm(mem, norm_mem[l]),
                                       w_q_x[l], w_kv_x[l], w_o_x[l])
        h = rmsnorm(x, norm_ffn[l])
        if l % 2 == 0:
            x = x + swiglu(h, w_gate_dense[l // 2], w_up_dense[l // 2], w_down_dense[l // 2])
        else:
            x = x + moe_swiglu(h, w_router[l // 2], w_gate_exp[l // 2], w_up_exp[l // 2], w_down_exp[l // 2])
    return rmsnorm(x, norm_final)


_drawn_inputs = setup_inputs


def setup_inputs(seed=0):
    import zlib

    import numpy as np

    out = dict(_drawn_inputs(seed))
    spreads = {}
    factors = {'norm_mix': 2.728,
     'lam_q2': 3.138,
     'da_subln': 3.421,
     'gd_norm': 3.216,
     'norm_x': 5.087,
     'norm_mem': 5.035,
     'norm_final': 33.682,
     'norm_ffn': 8.0}
    for name, (base, spread) in spreads.items():
        noise = np.random.default_rng([zlib.crc32(name.encode()), seed]).standard_normal(out[name].shape)
        drawn = base * np.exp(spread * noise) if base else spread * noise
        out[name] = jnp.asarray(drawn.astype(out[name].dtype))
    for name, factor in factors.items():
        out[name] = (out[name] * factor).astype(out[name].dtype)
    return out
```

```python
from contextlib import ExitStack

import numpy as np
import concourse.bass as bass
from concourse import mybir

F32 = mybir.dt.float32
I32 = mybir.dt.int32
U32 = mybir.dt.uint32
ALU = mybir.AluOpType
ACT = mybir.ActivationFunctionType
X = mybir.AxisListType.X

P = 128
D = 1024
SEQ = 256
NB = SEQ // P
KT = D // P
DEPTH = 2
H = 4
W = 512
DA_DIM = 64
SB_DIM = 128
N_EXP = 8
FF_DENSE = 2816
FF_EXP = 3584
CAP = 128
EPS = 1e-6
NEG = -1e30
CHUNK = 4096
RING = 3
GD0 = 6 * W
AB0 = 10 * W
GATE0 = 10 * W + 2 * H
LAM_INIT = [0.8 - 0.6 * float(np.exp(-0.3 * layer)) for layer in range(DEPTH)]
LEVELS = [1, 2, 4, 8, 16, 32, 64]

CONST = {}
_at = 0
for _name, _n in [("ident", P), ("triu", P), ("striu", P), ("ones", SEQ), ("causal", SEQ), ("strict_neg", SEQ),
                  ("strict01", SEQ), ("level", 7 * P), ("levelT", 7 * P), ("cos_q", 2 * DA_DIM), ("sin_q", 2 * DA_DIM),
                  ("cos_k", 2 * DA_DIM), ("sin_k", 2 * DA_DIM), ("iota", P), ("nhalf", 16), ("iota8", 8)]:
    CONST[_name] = (_at, _n)
    _at += _n
N_CONST = _at

CHUNKS = ["gd_q", "gd_k", "gd_v", "gd_z", "da_q", "da_k", "da_v", "sb_q", "sb_k", "sb_v",
          "gate_a0", "gate_a1", "br_a", "gate_b0", "gate_b1", "br_b", "gate_c0", "gate_c1", "br_c",
          "out0", "out1", "x_k", "x_v", "x_q", "x_o"]
COLUMN = {"da_q": 0, "da_k": W, "da_v": 2 * W, "sb_q": 3 * W, "sb_k": 4 * W, "sb_v": 5 * W,
          "gd_q": GD0, "gd_k": GD0 + W, "gd_v": GD0 + 2 * W, "gd_z": GD0 + 3 * W}
for _i, _g in enumerate("abc"):
    COLUMN[f"gate_{_g}0"] = GATE0 + _i * D
    COLUMN[f"gate_{_g}1"] = GATE0 + _i * D + W

UNITS = {}
for _c in CHUNKS:
    _eng = "dve" if _c in ("da_q", "da_k", "out0", "out1") or _c[:2] == "br" or _c == "x_o" else "act"
    _kind = "tok" if _c in ("gd_z", "da_q", "da_k", "da_v", "sb_v", "x_v", "out0", "out1", "x_o") else "T"
    if _c[:2] == "br" or _c == "x_o":
        UNITS[_c + ".0"] = (_c, _kind, H, 0, _eng)
        UNITS[_c + ".1"] = (_c, _kind, H, W, _eng)
    else:
        UNITS[_c] = (_c, _kind, KT, 0, _eng)
UNIT_NO = {u: i for i, u in enumerate(UNITS)}
N_UNITS = len(UNITS)

ORDER = ["norm_mix", "gd_q", "gd_k", "conv_q", "gd_v", "conv_k", "gd_z", "ab", "da_q", "conv_v", "da_k", "gd_tok", "da_v",
         "gd_gate", "sb_q", "gd_scale", "sb_k", "gd_T", "da_T", "gd_LA", "sb_v", "da_att0", "da_att1",
         "gd_inv", "da_out", "gate_a0", "gate_a1", "br_a.0", "br_a.1", "sb_att0", "sb_att1", "gate_b0", "gate_b1",
         "br_b.0", "br_b.1", "gd_scan", "gate_c0", "gate_c1", "gd_out", "br_c.0", "br_c.1", "norm_mem", "out0", "out1",
         "x_k", "x_v", "norm_x", "x_q", "x_att0", "x_att1", "x_o.0", "x_o.1", "norm_ffn", "ffn"]
NORM_NO = {"norm_mix": 0, "norm_mem": 1, "norm_x": 2, "norm_ffn": 3}


def chunk_no(layer, name):
    return layer * (len(CHUNKS) + 17) + CHUNKS.index(name)


FFN0 = len(CHUNKS)
MOE0 = 2 * len(CHUNKS) + 17
assert FF_DENSE == 11 * SEQ and FF_EXP == 14 * SEQ


def hybrid_layers(nc, t, out):
    ctx = ExitStack()
    with ctx:
        def sb(name, shape, dt=F32):
            return ctx.enter_context(nc.sbuf_tensor(name, shape, dt))

        sems = {}

        def sem(name):
            if name not in sems:
                sems[name] = ctx.enter_context(nc.semaphore(name))
            return sems[name]

        const = sb("const", [P, N_CONST])
        ring = sb("ring", [P, RING, CHUNK])
        x = sb("x", [P, NB, D])
        xn = sb("xn", [P, NB, D])
        hT = sb("hT", [P, KT, SEQ])
        work = sb("work", [P, 25, 1024])
        conv_in = sb("conv_in", [P, 12, SEQ + 3])
        gain = sb("gain", [P, 68 + 96])
        gain_rows = conv_in
        w_ab = sb("w_ab", [P, DEPTH, KT, 8])
        w_router = sb("w_router", [P, KT, N_EXP])
        lam_e = sb("lam_e", [P, 2, DEPTH])
        neg_lam = sb("neg_lam", [P, DEPTH])
        a_log = sb("a_log", [P, DEPTH * H])
        dt_bias = sb("dt_bias", [P, DEPTH * H])
        neg_a = sb("neg_a", [P, DEPTH * H])
        ss = sb("ss", [P, NB])
        s16 = sb("s16", [P, 10, 16])
        s16b = sb("s16b", [P, 8, 8])
        pow_in = sb("pow_in", [P, 16])
        pow_out = sb("pow_out", [P, 16])
        top = sb("top", [P, 18, 16])
        top_i = sb("top_i", [P, NB, 8], U32)
        overflow = sb("overflow", [P, 1], I32)

        def c(name, a=0, b=None):
            at, n = CONST[name]
            return const[:, at + a:at + (n if b is None else b)]

        def v3(ap, a):
            return ap.rearrange("p (a b) -> p a b", a=a)

        def tile(i, n=1):
            return work[:, i:i + n, :].rearrange("p a b -> p (a b)")

        W0, W1, W2, W3 = (tile(i) for i in range(4))
        lam_in = v3(W0[:, 0:4 * DEPTH * DA_DIM], 4)
        W01, W23 = tile(0, 2), tile(2, 2)
        da_qT, da_kT, da_v, oaT = tile(4), tile(5), tile(6), tile(7)
        mergedT = tile(4, 2)
        sb_qT, sb_kT, sb_v, obT, ocT = (tile(i) for i in range(8, 13))
        x_qT, x_kT, x_v, oxT = sb_qT, sb_kT, sb_v, oaT
        conv_out = tile(13, 3)
        knT, kbT, qnT = tile(13), tile(14), tile(15)
        memT = tile(13, 2)
        m1 = qnT
        tm = tile(16, 3)
        qn, kn, vb = tile(16), tile(17), tile(18)
        kb = uT = tile(19)
        decayT, intraT, scratch, qgT_wT, state_kbg = (tile(i) for i in range(20, 25))
        z = sb("z", [P, 1024])
        v_new, gd_o = scratch, decayT
        qgT, wT = qgT_wT[:, 0:W], qgT_wT[:, W:]
        state, kbg = state_kbg[:, 0:W], state_kbg[:, W:]
        conv_flat = conv_in[:, :, :].rearrange("p a b -> p (a b)")
        lT, l_, t_ = (conv_flat[:, 1024 * i:1024 * (i + 1)] for i in range(3))
        bT = scratch
        silu_g = [tile(0)[:, 0:W], tile(0)[:, W:]]
        hid = [tile(1)[:, 0:W], tile(1)[:, W:]]
        hgT, y_tok, select, selectT = tile(2), tile(3), tile(4)[:, 0:NB * CAP], tile(5)[:, 0:SEQ]

        psum = ctx.enter_context(nc.psum_tensor("psum", [P, 8, 512], F32))

        def pb(first, n=1):
            return psum[:, first:first + n, :].rearrange("p a b -> p (a b)")

        def bc(ap, shape):
            return ap.to_broadcast(shape)

        def rep(ap, n):
            return ap.unsqueeze(1).to_broadcast([P, n, ap.shape[1]])

        def each(ap, m):
            return ap.unsqueeze(2).to_broadcast([P, ap.shape[1], m])

        block = ctx.enter_context(nc.Block())

        def arrived(eng, n, extra=0):
            eng.wait_ge(sem(f"chunk_in{n % RING}"), 32 * (n // RING + 1) + extra)

        def unit_index(layer, u):
            return layer * N_UNITS + UNIT_NO[u]

        def unit_names():
            return [(layer, u) for layer in range(DEPTH) for u in UNITS]

        def wait_evacuated(eng, g):
            eng_name = UNITS[unit_names()[g][1]][4]
            n = sum(UNITS[u][4] == eng_name for _, u in unit_names()[:g + 1])
            eng.wait_ge(sem(f"unit_out_{eng_name}"), n)

        def unit_banks(layer, u):
            return 2 * (unit_index(layer, u) % 2)

        @block.sync
        def _(sp):
            S = slice
            wi = t["w_in"]
            sp.dma_start(x[:, :, :], t["x"][0].rearrange("(b p) d -> p b d", p=P)).then_inc(sem("x_in"), 16)

            def free(n):
                old = n - RING
                if old < 0:
                    return
                if FFN0 <= old < FFN0 + 17:
                    j = old - FFN0
                    last_down = {14: 10, 16: 11}
                    if j in last_down:
                        sp.wait_ge(sem("down_done"), last_down[j])
                    elif j == 15:
                        sp.wait_ge(sem("gate_up_done"), 11)
                    elif j % 3 == 2:
                        sp.wait_ge(sem("down_done"), 2 * (j // 3) + 2)
                    else:
                        sp.wait_ge(sem("gate_up_done"), 2 * (j // 3) + j % 3 + 1)
                else:
                    layer, i = (0, old) if old < FFN0 else (1, old - FFN0 - 17)
                    last_unit = [u for u in UNITS if UNITS[u][0] == CHUNKS[i]][-1]
                    sp.wait_ge(sem("unit_done"), unit_index(layer, last_unit) + 1)

            def load(n, dst, src):
                sp.dma_start(dst, src).then_inc(sem(f"chunk_in{n % RING}"), 16)

            def chunk(n, view, rows, cols):
                src = view.rearrange("(k p) n -> p k n", p=P)
                k = rows // P
                dst = ring[:, n % RING, 0:k * cols].rearrange("p (k n) -> p k n", k=k)
                for i in range(2):
                    load(n, dst[:, i * k // 2:(i + 1) * k // 2, :], src[:, i * k // 2:(i + 1) * k // 2, :])

            def gate_up(n, gate, up):
                dst = ring[:, n % RING, :].rearrange("p (k a n) -> p k a n", k=KT, a=2)
                load(n, dst[:, :, 0, :], gate.rearrange("(k p) n -> p k n", p=P))
                load(n, dst[:, :, 1, :], up.rearrange("(k p) n -> p k n", p=P))

            def experts(base, group0):
                with sp.Fori(0, N_EXP) as e:
                    with sp.Fori(0, 7) as p:
                        for j in range(3):
                            if j == 2:
                                sp.wait_ge(sem("down_done"), group0 + 14 * e + 2 * p)
                                chunk(base + j, t["w_down_exp"][0, bass.ds(e, 1), bass.ds(p * 512, 512), :]
                                      .rearrange("e k n -> (e k) n"), W, D)
                            else:
                                sp.wait_ge(sem("gate_up_done"), group0 + 14 * e + 2 * p + j - 1)
                                cols = bass.ds(p * 512 + j * 256, 256)
                                gate_up(base + j,
                                        t["w_gate_exp"][0, bass.ds(e, 1), :, cols].rearrange("e k n -> (e k) n"),
                                        t["w_up_exp"][0, bass.ds(e, 1), :, cols].rearrange("e k n -> (e k) n"))

            for layer in range(DEPTH):
                for name in CHUNKS:
                    n = chunk_no(layer, name)
                    free(n)
                    if name in COLUMN:
                        chunk(n, wi[layer, :, COLUMN[name]:COLUMN[name] + W], D, W)
                    elif name[:3] == "out":
                        i = int(name[3])
                        chunk(n, t["w_out"][layer, :, i * W:(i + 1) * W], D, W)
                    elif name[:2] == "br":
                        chunk(n, t["w_br_" + name[3]][layer], W, D)
                    elif name == "x_q":
                        chunk(n, t["w_q_x"][layer], D, W)
                    elif name in ("x_k", "x_v"):
                        i = int(name == "x_v")
                        chunk(n, t["w_kv_x"][layer, :, i * W:(i + 1) * W], D, W)
                    else:
                        chunk(n, t["w_o_x"][layer], W, D)
                    if name == "br_a":
                        sp.wait_ge(sem("norm_transposed"), 2 * (4 * layer) + 2)
                        sp.dma_start(xn[:, :, :], t["mem"][0].rearrange("(b p) d -> p b d", p=P)) \
                          .then_inc(sem("mem_in"), 16)
                if layer == 0:
                    for p in range(6):
                        for j in range(2 if p < 5 else 1):
                            n = FFN0 + 3 * p + j
                            free(n)
                            cols = slice(p * 512 + j * 256, p * 512 + j * 256 + 256)
                            gate_up(n, t["w_gate_dense"][0, :, cols], t["w_up_dense"][0, :, cols])
                        rows = 4 * P if p < 5 else 2 * P
                        n = FFN0 + 3 * p + (2 if p < 5 else 1)
                        free(n)
                        chunk(n, t["w_down_dense"][0, p * 512:p * 512 + rows, :], rows, D)
                else:
                    for j in range(RING):
                        free(MOE0 + j)
                    experts(MOE0, 11)
                    sp.wait_ge(sem("overflow_known"), 1)
                    with sp.If(sp.value_load(overflow[0:1, 0:1], min_val=0, max_val=1) > 0):
                        experts(MOE0 + 21 * N_EXP, 11 + 14 * N_EXP)
            sp.wait_ge(sem("out_ready"), 1)
            sp.dma_start(out[0].rearrange("(b p) d -> p b d", p=P), xn[:, :, :]).then_inc(sem("out_stored"), 16)
            sp.wait_ge(sem("out_stored"), 16)

        @block.tensor
        def _(pe):
            ident = c("ident")

            def mm(o, a, b, start=True, stop=True):
                return nc.tensor.matmul(o, a, b, start=start, stop=stop)

            def tr(o, a):
                return nc.tensor.transpose(o, a, ident)

            source = {"x_k": memT, "x_v": memT, "out0": mergedT, "out1": mergedT, "br_a": oaT, "br_b": obT,
                      "br_c": ocT, "x_o": oxT}

            def unit(layer, u):
                name, kind, k_tiles, col, _ = UNITS[u]
                g = unit_index(layer, u)
                n = chunk_no(layer, name)
                arrived(pe, n)
                if g >= 2:
                    wait_evacuated(pe, g - 2)
                if u == "gd_q":
                    pe.wait_ge(sem("norm_out"), 2 * (4 * layer) + 2)
                if u == "x_k":
                    pe.wait_ge(sem("norm_out"), 2 * (4 * layer + 1) + 2)
                if u == "x_q":
                    pe.wait_ge(sem("norm_out"), 2 * (4 * layer + 2) + 2)
                if u == "br_a.0":
                    pe.wait_ge(sem("oaT_ready"), layer + 1)
                if u == "br_b.0":
                    pe.wait_ge(sem("obT_ready"), NB * (layer + 1))
                if u == "br_c.0":
                    pe.wait_ge(sem("ocT_ready"), layer + 1)
                if u == "out0":
                    pe.wait_ge(sem("merged_ready"), layer + 1)
                if u == "x_o.0":
                    pe.wait_ge(sem("oxT_ready"), NB * (layer + 1))
                w = ring[:, n % RING, :].rearrange("p (k n) -> p k n", k=k_tiles)
                act = source[name] if name in source else hT[:, :, :].rearrange("p k n -> p (k n)")
                act = act.rearrange("p (k n) -> p k n", k=k_tiles)
                base = unit_banks(layer, u)
                if kind == "T":
                    for nt in range(4):
                        o = psum[:, base + nt // 2, (nt % 2) * SEQ:(nt % 2 + 1) * SEQ]
                        for k in range(k_tiles):
                            last = mm(o, w[:, k, col + nt * P:col + (nt + 1) * P], act[:, k, :], k == 0, k == k_tiles - 1)
                            if nt == 3 and k == k_tiles - 1:
                                last.then_inc(sem("unit_done"), 1)
                else:
                    for b in range(NB):
                        for k in range(k_tiles):
                            last = mm(psum[:, base + b, :], act[:, k, b * P:(b + 1) * P], w[:, k, col:col + W], k == 0,
                                      k == k_tiles - 1)
                            if b == 1 and k == k_tiles - 1:
                                last.then_inc(sem("unit_done"), 1)
                return n

            def norm(layer, s):
                i = 4 * layer + NORM_NO[s]
                pe.wait_ge(sem("xn_ready"), i + 1)
                for kt in range(KT):
                    for b in range(NB):
                        last = tr(psum[:, 4 + kt // 2, (kt % 2) * SEQ + b * P:(kt % 2) * SEQ + (b + 1) * P],
                                  xn[:, b, kt * P:(kt + 1) * P])
                    if kt % 4 == 3:
                        last.then_inc(sem("norm_transposed"), 1)

            def blocks_T(dst_bank, src, n=8):
                for s in range(n):
                    last = tr(pb(dst_bank, 2)[:, s * P:(s + 1) * P], src[:, s * P:(s + 1) * P])
                return last

            def heads_T(dst_bank, src):
                for h in range(H):
                    for b in range(NB):
                        last = tr(pb(dst_bank, 2)[:, h * SEQ + b * P:h * SEQ + (b + 1) * P],
                                  src[:, b * W + h * P:b * W + (h + 1) * P])
                return last

            def attend(layer, i, probs, tag, transposed_bank):
                wd = (i + 1) * P if tag != "x" else SEQ
                nk = wd // P
                pe.wait_ge(sem(f"{tag}_probs"), NB * layer + i + 1)
                for h in range(H):
                    for k in range(nk):
                        last = tr(pb(transposed_bank, 2)[:, (h * nk + k) * P:(h * nk + k + 1) * P],
                                  probs[:, h * wd + k * P:h * wd + (k + 1) * P])
                last.then_inc(sem(f"{tag}_probsT"), 1)
                pe.wait_ge(sem(f"{tag}_probsT_out"), NB * layer + i + 1)
                return nk

            def ffn(layer, wd, blocks, base, group0, exp=None):
                src = hT if exp is None else hgT.rearrange("p (k n) -> p k n", k=KT)
                pairs = 5 if exp is None else 7

                def gate_up(j, g, extra):
                    arrived(pe, j, 32 * extra)
                    if not isinstance(g, int) or g >= 2:
                        pe.wait_ge(sem("hidden_ready"), g - 1)
                    w = ring[:, j % RING, :].rearrange("p (k a n) -> p k a n", k=KT, a=2)
                    slot = 2 * (gpar[0] % 2)
                    gpar[0] += 1
                    for a in range(2):
                        for nt in range(2):
                            for k in range(KT):
                                last = mm(psum[:, slot + a, nt * wd:(nt + 1) * wd], w[:, k, a, nt * P:(nt + 1) * P],
                                          src[:, k, 0:wd], k == 0, k == KT - 1)
                    last.then_inc(sem("gate_up_done"), 1)

                def down(j, part, g, extra, first, last_group):
                    arrived(pe, j, 32 * extra)
                    pe.wait_ge(sem("hidden_ready"), g + 1)
                    w = ring[:, j % RING, :].rearrange("p (k n) -> p k n", k=4)
                    hv = hid[dpar[0] % 2][:, 0:2 * wd].rearrange("p (a n) -> p a n", a=2)
                    dpar[0] += 1
                    for ft in range(2):
                        for b in range(blocks):
                            for half in range(2):
                                last = mm(psum[:, 4 + 2 * b + half, :], hv[:, ft, b * P:(b + 1) * P],
                                          w[:, 2 * part + ft, half * W:(half + 1) * W],
                                          first and ft == 0, last_group and ft == 1)
                    last.then_inc(sem("down_done"), 1)

                gpar, dpar = [0], [0]
                e = 0 if exp is None else exp
                g0 = group0 + 14 * e

                def x7(p):
                    return 7 * e + p

                gate_up(base, g0, x7(0))
                gate_up(base + 1, g0 + 1, x7(0))
                down(base + 2, 0, g0, x7(0), True, False)
                with pe.Fori(1, pairs) as p:
                    gate_up(base, g0 + 2 * p, x7(p))
                    down(base + 2, 1, g0 + 2 * p - 1, x7(p) - 1, False, False)
                    gate_up(base + 1, g0 + 2 * p + 1, x7(p))
                    down(base + 2, 0, g0 + 2 * p, x7(p), False, False)
                if exp is None:
                    gate_up(base + 15, g0 + 10, 0)
                    down(base + 14, 1, g0 + 9, 0, False, False)
                    down(base + 16, 0, g0 + 10, 0, False, True)
                else:
                    down(base + 2, 1, g0 + 13, x7(6), False, True)

            def expert(base, group0, n0):
                with pe.Fori(0, N_EXP) as e:
                    pe.wait_ge(sem("select_ready"), n0 + e + 1)
                    pe.wait_ge(sem("x_added"), n0 + e + 1)
                    for kt in range(KT):
                        for b in range(NB):
                            last = mm(pb(0, 2)[:, kt * CAP:(kt + 1) * CAP], xn[:, b, kt * P:(kt + 1) * P],
                                      select[:, b * CAP:(b + 1) * CAP], b == 0, b == 1)
                    last.then_inc(sem("gathered"), 1)
                    for b in range(NB):
                        last = tr(psum[:, 2, b * P:(b + 1) * P], select[:, b * CAP:(b + 1) * CAP])
                    last.then_inc(sem("selectT_done"), 1)
                    pe.wait_ge(sem("gathered_out"), n0 + e + 1)
                    pe.wait_ge(sem("selectT_out"), n0 + e + 1)
                    ffn(1, CAP, 1, base, group0, e)
                    pe.wait_ge(sem("y_ready"), n0 + e + 1)
                    for b in range(NB):
                        for half in range(2):
                            last = mm(psum[:, 2 * b + half, :], selectT[:, b * P:(b + 1) * P],
                                      y_tok[:, half * W:(half + 1) * W])
                    last.then_inc(sem("scattered"), 1)

            pe.wait_ge(sem("const_in"), 16)
            pe.wait_ge(sem("rows_in"), 16 * 7)
            tr_rows = nc.tensor.transpose(psum[:, 4, 0:68], gain_rows[0:68, 0, 0:P], c("ident")[0:68, 0:68])
            tr_rows = nc.tensor.transpose(psum[:, 4, P:P + 96], gain_rows[0:96, 1, 0:P], c("ident")[0:96, 0:96])
            tr_rows.then_inc(sem("gains_transposed"), 1)

            for layer in range(DEPTH):
                for s in ORDER:
                    if s in UNITS:
                        unit(layer, s)
                    elif s in NORM_NO:
                        norm(layer, s)
                    elif s == "ab":
                        pe.wait_ge(sem("small_in"), 16 * 8)
                        for b in range(NB):
                            for k in range(KT):
                                last = mm(psum[:, 4, b * 8:(b + 1) * 8], hT[:, k, b * P:(b + 1) * P],
                                          w_ab[:, layer, k, :], k == 0, k == KT - 1)
                        last.then_inc(sem("ab_done"), 1)
                    elif s == "gd_tok":
                        for part in range(3):
                            pe.wait_ge(sem("conv_ready"), 3 * layer + part + 1)
                            if part == 2:
                                pe.wait_ge(sem("gd_tok_out"), 3 * layer + 1)
                            first = 6 if part == 1 else 4
                            if part == 0:
                                pe.wait_ge(sem("ab_out"), layer + 1)
                            for b in range(NB):
                                for h in range(H):
                                    last = tr(pb(first, 2)[:, b * W + h * P:b * W + (h + 1) * P],
                                              conv_out[:, part * 1024 + h * SEQ + b * P:part * 1024 + h * SEQ + (b + 1) * P])
                            last.then_inc(sem("gd_tok_done"), 1)
                    elif s == "gd_gate":
                        pe.wait_ge(sem("g_ready"), layer + 1)
                        pe.wait_ge(sem("gd_tok_out"), 3 * layer + 3)
                        mm(psum[:, 4, 0:8], c("triu"), s16[:, 0, 0:8]).then_inc(sem("gc_done"), 1)
                        for i in range(8):
                            last = mm(pb(6, 2)[:, i * P:(i + 1) * P], bc(s16[:, 0, i:i + 1], [P, P]), c("triu"))
                        last.then_inc(sem("gc_done"), 1)
                    elif s == "gd_T":
                        pe.wait_ge(sem("gd_scaled"), layer + 1)
                        blocks_T(4, kn).then_inc(sem("gd_T_done"), 1)
                        blocks_T(6, kb).then_inc(sem("gd_T_done"), 1)
                        pe.wait_ge(sem("gd_T_out"), 4 * layer + 1)
                        blocks_T(4, qn).then_inc(sem("gd_T_done"), 1)
                        pe.wait_ge(sem("qg_ready"), layer + 1)
                        pe.wait_ge(sem("gd_T_out"), 4 * layer + 2)
                        blocks_T(6, qn[:, W:], 4).then_inc(sem("gd_T_done"), 1)
                    elif s == "da_T":
                        pe.wait_ge(sem("gd_T_out"), 4 * layer + 4)
                        pe.wait_ge(sem("roped"), 2 * layer + 2)
                        heads_T(4, W0).then_inc(sem("da_T_done"), 1)
                        heads_T(6, W1).then_inc(sem("da_T_done"), 1)
                    elif s == "gd_LA":
                        pe.wait_ge(sem("da_T_out"), 2 * layer + 2)
                        for i in range(8):
                            q = slice(i * P, (i + 1) * P)
                            last = mm(pb(4, 2)[:, q], knT[:, q], kbT[:, q])
                        last.then_inc(sem("gd_LA_done"), 1)
                        for i in range(8):
                            q = slice(i * P, (i + 1) * P)
                            last = mm(pb(6, 2)[:, q], knT[:, q], qnT[:, q])
                        last.then_inc(sem("gd_LA_done"), 1)
                        pe.wait_ge(sem("lT_ready"), layer + 1)
                        blocks_T(4, lT).then_inc(sem("gd_LA_done"), 1)
                    elif s in ("da_att0", "da_att1"):
                        i = int(s[-1])
                        wd = (i + 1) * P
                        pe.wait_ge(sem("intra_ready"), layer + 1)
                        pe.wait_ge(sem("l_ready"), layer + 1)
                        if i:
                            pe.wait_ge(sem("da_o_out"), NB * layer + 1)
                        for half in range(2):
                            rows = slice(half * 64, half * 64 + 64)
                            for h in range(H):
                                last = mm(pb(4 + 2 * half, 2)[:, h * SEQ:h * SEQ + wd],
                                          da_qT[rows, h * SEQ + i * P:h * SEQ + (i + 1) * P],
                                          da_kT[rows, h * SEQ:h * SEQ + wd])
                        last.then_inc(sem("da_scores"), 1)
                        nk = attend(layer, i, W23, "da", 4)
                        arr = W0
                        for h in range(H):
                            for k in range(nk):
                                last = mm(psum[:, 6, h * P:(h + 1) * P], arr[:, (h * nk + k) * P:(h * nk + k + 1) * P],
                                          da_v[:, k * W + h * P:k * W + (h + 1) * P], k == 0, k == nk - 1)
                        last.then_inc(sem("da_o_done"), 1)
                    elif s == "gd_inv":
                        pe.wait_ge(sem("da_o_out"), NB * layer + 2)
                        with pe.Fori(0, 6) as it:
                            n = 6 * layer + it
                            pe.wait_ge(sem("bT_ready"), n + 1)
                            pe.wait_ge(sem("tu_ready"), 2 * n + 2 * layer + 2)
                            for i in range(8):
                                q = slice(i * P, (i + 1) * P)
                                last = mm(pb(4, 2)[:, q], bT[:, q], t_[:, q])
                            last.then_inc(sem("m1_done"), 1)
                            pe.wait_ge(sem("m1_out"), n + 1)
                            for i in range(8):
                                q = slice(i * P, (i + 1) * P)
                                last = mm(pb(6, 2)[:, q], uT[:, q], m1[:, q])
                            last.then_inc(sem("tmu_done"), 1)
                            for i in range(8):
                                q = slice(i * P, (i + 1) * P)
                                last = mm(pb(4, 2)[:, q], m1[:, q], uT[:, q])
                            last.then_inc(sem("tmu_done"), 1)
                    elif s == "da_out":
                        pe.wait_ge(sem("da_normed"), layer + 1)
                        pe.wait_ge(sem("tu_ready"), 14 * layer + 14)
                        heads_T(4, W1).then_inc(sem("da_oT_done"), 1)
                    elif s in ("sb_att0", "sb_att1"):
                        i = int(s[-1])
                        wd = (i + 1) * P
                        pe.wait_ge(sem("oaT_ready"), layer + 1)
                        if i:
                            pe.wait_ge(sem("obT_ready"), NB * layer + 1)
                        for h in range(H):
                            last = mm(pb(4, 2)[:, h * wd:(h + 1) * wd], sb_qT[:, h * SEQ + i * P:h * SEQ + (i + 1) * P],
                                      sb_kT[:, h * SEQ:h * SEQ + wd])
                        last.then_inc(sem("sb_scores"), 1)
                        nk = attend(layer, i, W2, "sb", 4)
                        for h in range(H):
                            for k in range(nk):
                                last = mm(psum[:, 6, h * P:(h + 1) * P], sb_v[:, k * W + h * P:k * W + (h + 1) * P],
                                          W0[:, (h * nk + k) * P:(h * nk + k + 1) * P], k == 0, k == nk - 1)
                        last.then_inc(sem("sb_oT_done"), 1)
                    elif s == "gd_scan":
                        pe.wait_ge(sem("kd_ready"), layer + 1)
                        pe.wait_ge(sem("obT_ready"), NB * layer + 2)
                        for h in range(H):
                            q = slice(h * P, (h + 1) * P)
                            last = mm(psum[:, 4, q], uT[:, q], vb[:, q])
                        last.then_inc(sem("scan_done"), 1)
                        for h in range(H):
                            q = slice(h * P, (h + 1) * P)
                            last = mm(psum[:, 5, q], kbg[:, q], uT[:, W + h * P:W + (h + 1) * P])
                        last.then_inc(sem("scan_done"), 1)
                        pe.wait_ge(sem("scan_out_act"), 2 * layer + 1)
                        for h in range(H):
                            q = slice(h * P, (h + 1) * P)
                            last = mm(psum[:, 6, q], kn[:, q], v_new[:, q])
                        last.then_inc(sem("scan_done"), 1)
                        for h in range(H):
                            q = slice(h * P, (h + 1) * P)
                            last = mm(psum[:, 7, q], intraT[:, q], v_new[:, q])
                        last.then_inc(sem("scan_done"), 1)
                        pe.wait_ge(sem("scan_out_dve"), 4 * layer + 2)
                        for h in range(H):
                            q, q1 = slice(h * P, (h + 1) * P), slice(W + h * P, W + (h + 1) * P)
                            mm(psum[:, 4, q], uT[:, q1], vb[:, q1], True, False)
                            last = mm(psum[:, 4, q], wT[:, q], state[:, q], False, True)
                        last.then_inc(sem("scan_done"), 1)
                        pe.wait_ge(sem("scan_out_act"), 2 * layer + 2)
                        for h in range(H):
                            q, q1 = slice(h * P, (h + 1) * P), slice(W + h * P, W + (h + 1) * P)
                            mm(psum[:, 5, q], qgT[:, q], state[:, q], True, False)
                            last = mm(psum[:, 5, q], intraT[:, q1], v_new[:, q1], False, True)
                        last.then_inc(sem("scan_done"), 1)
                    elif s == "gd_out":
                        pe.wait_ge(sem("gd_normed"), layer + 1)
                        heads_T(6, gd_o).then_inc(sem("gd_oT_done"), 1)
                    elif s in ("x_att0", "x_att1"):
                        i = int(s[-1])
                        if i == 0:
                            wait_evacuated(pe, unit_index(layer, "x_q"))
                        else:
                            pe.wait_ge(sem("oxT_ready"), NB * layer + 1)
                        for h in range(H):
                            last = mm(pb(4, 2)[:, h * SEQ:(h + 1) * SEQ], x_qT[:, h * SEQ + i * P:h * SEQ + (i + 1) * P],
                                      x_kT[:, h * SEQ:(h + 1) * SEQ])
                        last.then_inc(sem("x_scores"), 1)
                        nk = attend(layer, i, W2, "x", 6)
                        for h in range(H):
                            for k in range(nk):
                                last = mm(psum[:, 4, h * P:(h + 1) * P], x_v[:, k * W + h * P:k * W + (h + 1) * P],
                                          W0[:, (h * nk + k) * P:(h * nk + k + 1) * P], k == 0, k == nk - 1)
                        last.then_inc(sem("x_oT_done"), 1)
                    elif s == "ffn":
                        pe.wait_ge(sem("norm_out"), 2 * (4 * layer + 3) + 2)
                        if layer == 0:
                            ffn(0, SEQ, NB, FFN0, 0)
                        else:
                            for b in range(NB):
                                for k in range(KT):
                                    last = mm(psum[:, 4, b * 8:(b + 1) * 8], hT[:, k, b * P:(b + 1) * P], w_router[:, k, :],
                                              k == 0, k == KT - 1)
                            last.then_inc(sem("router_done"), 1)
                            pe.wait_ge(sem("chosen_ready"), 1)
                            chosen = top[:, 0, :]
                            mm(psum[:, 5, 0:8], c("striu"), chosen[:, 0:8])
                            mm(psum[:, 5, 8:16], c("ones", 0, P), chosen[:, 0:8], True, False)
                            mm(psum[:, 5, 8:16], c("striu"), chosen[:, 8:16], False, True)
                            mm(psum[:, 5, 16:24], c("ones", 0, P), chosen[:, 0:8], True, False)
                            mm(psum[:, 5, 16:24], c("ones", 0, P), chosen[:, 8:16], False, True) \
                                .then_inc(sem("ranks_done"), 1)
                            expert(MOE0, 11, 0)
                            pe.wait_ge(sem("overflow_known"), 1)
                            with pe.If(pe.value_load(overflow[0:1, 0:1], min_val=0, max_val=1) > 0):
                                expert(MOE0 + 21 * N_EXP, 11 + 14 * N_EXP, N_EXP)

        POW = [(layer, s) for layer in range(DEPTH) for s in ORDER
               if s in NORM_NO or s in ("gd_scale", "da_out", "gd_out")] + [(DEPTH, "final")]

        def pow_width(s):
            return {"gd_scale": 16, "da_out": 8, "gd_out": 8}.get(s, NB)

        @block.gpsimd
        def _(pool):
            pool.wait_ge(sem("const_in"), 16)
            for i, (layer, s) in enumerate(POW):
                n = pow_width(s)
                pool.wait_ge(sem("pow_in"), i + 1)
                nc.gpsimd.tensor_tensor(pow_out[:, 0:n], pow_in[:, 0:n], c("nhalf", 0, n), ALU.pow) \
                    .then_inc(sem("pow_out"), 1)

        @block.scalar
        def _(act):
            steps = [0]

            def step(ins):
                steps[0] += 1
                ins.then_inc(sem("act_step"), 1)
                act.wait_ge(sem("act_step"), steps[0])

            def f(o, i, func, **kw):
                return nc.scalar.activation(o, i, func, **kw)

            def copy(o, i):
                return nc.scalar.activation(o, i, ACT.Copy)

            for dst, src in [(gain_rows[0:16, 0, 0:P], t["norm_mix"]), (gain_rows[16:32, 0, 0:P], t["norm_mem"]),
                             (gain_rows[32:48, 0, 0:P], t["norm_x"]), (gain_rows[48:64, 0, 0:P], t["norm_ffn"])]:
                act.dma_start(dst, src.rearrange("l (k p) -> (l k) p", p=P)).then_inc(sem("rows_in"), 16)
            act.dma_start(gain_rows[64:66, 0, 0:P], t["da_subln"]).then_inc(sem("rows_in"), 16)
            act.dma_start(gain_rows[66:68, 0, 0:P], t["gd_norm"]).then_inc(sem("rows_in"), 16)
            act.dma_start(gain_rows[0:96, 1, 0:P], t["gd_conv"].rearrange("l j (c p) -> (l j c) p", p=P)) \
               .then_inc(sem("rows_in"), 16)
            act.dma_start(const[:, :], t["const"]).then_inc(sem("const_in"), 16)
            for i, name in enumerate(("lam_q1", "lam_k1", "lam_q2", "lam_k2")):
                act.dma_start(lam_in[:, i, :], t[name].rearrange("l d -> (l d)").partition_broadcast(P)) \
                   .then_inc(sem("small_in"), 16)
            act.dma_start(a_log[:, :], t["gd_a_log"].rearrange("l h -> (l h)").partition_broadcast(P)) \
               .then_inc(sem("small_in"), 16)
            act.dma_start(dt_bias[:, :], t["gd_dt_bias"].rearrange("l h -> (l h)").partition_broadcast(P)) \
               .then_inc(sem("small_in"), 16)
            act.dma_start(w_ab[:, :, :, :].rearrange("p l k n -> p (l k) n"),
                          t["w_in"][:, :, AB0:AB0 + 8].rearrange("l (k p) n -> p (l k) n", p=P)).then_inc(sem("small_in"), 16)
            act.dma_start(w_router[:, :, :], t["w_router"][0].rearrange("(k p) n -> p k n", p=P)) \
               .then_inc(sem("small_in"), 16)
            nc.scalar.preload_act_table_set("natural_log_exp_and_others")
            act.wait_ge(sem("small_in"), 16 * 8)
            f(neg_a[:, :], a_log[:, :], ACT.Exp).then_inc(sem("init_act"), 1)
            act.wait_ge(sem("lam_dots"), 1)
            f(lam_e[:, :, :], lam_e[:, :, :], ACT.Exp).then_inc(sem("init_act"), 1)

            def norm_squares(layer, s):
                i = 4 * layer + NORM_NO.get(s, 0)
                src, junk = x, [xn[:, 0, :], xn[:, 1, :]]
                if s == "norm_mem":
                    src, junk = xn, [W0, W1]
                    act.wait_ge(sem("mem_in"), 16 * (layer + 1))
                    act.wait_ge(sem("obT_ready"), NB * (layer + 1))
                elif s == "norm_mix":
                    if layer == 0:
                        act.wait_ge(sem("x_in"), 16)
                    else:
                        act.wait_ge(sem("ffn_added"), 1)
                elif s != "final":
                    wait_evacuated(act, unit_index(layer, "out1" if s == "norm_x" else "x_o.1"))
                if i and s != "norm_mem":
                    act.wait_ge(sem("norm_transposed"), 2 * i)
                for b in range(NB):
                    last = f(junk[b], src[:, b, :], ACT.Square, accum_out=ss[:, b:b + 1])
                last.then_inc(sem("squares_ready"), 1)

            def ffn(group0, wd, exp=None):
                def silu(par, g):
                    act.wait_ge(sem("gate_up_done"), g + 1)
                    f(silu_g[par][:, 0:2 * wd], psum[:, 2 * par, 0:2 * wd], ACT.Silu).then_inc(sem("silu_ready"), 1)

                if exp is None:
                    with act.Fori(0, 5) as p:
                        silu(0, group0 + 2 * p)
                        silu(1, group0 + 2 * p + 1)
                    silu(0, group0 + 10)
                else:
                    with act.Fori(0, 7) as p:
                        silu(0, group0 + 14 * exp + 2 * p)
                        silu(1, group0 + 14 * exp + 2 * p + 1)

            def expert(group0, n0):
                with act.Fori(0, N_EXP) as e:
                    act.wait_ge(sem("selectT_done"), n0 + e + 1)
                    copy(selectT[:, :], psum[:, 2, 0:SEQ]).then_inc(sem("selectT_out"), 1)
                    ffn(group0, CAP, e)
                    act.wait_ge(sem("down_done"), group0 + 14 * e + 14)
                    copy(y_tok[:, :], pb(4, 2)).then_inc(sem("y_ready"), 1)

            target = {"gd_z": z[:, :], "da_v": da_v, "sb_k": sb_kT, "sb_v": sb_v, "x_k": x_kT, "x_v": x_v}

            for layer in range(DEPTH):
                for s in ORDER:
                    if s in UNITS and UNITS[s][4] == "act":
                        act.wait_ge(sem("unit_done"), unit_index(layer, s) + 1)
                        src = pb(unit_banks(layer, s), 2)
                        done = sem("unit_out_act")
                        if s in ("gd_q", "gd_k", "gd_v"):
                            if s == "gd_q":
                                act.wait_ge(sem("pads_ready"), layer + 1)
                            part = ("gd_q", "gd_k", "gd_v").index(s)
                            f(conv_in[:, 4 * part:4 * part + 4, 3:], v3(src, 4), ACT.Copy).then_inc(done, 1)
                        elif s in ("sb_q", "x_q"):
                            f(sb_qT, src, ACT.Copy, scale=float(SB_DIM) ** -0.5).then_inc(done, 1)
                        elif s[:4] == "gate":
                            if s == "gate_a0":
                                act.wait_ge(sem("da_probsT"), NB * (layer + 1))
                            elif s == "gate_b0":
                                act.wait_ge(sem("obT_ready"), NB * (layer + 1))
                            elif s == "gate_c0":
                                wait_evacuated(act, unit_index(layer, "br_b.1"))
                                act.wait_ge(sem("merged_b"), layer + 1)
                            f(W2 if s[-1] == "0" else W3, src, ACT.Sigmoid).then_inc(done, 1)
                        else:
                            copy(target[s], src).then_inc(done, 1)
                    elif s in NORM_NO:
                        norm_squares(layer, s)
                    elif s[:5] == "conv_":
                        part = "qkv".index(s[5])
                        n = 3 * layer + part
                        act.wait_ge(sem("conv_taps"), n + 1)
                        if part:
                            act.wait_ge(sem("conv_ready"), n)
                        f(scratch, conv_out[:, part * 1024:(part + 1) * 1024], ACT.Sigmoid).then_inc(sem("conv_sig"), 1)
                    elif s == "gd_tok":
                        for part in range(3):
                            act.wait_ge(sem("gd_tok_done"), 3 * layer + part + 1)
                            copy(tile(16 + part), pb(6 if part == 1 else 4, 2)).then_inc(sem("gd_tok_out"), 1)
                    elif s == "gd_gate":
                        act.wait_ge(sem("ab_out"), layer + 1)
                        nc.scalar.preload_act_table_set("natural_log_exp_and_others")
                        step(f(s16[:, 5, 0:8], s16[:, 4, 0:8], ACT.Exp, scale=-1.0))
                        step(f(s16[:, 2, 0:8], s16[:, 1, 0:8], ACT.Abs))
                        step(f(s16[:, 2, 0:8], s16[:, 2, 0:8], ACT.Exp, scale=-1.0))
                        f(s16[:, 3, 0:8], s16[:, 2, 0:8], ACT.Ln, bias=c("ones", 0, 1)).then_inc(sem("gates_act"), 1)
                    elif s == "gd_scale":
                        act.wait_ge(sem("decay_logs"), layer + 1)
                        f(decayT, decayT, ACT.Exp)
                        f(s16[:, 8, 8:16], s16[:, 8, 0:8], ACT.Exp)
                        f(s16[:, 9, 8:16], s16[:, 9, 0:8], ACT.Exp).then_inc(sem("decay_exp"), 1)
                    elif s == "gd_T":
                        for i, dst in enumerate((knT, kbT, qnT, qgT)):
                            act.wait_ge(sem("gd_T_done"), 4 * layer + i + 1)
                            copy(dst, pb(4 + 2 * (i % 2), 1 if i == 3 else 2)).then_inc(sem("gd_T_out"), 1)
                    elif s == "da_T":
                        for i, dst in enumerate((da_qT, da_kT)):
                            act.wait_ge(sem("da_T_done"), 2 * layer + i + 1)
                            copy(dst, pb(4 + 2 * i, 2)).then_inc(sem("da_T_out"), 1)
                    elif s == "gd_LA":
                        act.wait_ge(sem("gd_LA_done"), 3 * layer + 3)
                        copy(l_, pb(4, 2)).then_inc(sem("l_ready"), 1)
                    elif s == "gd_inv":
                        with act.Fori(0, 6) as it:
                            n = 6 * layer + it
                            act.wait_ge(sem("m1_done"), n + 1)
                            copy(m1, pb(4, 2)).then_inc(sem("m1_out"), 1)
                    elif s[:6] == "da_att":
                        i = int(s[-1])
                        wd = (i + 1) * P
                        act.wait_ge(sem("da_max"), NB * layer + i + 1)
                        for j in range(8):
                            p = W23[:, j * wd:(j + 1) * wd]
                            last = f(p, p, ACT.Exp, bias=s16b[:, 1, j:j + 1], accum_out=s16b[:, 2, j:j + 1])
                        last.then_inc(sem("da_exp"), 1)
                        act.wait_ge(sem("da_probsT"), NB * layer + i + 1)
                        copy(W0[:, 0:4 * wd], pb(4, 2)[:, 0:4 * wd]).then_inc(sem("da_probsT_out"), 1)
                    elif s[:6] == "sb_att":
                        i = int(s[-1])
                        wd = (i + 1) * P
                        p = W2[:, 0:4 * wd]
                        act.wait_ge(sem("sb_scores"), NB * layer + i + 1)
                        wait_evacuated(act, unit_index(layer, "br_a.1"))
                        nc.scalar.preload_act_table_set("natural_log_exp_and_others")
                        step(f(p, pb(4, 2)[:, 0:4 * wd], ACT.Abs))
                        step(f(p, p, ACT.Exp, scale=-1.0))
                        f(p, p, ACT.Ln, bias=c("ones", 0, 1)).then_inc(sem("sb_ln"), 1)
                        act.wait_ge(sem("sb_log"), NB * layer + i + 1)
                        f(p, W3[:, 0:4 * wd], ACT.Exp).then_inc(sem("sb_probs"), 1)
                        act.wait_ge(sem("sb_probsT"), NB * layer + i + 1)
                        copy(W0[:, 0:4 * wd], pb(4, 2)[:, 0:4 * wd]).then_inc(sem("sb_probsT_out"), 1)
                    elif s[:5] == "x_att":
                        i = int(s[-1])
                        act.wait_ge(sem("x_max"), NB * layer + i + 1)
                        for j in range(H):
                            last = f(W2[:, j * SEQ:(j + 1) * SEQ], pb(4, 2)[:, j * SEQ:(j + 1) * SEQ], ACT.Exp,
                                     bias=s16b[:, 4, j:j + 1], accum_out=s16b[:, 5, j:j + 1])
                        last.then_inc(sem("x_exp"), 1)
                        act.wait_ge(sem("x_probsT"), NB * layer + i + 1)
                        copy(W0, pb(6, 2)).then_inc(sem("x_probsT_out"), 1)
                    elif s == "gd_scan":
                        for i, n in enumerate((1, 5)):
                            act.wait_ge(sem("scan_done"), 6 * layer + n)
                            copy(v_new[:, i * W:(i + 1) * W], psum[:, 4, :]).then_inc(sem("scan_out_act"), 1)
                    elif s == "gd_out":
                        act.wait_ge(sem("tu_ready"), 14 * (layer + 1))
                        f(l_, z[:, :], ACT.Sigmoid).then_inc(sem("z_sig"), 1)
                    elif s == "ffn":
                        if layer == 0:
                            ffn(0, SEQ)
                        else:
                            act.wait_ge(sem("norm_out"), 2 * (4 * layer + 3) + 2)
                            act.dma_start(da_v, t["norm_final"].partition_broadcast(P)).then_inc(sem("gain_row_in"), 16)
                            act.wait_ge(sem("top_diff"), 1)
                            f(top[:, 11, 0:2], top[:, 10, 0:2], ACT.Exp).then_inc(sem("top_exp"), 1)
                            expert(11, 0)
                            act.wait_ge(sem("overflow_known"), 1)
                            with act.If(act.value_load(overflow[0:1, 0:1], min_val=0, max_val=1) > 0):
                                expert(11 + 14 * N_EXP, N_EXP)
                                act.wait_ge(sem("x_added"), 2 * N_EXP + 1)
            act.wait_ge(sem("x_added"), N_EXP + 1)
            norm_squares(DEPTH, "final")

        @block.vector
        def _(dve):
            v = nc.vector
            steps = [0]

            def step(ins):
                steps[0] += 1
                ins.then_inc(sem("dve_step"), 1)
                dve.wait_ge(sem("dve_step"), steps[0])

            def tt(o, a, b, op):
                return v.tensor_tensor(o, a, b, op)

            def power(layer, s, src, width, scale):
                i = POW.index((layer, s))
                v.tensor_scalar(pow_in[:, 0:width], src, scale, EPS, ALU.mult, ALU.add).then_inc(sem("pow_in"), 1)
                dve.wait_ge(sem("pow_out"), i + 1)

            def norm_scale(layer, s):
                i = 4 * layer + NORM_NO.get(s, 0)
                dve.wait_ge(sem("squares_ready"), i + 1)
                power(layer, s, ss[:, :], NB, 1.0 / D)
                src = xn if s == "norm_mem" else x
                for b in range(NB):
                    last = v.tensor_scalar(xn[:, b, :], src[:, b, :], pow_out[:, b:b + 1], None, ALU.mult)
                return last

            def norm(layer, s):
                i = 4 * layer + NORM_NO[s]
                norm_scale(layer, s).then_inc(sem("xn_ready"), 1)
                which = ("norm_mix", "norm_mem", "norm_x", "norm_ffn").index(s)
                g = gain[:, which * 16 + layer * 8:which * 16 + layer * 8 + 8]
                dst = memT if s == "norm_mem" else hT[:, :, :].rearrange("p k n -> p (k n)")
                for j in range(2):
                    dve.wait_ge(sem("norm_transposed"), 2 * i + j + 1)
                    tt(v3(dst[:, j * 1024:(j + 1) * 1024], 4), v3(pb(4 + 2 * j, 2), 4), each(g[:, 4 * j:4 * j + 4], SEQ),
                       ALU.mult).then_inc(sem("norm_out"), 1)

            def conv(layer, part):
                n = 3 * layer + part
                wait_evacuated(dve, unit_index(layer, ("gd_q", "gd_k", "gd_v")[part]))
                for j in range(4):
                    for ch in range(4 * part, 4 * part + 4):
                        tap = gain[:, 68 + layer * 48 + j * 12 + ch:68 + layer * 48 + j * 12 + ch + 1]
                        o = conv_out[:, ch * SEQ:(ch + 1) * SEQ]
                        src = conv_in[:, ch, j:j + SEQ]
                        if j == 0:
                            last = v.tensor_scalar(o, src, tap, None, ALU.mult)
                        else:
                            last = v.scalar_tensor_tensor(o, src, tap, o, ALU.mult, ALU.add)
                    if j < 3:
                        step(last)
                last.then_inc(sem("conv_taps"), 1)
                o = conv_out[:, part * 1024:(part + 1) * 1024]
                dve.wait_ge(sem("conv_sig"), n + 1)
                tt(o, o, scratch, ALU.mult).then_inc(sem("conv_ready"), 1)

            def rope(layer, s):
                tab = s[3]
                dst = W0 if tab == "q" else W1
                src = pb(unit_banks(layer, s), 2)
                dve.wait_ge(sem("unit_done"), unit_index(layer, s) + 1)
                sin = W2
                for b in range(NB):
                    cs = c("cos_" + tab, b * DA_DIM, (b + 1) * DA_DIM)
                    sn = c("sin_" + tab, b * DA_DIM, (b + 1) * DA_DIM)
                    part = src[:, b * W:(b + 1) * W]
                    tt(v3(dst[:, b * W:(b + 1) * W], 8), v3(part, 8), rep(cs, 8), ALU.mult)
                    for half in range(2):
                        o = v3(sin[:, b * W:(b + 1) * W], 8)[:, :, half * 32:half * 32 + 32]
                        i = v3(part, 8)[:, :, (1 - half) * 32:(1 - half) * 32 + 32]
                        last = tt(o, i, rep(sn[:, half * 32:half * 32 + 32], 8), ALU.mult)
                last.then_inc(sem("unit_out_dve"), 1)
                wait_evacuated(dve, unit_index(layer, s))
                tt(dst, dst, sin[:, :], ALU.add).then_inc(sem("roped"), 1)

            def ffn(group0, wd, exp=None):
                def hidden(par, g, slot_used=True):
                    dve.wait_ge(sem("silu_ready"), g + 1)
                    if slot_used:
                        dve.wait_ge(sem("down_done"), g - 1)
                    tt(hid[par][:, 0:2 * wd], silu_g[par][:, 0:2 * wd], psum[:, 2 * par + 1, 0:2 * wd], ALU.mult) \
                        .then_inc(sem("hidden_ready"), 1)

                if exp is None:
                    hidden(0, 0, False)
                    hidden(1, 1, False)
                    with dve.Fori(1, 5) as p:
                        hidden(0, 2 * p)
                        hidden(1, 2 * p + 1)
                    hidden(0, 10)
                else:
                    with dve.Fori(0, 7) as p:
                        hidden(0, group0 + 14 * exp + 2 * p)
                        hidden(1, group0 + 14 * exp + 2 * p + 1)

            def expert(group0, n0, ranks):
                with dve.Fori(0, N_EXP) as e:
                    for b in range(NB):
                        last = v.tensor_scalar(select[:, b * CAP:(b + 1) * CAP], c("iota"),
                                               top[:, ranks, bass.ds(b * 8 + e, 1)], None, ALU.is_equal)
                    last.then_inc(sem("select_ready"), 1)
                    dve.wait_ge(sem("gathered"), n0 + e + 1)
                    tt(v3(hgT, KT), v3(pb(0, 2), KT), each(gain[:, 48 + 8:48 + 16], CAP), ALU.mult) \
                        .then_inc(sem("gathered_out"), 1)
                    ffn(group0, CAP, e)
                    dve.wait_ge(sem("scattered"), n0 + e + 1)
                    for b in range(NB):
                        last = v.scalar_tensor_tensor(x[:, b, :], pb(2 * b, 2), top[:, 6, bass.ds(b * 8 + e, 1)],
                                                      x[:, b, :], ALU.mult, ALU.add)
                    last.then_inc(sem("x_added"), 1)

            dve.wait_ge(sem("small_in"), 16 * 8)
            for i in range(2):
                step(tt(lam_in[:, 2 * i, :], lam_in[:, 2 * i, :], lam_in[:, 2 * i + 1, :], ALU.mult))
            v.tensor_reduce(lam_e[:, 0, :], v3(lam_in[:, 0, :], DEPTH), X, ALU.add)
            v.tensor_reduce(lam_e[:, 1, :], v3(lam_in[:, 2, :], DEPTH), X, ALU.add).then_inc(sem("lam_dots"), 1)
            dve.wait_ge(sem("init_act"), 2)
            v.tensor_scalar(neg_a[:, :], neg_a[:, :], -1.0, None, ALU.mult)
            step(tt(neg_lam[:, :], lam_e[:, 1, :], lam_e[:, 0, :], ALU.subtract))
            for layer in range(DEPTH):
                last = v.tensor_scalar(neg_lam[:, layer:layer + 1], neg_lam[:, layer:layer + 1], -LAM_INIT[layer], None,
                                       ALU.add)
            step(last)
            dve.wait_ge(sem("gains_transposed"), 1)
            v.tensor_copy(gain[:, 0:68], psum[:, 4, 0:68])
            step(v.tensor_copy(gain[:, 68:164], psum[:, 4, P:P + 96]))

            for layer in range(DEPTH):
                for s in ORDER:
                    if s in ("da_q", "da_k"):
                        rope(layer, s)
                    elif s in UNITS and UNITS[s][4] == "dve":
                        g = unit_index(layer, s)
                        src = pb(unit_banks(layer, s), 2)
                        dve.wait_ge(sem("unit_done"), g + 1)
                        if s[:2] == "br":
                            i = int(s[-1])
                            gate = W2 if i == 0 else W3
                            dst = mergedT[:, i * 1024:(i + 1) * 1024]
                            wait_evacuated(dve, unit_index(layer, f"gate_{s[3]}{i}"))
                            if s[3] == "a":
                                tt(dst, src, gate, ALU.mult).then_inc(sem("unit_out_dve"), 1)
                            else:
                                tt(gate, src, gate, ALU.mult).then_inc(sem("unit_out_dve"), 1)
                                wait_evacuated(dve, g)
                                last = tt(dst, dst, gate, ALU.add)
                                if i == 1:
                                    last.then_inc(sem("merged_b" if s[3] == "b" else "merged_ready"), 1)
                        else:
                            half = int(s[-1])
                            xs = x[:, :, half * W:(half + 1) * W]
                            tt(xs, xs, v3(src, 2), ALU.add).then_inc(sem("unit_out_dve"), 1)
                    elif s in NORM_NO:
                        if s == "norm_mix":
                            v.memset(conv_in[:, :, 0:3], 0.0).then_inc(sem("pads_ready"), 1)
                        norm(layer, s)
                    elif s[:5] == "conv_":
                        conv(layer, "qkv".index(s[5]))
                    elif s == "ab":
                        dve.wait_ge(sem("ab_done"), layer + 1)
                        src = v3(psum[:, 4, 0:16], 2)
                        tt(v3(s16[:, 1, 0:8], 2), src[:, :, 0:4], rep(dt_bias[:, layer * H:(layer + 1) * H], 2), ALU.add)
                        v.tensor_copy(v3(s16[:, 4, 0:8], 2), src[:, :, 4:8]).then_inc(sem("ab_out"), 1)
                    elif s == "gd_gate":
                        dve.wait_ge(sem("gates_act"), layer + 1)
                        step(v.scalar_tensor_tensor(s16[:, 2, 0:8], s16[:, 1, 0:8], 0.0, s16[:, 3, 0:8], ALU.max, ALU.add))
                        tt(v3(s16[:, 0, 0:8], 2), v3(s16[:, 2, 0:8], 2), rep(neg_a[:, layer * H:(layer + 1) * H], 2),
                           ALU.mult).then_inc(sem("g_ready"), 1)
                        step(v.tensor_scalar(s16[:, 5, 0:8], s16[:, 5, 0:8], 1.0, None, ALU.add))
                        step(v.reciprocal(s16[:, 4, 0:8], s16[:, 5, 0:8]))
                    elif s == "gd_scale":
                        beta, eg, ekd = s16[:, 4, 0:8], s16[:, 8, 8:16], s16[:, 9, 8:16]
                        dve.wait_ge(sem("gd_tok_out"), 3 * layer + 3)
                        for i, src in enumerate((qn, kn)):
                            step(tt(scratch, src, src, ALU.mult))
                            step(v.tensor_reduce(s16[:, 6, 8 * i:8 * i + 8], v3(scratch, 8), X, ALU.add))
                        dve.wait_ge(sem("gc_done"), 2 * layer + 2)
                        spread = v3(pb(6, 2), 8)
                        step(v.tensor_copy(s16[:, 8, 0:8], psum[:, 4, 0:8]))
                        step(tt(v3(decayT, 8), spread, each(s16[:, 8, 0:8], P), ALU.subtract))
                        v.tensor_scalar(decayT, decayT, 0.0, None, ALU.min)
                        tt(s16[:, 9, 0:8], spread[:, :, P - 1], s16[:, 8, 0:8], ALU.subtract).then_inc(sem("decay_logs"), 1)
                        power(layer, s, s16[:, 6, :], 16, 1.0)
                        step(v.tensor_scalar(s16[:, 7, 0:8], pow_out[:, 0:8], float(SB_DIM) ** -0.5, None, ALU.mult))
                        tt(v3(qn, 8), v3(qn, 8), each(s16[:, 7, 0:8], P), ALU.mult)
                        step(tt(v3(kn, 8), v3(kn, 8), each(pow_out[:, 8:16], P), ALU.mult))
                        tt(v3(kb, 8), v3(kn, 8), each(beta, P), ALU.mult)
                        tt(v3(vb, 8), v3(vb, 8), each(beta, P), ALU.mult).then_inc(sem("gd_scaled"), 1)
                        dve.wait_ge(sem("decay_exp"), layer + 1)
                        dve.wait_ge(sem("gd_scaled"), layer + 1)
                        step(tt(v3(kbg, 4), v3(kb[:, W:], 4), each(eg[:, 4:8], P), ALU.mult))
                        v.tensor_scalar(kbg, kbg, -1.0, None, ALU.mult)
                        step(tt(v3(decayT, 8), v3(decayT, 8), rep(c("triu"), 8), ALU.mult))
                    elif s == "gd_T":
                        eg, ekd = s16[:, 8, 8:16], s16[:, 9, 8:16]
                        dve.wait_ge(sem("gd_T_done"), 4 * layer + 3)
                        tt(v3(qn[:, W:], 4), v3(qn[:, W:], 4), each(eg[:, 4:8], P), ALU.mult).then_inc(sem("qg_ready"), 1)
                        tt(v3(kn[:, 0:W], 4), v3(kn[:, 0:W], 4), each(ekd[:, 0:4], P), ALU.mult).then_inc(sem("kd_ready"), 1)
                    elif s == "gd_LA":
                        dve.wait_ge(sem("gd_LA_done"), 3 * layer + 1)
                        step(tt(lT, pb(4, 2), decayT, ALU.mult))
                        tt(v3(lT, 8), v3(lT, 8), rep(c("striu"), 8), ALU.mult).then_inc(sem("lT_ready"), 1)
                        dve.wait_ge(sem("gd_LA_done"), 3 * layer + 2)
                        tt(intraT, pb(6, 2), decayT, ALU.mult).then_inc(sem("intra_ready"), 1)
                        dve.wait_ge(sem("lT_ready"), layer + 1)
                        dve.wait_ge(sem("l_ready"), layer + 1)
                        tt(v3(uT, 8), v3(lT, 8), rep(c("levelT", 0, P), 8), ALU.mult)
                        step(tt(v3(t_, 8), v3(l_, 8), rep(c("level", 0, P), 8), ALU.mult))
                        for m in (uT, t_):
                            v.scalar_tensor_tensor(v3(m, 8), v3(m, 8), -1.0, rep(c("ident"), 8), ALU.mult, ALU.add) \
                                .then_inc(sem("tu_ready"), 1)
                    elif s == "gd_inv":
                        at = CONST["levelT"][0]
                        dve.wait_ge(sem("tu_ready"), 14 * layer + 2)
                        with dve.Fori(0, 6) as it:
                            n = 6 * layer + it
                            dve.wait_ge(sem("tu_ready"), 14 * layer + 2 + 2 * it)
                            tt(v3(bT, 8), v3(lT, 8), rep(const[:, bass.ds(at + P + it * P, P)], 8), ALU.mult) \
                                .then_inc(sem("bT_ready"), 1)
                            dve.wait_ge(sem("tmu_done"), 2 * n + 1)
                            tt(t_, t_, pb(6, 2), ALU.subtract).then_inc(sem("tu_ready"), 1)
                            dve.wait_ge(sem("tmu_done"), 2 * n + 2)
                            tt(uT, uT, pb(4, 2), ALU.subtract).then_inc(sem("tu_ready"), 1)
                    elif s[:6] == "da_att":
                        i = int(s[-1])
                        wd = (i + 1) * P
                        n = NB * layer + i + 1
                        dve.wait_ge(sem("da_scores"), n)
                        for half in range(2):
                            last = tt(v3(W23[:, half * 4 * wd:(half + 1) * 4 * wd], 4), v3(pb(4 + 2 * half, 2), 4)[:, :, 0:wd],
                                      rep(c("causal", SEQ - wd, SEQ), 4), ALU.add)
                        step(last)
                        p8 = v3(W23[:, 0:8 * wd], 8)
                        step(v.tensor_reduce(s16b[:, 0, 0:8], p8, X, ALU.max))
                        v.tensor_scalar(s16b[:, 1, 0:8], s16b[:, 0, 0:8], -1.0, None, ALU.mult).then_inc(sem("da_max"), 1)
                        dve.wait_ge(sem("da_exp"), n)
                        step(v.reciprocal(s16b[:, 3, 0:8], s16b[:, 2, 0:8]))
                        step(v.tensor_scalar(s16b[:, 3, 4:8], s16b[:, 3, 4:8], neg_lam[:, layer:layer + 1], None, ALU.mult))
                        step(tt(p8, p8, each(s16b[:, 3, 0:8], wd), ALU.mult))
                        tt(W23[:, 0:4 * wd], W23[:, 0:4 * wd], W23[:, 4 * wd:8 * wd], ALU.add).then_inc(sem("da_probs"), 1)
                        dve.wait_ge(sem("da_o_done"), n)
                        v.tensor_copy(W1[:, i * W:(i + 1) * W], psum[:, 6, :]).then_inc(sem("da_o_out"), 1)
                    elif s == "da_out":
                        dve.wait_ge(sem("da_o_out"), NB * (layer + 1))
                        step(tt(W0, W1, W1, ALU.mult))
                        step(v.tensor_reduce(s16b[:, 6, 0:8], v3(W0, 8), X, ALU.add))
                        power(layer, s, s16b[:, 6, 0:8], 8, 1.0 / P)
                        tt(v3(W1, 8), v3(W1, 8), each(pow_out[:, 0:8], P), ALU.mult).then_inc(sem("da_normed"), 1)
                        dve.wait_ge(sem("da_oT_done"), layer + 1)
                        v.tensor_scalar(oaT, pb(4, 2), gain[:, 64 + layer:65 + layer], 1.0 - LAM_INIT[layer], ALU.mult,
                                        ALU.mult).then_inc(sem("oaT_ready"), 1)
                    elif s[:6] == "sb_att":
                        i = int(s[-1])
                        wd = (i + 1) * P
                        n = NB * layer + i + 1
                        scores, lg = pb(4, 2)[:, 0:4 * wd], W3[:, 0:4 * wd]
                        dve.wait_ge(sem("sb_ln"), n)
                        step(v.scalar_tensor_tensor(lg, scores, 0.0, W2[:, 0:4 * wd], ALU.max, ALU.add))
                        step(tt(v3(lg, 4), v3(lg, 4), rep(c("strict01", SEQ - wd, SEQ), 4), ALU.mult))
                        for h in range(H):
                            rev = W3[:, h * wd:(h + 1) * wd][:, ::-1]
                            last = v.tensor_tensor_scan(W1[:, h * wd:(h + 1) * wd][:, ::-1], c("ones", 0, wd), rev, 0.0,
                                                        ALU.mult, ALU.add)
                        step(last)
                        step(tt(lg, scores, W1[:, 0:4 * wd], ALU.subtract))
                        tt(v3(lg, 4), v3(lg, 4), rep(c("strict_neg", SEQ - wd, SEQ), 4), ALU.add).then_inc(sem("sb_log"), 1)
                        dve.wait_ge(sem("sb_oT_done"), n)
                        v.tensor_copy(v3(obT, 4)[:, :, i * P:(i + 1) * P], v3(psum[:, 6, :], 4)).then_inc(sem("obT_ready"), 1)
                    elif s[:5] == "x_att":
                        i = int(s[-1])
                        n = NB * layer + i + 1
                        dve.wait_ge(sem("x_scores"), n)
                        step(v.tensor_reduce(s16b[:, 7, 0:4], v3(pb(4, 2), 4), X, ALU.max))
                        v.tensor_scalar(s16b[:, 4, 0:4], s16b[:, 7, 0:4], -1.0, None, ALU.mult).then_inc(sem("x_max"), 1)
                        dve.wait_ge(sem("x_exp"), n)
                        step(v.reciprocal(s16b[:, 5, 4:8], s16b[:, 5, 0:4]))
                        tt(v3(W2, 4), v3(W2, 4), each(s16b[:, 5, 4:8], SEQ), ALU.mult).then_inc(sem("x_probs"), 1)
                        dve.wait_ge(sem("x_oT_done"), n)
                        v.tensor_copy(v3(oxT, 4)[:, :, i * P:(i + 1) * P], v3(psum[:, 4, :], 4)).then_inc(sem("oxT_ready"), 1)
                    elif s == "gd_scan":
                        for n, dst, b in ((2, wT, 5), (3, state, 6), (4, gd_o[:, 0:W], 7), (6, gd_o[:, W:], 5)):
                            dve.wait_ge(sem("scan_done"), 6 * layer + n)
                            v.tensor_copy(dst, psum[:, b, :]).then_inc(sem("scan_out_dve"), 1)
                    elif s == "gd_out":
                        dve.wait_ge(sem("scan_out_dve"), 4 * (layer + 1))
                        step(tt(lT, gd_o, gd_o, ALU.mult))
                        step(v.tensor_reduce(s16[:, 6, 0:8], v3(lT, 8), X, ALU.add))
                        power(layer, s, s16[:, 6, 0:8], 8, 1.0 / P)
                        step(tt(v3(gd_o, 8), v3(gd_o, 8), each(pow_out[:, 0:8], P), ALU.mult))
                        dve.wait_ge(sem("z_sig"), layer + 1)
                        step(tt(z[:, :], z[:, :], l_, ALU.mult))
                        tt(gd_o, gd_o, z[:, :], ALU.mult).then_inc(sem("gd_normed"), 1)
                        dve.wait_ge(sem("gd_oT_done"), layer + 1)
                        v.tensor_scalar(ocT, pb(6, 2), gain[:, 66 + layer:67 + layer], None, ALU.mult) \
                            .then_inc(sem("ocT_ready"), 1)
                    elif s == "ffn" and layer == 0:
                        ffn(0, SEQ)
                        dve.wait_ge(sem("down_done"), 11)
                        xf = x[:, :, :].rearrange("p b d -> p (b d)")
                        tt(xf, xf, pb(4, 4), ALU.add).then_inc(sem("ffn_added"), 1)
                    elif s == "ffn":
                        iota8 = c("iota8")
                        dve.wait_ge(sem("router_done"), 1)
                        step(v.tensor_copy(top[:, 1, :], psum[:, 4, 0:16]))
                        for b in range(NB):
                            lg, mx = top[:, 1, b * 8:b * 8 + 8], top[:, 2, b * 8:b * 8 + 8]
                            step(v.max(mx, lg))
                            step(v.max_index(top_i[:, b, :], mx, lg))
                            step(v.tensor_copy(top[:, 9, b * 8:b * 8 + 8], top_i[:, b, :]))
                            for j in range(2):
                                step(v.tensor_scalar(top[:, 3 + j, b * 8:b * 8 + 8], iota8, top[:, 9, b * 8 + j:b * 8 + j + 1],
                                                     None, ALU.is_equal))
                        tops = v3(top[:, 2, :], 2)
                        tt(top[:, 10, 0:2], tops[:, :, 1], tops[:, :, 0], ALU.subtract).then_inc(sem("top_diff"), 1)
                        tt(top[:, 0, :], top[:, 3, :], top[:, 4, :], ALU.add).then_inc(sem("chosen_ready"), 1)
                        dve.wait_ge(sem("top_exp"), 1)
                        step(v.tensor_scalar(top[:, 12, 0:2], top[:, 11, 0:2], 1.0, None, ALU.add))
                        step(v.reciprocal(top[:, 13, 0:2], top[:, 12, 0:2]))
                        step(tt(top[:, 14, 0:2], top[:, 11, 0:2], top[:, 13, 0:2], ALU.mult))
                        for b in range(NB):
                            q = slice(b * 8, b * 8 + 8)
                            step(v.tensor_scalar(top[:, 5, q], top[:, 3, q], top[:, 13, b:b + 1], None, ALU.mult))
                            step(v.scalar_tensor_tensor(top[:, 6, q], top[:, 4, q], top[:, 14, b:b + 1], top[:, 5, q],
                                                        ALU.mult, ALU.add))
                        dve.wait_ge(sem("ranks_done"), 1)
                        step(v.scalar_tensor_tensor(top[:, 15, :], psum[:, 5, 0:16], 1.0, top[:, 0, :], ALU.add, ALU.mult))
                        step(v.tensor_scalar(top[:, 7, :], top[:, 15, :], -1.0, None, ALU.add))
                        step(v.tensor_scalar(top[:, 8, :], top[:, 7, :], -float(CAP), None, ALU.add))
                        step(v.tensor_reduce(top[:, 16, 0:1], psum[:, 5, 16:24], X, ALU.max))
                        v.tensor_scalar(overflow[:, :], top[:, 16, 0:1], float(CAP), None, ALU.is_gt) \
                            .then_inc(sem("overflow_known"), 1)
                        dve.wait_ge(sem("overflow_known"), 1)
                        v.tensor_copy(top[:, 17, 0:1], top[:, 16, 0:1]).then_inc(sem("x_added"), 1)
                        expert(11, 0, 7)
                        with dve.If(dve.value_load(overflow[0:1, 0:1], min_val=0, max_val=1) > 0):
                            expert(11 + 14 * N_EXP, N_EXP, 8)
            last = norm_scale(DEPTH, "final")
            step(last)
            dve.wait_ge(sem("gain_row_in"), 16)
            for b in range(NB):
                last = tt(xn[:, b, :], xn[:, b, :], da_v, ALU.mult)
            last.then_inc(sem("out_ready"), 1)


def constants():
    a = np.zeros((P, N_CONST), np.float32)

    def put(name, m):
        at, n = CONST[name]
        a[:, at:at + n] = m.reshape(P, n)

    p, j = np.arange(P)[:, None], np.arange(P)[None, :]
    k = np.arange(SEQ)[None, :]
    put("ident", (p == j).astype(np.float32))
    put("triu", (p <= j).astype(np.float32))
    put("striu", (p < j).astype(np.float32))
    put("ones", np.ones((P, SEQ), np.float32))
    put("causal", np.where(k <= p + P, 0.0, NEG).astype(np.float32))
    put("strict_neg", np.where(k < p + P, 0.0, NEG).astype(np.float32))
    put("strict01", (k < p + P).astype(np.float32))
    level = np.stack([((p // m) % 2 == 1) & (j // m == p // m - 1) for m in LEVELS], 1)
    put("level", level.astype(np.float32))
    put("levelT", np.stack([((j // m) % 2 == 1) & (p // m == j // m - 1) for m in LEVELS], 1).astype(np.float32))
    inv = (1.0 / (np.float32(10000.0) ** (np.arange(0, DA_DIM, 2, dtype=np.float32) / np.float32(DA_DIM)))).astype(np.float32)
    ang = np.arange(SEQ, dtype=np.float32)[:, None] * inv[None, :]
    cos, sin = np.cos(ang), np.sin(ang)
    for name, m in (("cos", np.concatenate([cos, cos], 1)), ("sin", np.concatenate([-sin, sin], 1))):
        m = m.reshape(NB, P, DA_DIM).transpose(1, 0, 2).astype(np.float32)
        put(name + "_k", m)
        put(name + "_q", m * np.float32(DA_DIM ** -0.5))
    put("iota", np.broadcast_to(np.arange(P, dtype=np.float32), (P, P)))
    put("nhalf", np.full((P, 16), -0.5, np.float32))
    put("iota8", np.broadcast_to(np.arange(8, dtype=np.float32), (P, 8)))
    return a


_INS = ["x", "mem", "norm_mix", "w_in", "gd_conv", "lam_q1", "lam_k1", "lam_q2", "lam_k2", "da_subln", "gd_a_log",
        "gd_dt_bias", "gd_norm", "w_br_a", "w_br_b", "w_br_c", "w_out", "norm_x", "norm_mem", "w_q_x", "w_kv_x", "w_o_x",
        "norm_ffn", "w_gate_dense", "w_up_dense", "w_down_dense", "w_router", "w_gate_exp", "w_up_exp", "w_down_exp",
        "norm_final"]


def kernel(**inputs):
    import concourse.bacc as _bacc
    from concourse.bass_utils import run_bass_kernel_spmd as _run

    nc = _bacc.Bacc("TRN2", target_bir_lowering=False, num_devices=1)
    arrays = {f"in_{name}_dram": np.ascontiguousarray(inputs[name]) for name in _INS}
    arrays["const_dram"] = constants()
    t = {}
    for name in _INS + ["const"]:
        key = "const_dram" if name == "const" else f"in_{name}_dram"
        a = arrays[key]
        t[name] = nc.dram_tensor(key, a.shape, mybir.dt.from_np(a.dtype), kind="ExternalInput").ap()
    out = nc.dram_tensor("out_0_dram", (1, SEQ, D), F32, kind="ExternalOutput").ap()
    hybrid_layers(nc, t, out)
    r = _run(nc, [arrays], core_ids=[0])
    return r.results[0]["out_0_dram"]
```

```python
from contextlib import ExitStack

import numpy as np
import concourse.bass as bass
from concourse import mybir

F32 = mybir.dt.float32
F32R = mybir.dt.float32r
I32 = mybir.dt.int32
U32 = mybir.dt.uint32
ALU = mybir.AluOpType
ACT = mybir.ActivationFunctionType
X = mybir.AxisListType.X

P = 128
D = 1024
SEQ = 256
NB = SEQ // P
KT = D // P
DEPTH = 2
H = 4
W = 512
DA_DIM = 64
SB_DIM = 128
N_EXP = 8
FF_DENSE = 2816
FF_EXP = 3584
CAP = 128
EPS = 1e-6
NEG = -1e30
PIECE = 2048
RAW = 3
SPLIT = 2
GD0 = 6 * W
AB0 = 10 * W
GATE0 = 10 * W + 2 * H
LAM_INIT = [0.8 - 0.6 * float(np.exp(-0.3 * layer)) for layer in range(DEPTH)]
LEVELS = [1, 2, 4, 8, 16, 32, 64]

CONST = {}
_at = 0
for _name, _n in [("ident", P), ("triu", P), ("striu", P), ("ones", SEQ), ("causal", SEQ), ("strict_neg", SEQ),
                  ("strict01", SEQ), ("level", 7 * P), ("levelT", 7 * P), ("cos_q", 2 * DA_DIM), ("sin_q", 2 * DA_DIM),
                  ("cos_k", 2 * DA_DIM), ("sin_k", 2 * DA_DIM), ("iota", P), ("nhalf", 16), ("iota8", 8)]:
    CONST[_name] = (_at, _n)
    _at += _n
N_CONST = _at

CHUNKS = ["gd_q", "gd_k", "gd_v", "da_q", "da_k", "da_v", "sb_q", "sb_k", "sb_v", "gd_z",
          "gate_a0", "gate_a1", "br_a", "gate_b0", "gate_b1", "br_b", "gate_c0", "gate_c1", "br_c",
          "out0", "out1", "x_k", "x_v", "x_q", "x_o"]
COLUMN = {"da_q": 0, "da_k": W, "da_v": 2 * W, "sb_q": 3 * W, "sb_k": 4 * W, "sb_v": 5 * W,
          "gd_q": GD0, "gd_k": GD0 + W, "gd_v": GD0 + 2 * W, "gd_z": GD0 + 3 * W}
for _i, _g in enumerate("abc"):
    COLUMN[f"gate_{_g}0"] = GATE0 + _i * D
    COLUMN[f"gate_{_g}1"] = GATE0 + _i * D + W

UNITS = {}
for _c in CHUNKS:
    _eng = "dve" if _c in ("da_q", "da_k", "out0", "out1") or _c[:2] == "br" or _c == "x_o" else "act"
    _kind = "tok" if _c in ("gd_z", "da_q", "da_k", "da_v", "sb_v", "x_v", "out0", "out1", "x_o") else "T"
    if _c[:2] == "br" or _c == "x_o":
        UNITS[_c + ".0"] = (_c, _kind, H, 0, _eng)
        UNITS[_c + ".1"] = (_c, _kind, H, W, _eng)
    else:
        UNITS[_c] = (_c, _kind, KT, 0, _eng)
UNIT_NO = {u: i for i, u in enumerate(UNITS)}
N_UNITS = len(UNITS)

ORDER = ["norm_mix", "gd_q", "gd_k", "conv_q", "gd_v", "conv_k", "ab", "da_q", "conv_v", "da_k", "gd_tok", "da_v",
         "gd_gate", "sb_q", "gd_scale", "sb_k", "gd_T", "da_T", "gd_LA", "sb_v", "da_sc0", "gd_z", "da_pv0", "da_sc1",
         "gate_a0", "da_pv1", "gd_inv", "da_out", "gate_a1", "br_a.0", "br_a.1", "sb_sc0", "gate_b0w", "sb_pv0", "sb_sc1",
         "sb_pv1", "gate_b0", "gate_b1", "gd_scan", "br_b.0", "br_b.1", "gd_out", "gate_c0", "gate_c1", "norm_mem",
         "br_c.0", "br_c.1", "out0", "out1", "x_k", "x_v", "norm_x", "x_q", "x_sc0", "x_pv0", "x_sc1", "x_pv1",
         "x_o.0", "x_o.1", "norm_ffn", "ffn"]
ORDER.remove("gate_b0w")
NORM_NO = {"norm_mix": 0, "norm_mem": 1, "norm_x": 2, "norm_ffn": 3}


def unit_pieces(layer, u):
    c, _, k, col, _ = UNITS[u]
    first = 2 * (layer * len(CHUNKS) + CHUNKS.index(c))
    return [first, first + 1] if k == KT else [first + col // W]


FF_UNIT = 256
DENSE_GROUPS = FF_DENSE // FF_UNIT
EXP_GROUPS = FF_EXP // FF_UNIT
assert FF_DENSE % FF_UNIT == 0 and FF_EXP % FF_UNIT == 0 and EXP_GROUPS % 2 == 0 and DENSE_GROUPS % 2 == 1


def hybrid_layers(nc, t, out):
    ctx = ExitStack()
    with ctx:
        def sb(name, shape, dt=F32):
            return ctx.enter_context(nc.sbuf_tensor(name, shape, dt))

        sems = {}

        def sem(name):
            if name not in sems:
                sems[name] = ctx.enter_context(nc.semaphore(name))
            return sems[name]

        const = sb("const", [P, N_CONST])
        base = (nc.sbuf_base + 31) // 32 * 32
        work = sb("work", [P, 44, 1024])
        r_views = {}
        conv_in = sb("conv_in", [P, 12, SEQ + 3])
        gain = sb("gain", [P, 4 + 96])
        gain_rows = conv_in
        w_small = [sb(f"w_small_{part}", [P, 3, KT, 8], F32R) for part in ("hi", "lo")]
        lam_e = sb("lam_e", [P, 2, DEPTH])
        neg_lam = sb("neg_lam", [P, DEPTH])
        a_log = sb("a_log", [P, DEPTH * H])
        dt_bias = sb("dt_bias", [P, DEPTH * H])
        neg_a = sb("neg_a", [P, DEPTH * H])
        ss = sb("ss", [P, NB])
        s16 = sb("s16", [P, 10, 16])
        s16b = sb("s16b", [P, 8, 8])
        pow_in = sb("pow_in", [P, 16])
        pow_out = sb("pow_out", [P, 16])
        top = sb("top", [P, 18, 16])
        top_i = sb("top_i", [P, NB, 8], U32)
        overflow = sb("overflow", [P, 1], I32)

        def c(name, a=0, b=None):
            at, n = CONST[name]
            return const[:, at + a:at + (n if b is None else b)]

        def v3(ap, a):
            return ap.rearrange("p (a b) -> p a b", a=a)

        def tile(i, n=1):
            return work[:, i:i + n, :].rearrange("p a b -> p (a b)")

        def rtile(i, n=1):
            if (i, n) not in r_views:
                r_views[i, n] = nc.alloc_sbuf_tensor_at(f"work_r_{i}_{n}", [P, n * 1024], F32R, offset=base + 4096 * i)
            return r_views[i, n][:, :]

        def stored(i, n=1):
            return rtile(i, n).bitcast(F32)

        W0, W1, W2, W3 = (tile(i) for i in range(4))
        lam_in = v3(W0[:, 0:4 * DEPTH * DA_DIM], 4)
        w_small_in = W1[:, 0:192]
        W01, W23 = tile(0, 2), tile(2, 2)
        da_qT, da_kT, da_v = tile(4), tile(5), tile(6)
        merged = tile(4, 2)
        oaT = (6, 7, 1)
        sb_qT, sb_kT, sb_v = tile(8), tile(9), tile(10)
        obT = (11, 12, 1)
        mergedT = (11, 8, 2)
        x_qT, x_kT, x_v, oxT = sb_qT, sb_kT, sb_v, oaT
        conv_out = tile(13, 3)
        knT, kbT, qnT = tile(13), tile(14), tile(15)
        z, gd_o = tile(13), tile(14)
        m1 = qnT
        wT, state = tile(15)[:, 0:W], tile(15)[:, W:]
        memT = (13, 16, 2)
        tm = tile(16, 3)
        qn, kn, vb = tile(16), tile(17), tile(18)
        mem_tok = tile(18, 2)
        kb = uT = tile(19)
        decayT = intraT = tile(20)
        ocT = (20, 21, 1)
        scratch = bT = v_new = tile(21)
        qgT, kbg = tile(22)[:, 0:W], tile(22)[:, W:]
        x = work[:, 23:25, :]
        xn = work[:, 25:27, :]
        hT = (27, 25, 2)
        hT_router = (27, 8, 2)
        RAW_AT, SPLIT_AT, GAIN_ROW = 29, 35, tile(43)
        conv_flat = conv_in[:, :, :].rearrange("p a b -> p (a b)")
        lT, l_, t_ = (conv_flat[:, 1024 * i:1024 * (i + 1)] for i in range(3))
        silu_g = [tile(0)[:, 0:W], tile(0)[:, W:]]
        hid = [tile(1)[:, 0:W], tile(1)[:, W:]]
        hgT = (4, 5, 1)
        y_tok, select, selectT = tile(6), tile(7)[:, 0:NB * CAP], tile(7)[:, 256:256 + SEQ]
        FFN_EARLY = 13

        def halves(where):
            hi, lo, n = where
            return rtile(hi, n), rtile(lo, n)

        def raw_slot(q):
            return tile(RAW_AT + 2 * (q % RAW), 2)

        def split_slot(q, r=True):
            at = SPLIT_AT + 4 * (q % SPLIT)
            return (rtile if r else stored)(at, 2), (rtile if r else stored)(at + 2, 2)

        def ffn_raw(par, j):
            return tile((RAW_AT if par else FFN_EARLY) + 2 * j, 2)

        def ffn_split(j, r=True):
            at = (SPLIT_AT, SPLIT_AT + 4, FFN_EARLY + 6)[j]
            return (rtile if r else stored)(at, 2), (rtile if r else stored)(at + 2, 2)

        psum = ctx.enter_context(nc.psum_tensor("psum", [P, 8, 512], F32))

        def pb(first, n=1):
            return psum[:, first:first + n, :].rearrange("p a b -> p (a b)")

        def bc(ap, shape):
            return ap.to_broadcast(shape)

        def rep(ap, n):
            return ap.unsqueeze(1).to_broadcast([P, n, ap.shape[1]])

        def each(ap, m):
            return ap.unsqueeze(2).to_broadcast([P, ap.shape[1], m])

        block = ctx.enter_context(nc.Block())

        def unit_index(layer, u):
            return layer * N_UNITS + UNIT_NO[u]

        def unit_names():
            return [(layer, u) for layer in range(DEPTH) for u in UNITS]

        def wait_evacuated(eng, g):
            eng_name = UNITS[unit_names()[g][1]][4]
            n = sum(UNITS[u][4] == eng_name for _, u in unit_names()[:g + 1])
            eng.wait_ge(sem(f"unit_out_{eng_name}"), n)

        def unit_banks(layer, u):
            return 2 * (unit_index(layer, u) % 2)

        def wait_computed(eng, layer, u):
            eng.wait_ge(sem("piece_used"), unit_pieces(layer, u)[-1] + 1)

        def units_after(layer, u):
            every = [(l, s) for l in range(DEPTH) for s in ORDER if s in UNITS]
            i = every.index((layer, u)) + 1
            return [every[i]] if i < len(every) and every[i][0] == layer else []

        def ffn_loop(eng, groups, group):
            pairs = (groups - 3) // 2
            group(0, 0)
            group(1, 1)
            with eng.Fori(0, pairs) as p:
                group(2 * p + 2, 0)
                group(2 * p + 3, 1)
            for g in range(2 + 2 * pairs, groups):
                group(g, g % 2)

        @block.sync
        def _(sp):
            wi = t["w_in"]
            sp.dma_start(x, t["x"][0].rearrange("(b p) d -> p b d", p=P)).then_inc(sem("x_in"), 16)

            def rows_by_cols(dst, view, k):
                return dst.rearrange("p (k n) -> p k n", k=k), view.rearrange("(k p) n -> p k n", p=P)

            def mixer_chunk(layer, name):
                for i in range(2):
                    q = 2 * (layer * len(CHUNKS) + CHUNKS.index(name)) + i
                    rows = slice(i * W, (i + 1) * W)
                    if name in COLUMN:
                        src = wi[layer, rows, COLUMN[name]:COLUMN[name] + W]
                    elif name[:3] == "out":
                        src = t["w_out"][layer, rows, int(name[3]) * W:(int(name[3]) + 1) * W]
                    elif name == "x_q":
                        src = t["w_q_x"][layer, rows, :]
                    elif name in ("x_k", "x_v"):
                        v0 = W * int(name == "x_v")
                        src = t["w_kv_x"][layer, rows, v0:v0 + W]
                    else:
                        w = t["w_o_x"] if name == "x_o" else t["w_br_" + name[3]]
                        src = w[layer, :, rows]
                    if q >= RAW:
                        sp.wait_ge(sem("lo_ready"), q - RAW + 1)
                    d, s = rows_by_cols(raw_slot(q), src, 4)
                    sp.dma_start(d, s).then_inc(sem(f"piece_in{q % RAW}"), 16)

            def ffn_stream(groups, group0, gate, up, down, fresh=False):
                def gate_up(g, par, wait):
                    for j in range(2):
                        if wait:
                            sp.wait_ge(sem(f"ffn_lo{j}"), group0 + g - 1)
                        dst = ffn_raw(par, j).rearrange("p (k a n) -> p k a n", k=4, a=2)
                        for a, w in enumerate((gate(g), up(g))):
                            src = w.rearrange("(k p) n -> p k n", p=P)[:, 4 * j:4 * j + 4, :]
                            sp.dma_start(dst[:, :, a, :], src).then_inc(sem(f"ffn_in{par}{j}"), 16)

                def group(g, par):
                    static = isinstance(g, int)
                    if fresh and static and g == 0:
                        sp.wait_ge(sem("lo_ready"), 2 * len(CHUNKS))
                    if not static or g < groups - 1:
                        gate_up(g + 1, 1 - par, not (fresh and static and g == 0))
                    if not (fresh and static and g < 2):
                        sp.wait_ge(sem("ffn_lo2"), group0 + g - 1)
                    d, s = rows_by_cols(ffn_raw(par, 2), down(g), 2)
                    sp.dma_start(d, s).then_inc(sem(f"ffn_in{par}2"), 16)

                gate_up(0, 0, not fresh)
                ffn_loop(sp, groups, group)

            def experts(group0):
                def view(w, e, g):
                    return w[0, bass.ds(e, 1), :, bass.ds(g * FF_UNIT, FF_UNIT)].rearrange("e k n -> (e k) n")

                with sp.Fori(0, N_EXP) as e:
                    ffn_stream(EXP_GROUPS, group0 + EXP_GROUPS * e, lambda g: view(t["w_gate_exp"], e, g),
                               lambda g: view(t["w_up_exp"], e, g),
                               lambda g: t["w_down_exp"][0, bass.ds(e, 1), bass.ds(g * FF_UNIT, FF_UNIT), :]
                               .rearrange("e k n -> (e k) n"))

            for layer in range(DEPTH):
                if layer:
                    for j in range(3):
                        sp.wait_ge(sem(f"ffn_lo{j}"), DENSE_GROUPS - 1)
                for name in CHUNKS:
                    mixer_chunk(layer, name)
                    if name == "br_b":
                        sp.wait_ge(sem("scan_done"), 6 * (layer + 1))
                        sp.dma_start(mem_tok.rearrange("p (b d) -> p b d", b=NB),
                                     t["mem"][0].rearrange("(b p) d -> p b d", p=P)).then_inc(sem("mem_in"), 16)
                if layer == 0:
                    def cols(g):
                        return slice(g * FF_UNIT, (g + 1) * FF_UNIT) if isinstance(g, int) else bass.ds(g * FF_UNIT, FF_UNIT)
                    wait_computed(sp, layer, "x_v")
                    ffn_stream(DENSE_GROUPS, 0, lambda g: t["w_gate_dense"][0, :, cols(g)],
                               lambda g: t["w_up_dense"][0, :, cols(g)], lambda g: t["w_down_dense"][0, cols(g), :],
                               fresh=True)
                else:
                    wait_computed(sp, layer, "x_v")
                    sp.wait_ge(sem("lo_ready"), 2 * len(CHUNKS) * (layer + 1))
                    experts(DENSE_GROUPS)
                    sp.wait_ge(sem("overflow_known"), 1)
                    with sp.If(sp.value_load(overflow[0:1, 0:1], min_val=0, max_val=1) > 0):
                        experts(DENSE_GROUPS + EXP_GROUPS * N_EXP)
            sp.wait_ge(sem("out_ready"), 1)
            sp.dma_start(out[0].rearrange("(b p) d -> p b d", p=P), xn).then_inc(sem("out_stored"), 16)
            sp.wait_ge(sem("out_stored"), 16)

        @block.tensor
        def _(pe):
            ident = c("ident")

            def mm(o, a, b, start=True, stop=True):
                return nc.tensor.matmul(o, a, b, start=start, stop=stop)

            def tr(o, a, rows=P):
                return nc.tensor.transpose(o, a, ident[0:rows, 0:rows])

            def mm3(o, a, b, first=True, last=True, check=True):
                nc.tensor.matmul(o, a[0], b[0], start=first, stop=False, skip_group_check=not check)
                nc.tensor.matmul(o, a[0], b[1], start=False, stop=False, skip_group_check=not check)
                return nc.tensor.matmul(o, a[1], b[0], start=False, stop=last, skip_group_check=not check)

            def pick(pair, *index):
                return tuple(p[index] for p in pair)

            source = {"x_k": memT, "x_v": memT, "out0": mergedT, "out1": mergedT, "br_a": oaT, "br_b": obT,
                      "br_c": ocT, "x_o": oxT}

            def unit(layer, u):
                name, kind, k_tiles, _, _ = UNITS[u]
                g = unit_index(layer, u)
                if g >= 2:
                    wait_evacuated(pe, g - 2)
                if u == "gd_q":
                    pe.wait_ge(sem("norm_out"), 4 * layer + 1)
                if u == "x_k":
                    pe.wait_ge(sem("norm_out"), 4 * layer + 2)
                if u == "x_q":
                    pe.wait_ge(sem("norm_out"), 4 * layer + 3)
                if u == "br_a.0":
                    pe.wait_ge(sem("oaT_ready"), layer + 1)
                if u == "br_b.0":
                    pe.wait_ge(sem("obT_ready"), NB * (layer + 1))
                if u == "br_c.0":
                    pe.wait_ge(sem("ocT_ready"), layer + 1)
                if u == "out0":
                    pe.wait_ge(sem("merged_ready"), 2 * (layer + 1))
                if u == "x_o.0":
                    pe.wait_ge(sem("oxT_ready"), NB * (layer + 1))
                act = [a.rearrange("p (k n) -> p k n", k=k_tiles) for a in halves(source.get(name, hT))]
                base = unit_banks(layer, u)
                pieces = unit_pieces(layer, u)
                for i, q in enumerate(pieces):
                    pe.wait_ge(sem("lo_ready"), q + 1)
                    w = [a.rearrange("p (k n) -> p k n", k=4) for a in split_slot(q)]
                    end = i == len(pieces) - 1
                    if kind == "T":
                        for nt in range(4):
                            o = psum[:, base + nt // 2, (nt % 2) * SEQ:(nt % 2 + 1) * SEQ]
                            for k in range(4):
                                last = mm3(o, pick(w, slice(None), k, slice(nt * P, (nt + 1) * P)),
                                           pick(act, slice(None), 4 * i + k), i == 0 and k == 0 and nt % 2 == 0,
                                           end and k == 3, False)
                    else:
                        for b in range(NB):
                            for k in range(4):
                                last = mm3(psum[:, base + b, :], pick(act, slice(None), 4 * i + k, slice(b * P, (b + 1) * P)),
                                           pick(w, slice(None), k), i == 0 and k == 0, end and k == 3)
                    last.then_inc(sem("piece_used"), 1)

            def norm(layer, s):
                i = 4 * layer + NORM_NO[s]
                src = v3(mem_tok, NB) if s == "norm_mem" else xn
                pe.wait_ge(sem("xn_ready"), i + 1)
                for kt in range(KT):
                    for b in range(NB):
                        last = tr(psum[:, 4 + kt // 2, (kt % 2) * SEQ + b * P:(kt % 2) * SEQ + (b + 1) * P],
                                  src[:, b, kt * P:(kt + 1) * P])
                    if kt % 4 == 3:
                        last.then_inc(sem("norm_transposed"), 1)

            def blocks_T(dst_bank, src, n=8):
                for s in range(n):
                    last = tr(pb(dst_bank, 2)[:, s * P:(s + 1) * P], src[:, s * P:(s + 1) * P])
                return last

            def heads_T(dst_bank, src):
                for h in range(H):
                    for b in range(NB):
                        last = tr(pb(dst_bank, 2)[:, h * SEQ + b * P:h * SEQ + (b + 1) * P],
                                  src[:, b * W + h * P:b * W + (h + 1) * P])
                return last

            def transpose_probs(layer, i, probs, tag, bank):
                wd = (i + 1) * P if tag != "x" else SEQ
                nk = wd // P
                pe.wait_ge(sem(f"{tag}_probs"), NB * layer + i + 1)
                for h in range(H):
                    for k in range(nk):
                        last = tr(pb(bank, 2)[:, (h * nk + k) * P:(h * nk + k + 1) * P],
                                  probs[:, h * wd + k * P:h * wd + (k + 1) * P])
                last.then_inc(sem(f"{tag}_probsT"), 1)
                pe.wait_ge(sem(f"{tag}_probsT_out"), NB * layer + i + 1)
                return nk

            def ffn(where, blocks, groups, group0):
                src = [a.rearrange("p (k n) -> p k n", k=KT) for a in halves(where)]

                def gate_up(g, par, j):
                    pe.wait_ge(sem(f"ffn_lo{j}"), g + 1)
                    w = [a.rearrange("p (k n) -> p k n", k=4) for a in ffn_split(j)]
                    for b in range(blocks):
                        for k in range(4):
                            last = mm3(psum[:, blocks * par + b, :], pick(src, slice(None), 4 * j + k, slice(b * P, (b + 1) * P)),
                                       pick(w, slice(None), k), j == 0 and k == 0, j == 1 and k == 3)
                    last.then_inc(sem(f"ffn_used{j}"), 1)

                def hidden_T(g, par):
                    pe.wait_ge(sem("hidden_ready"), g + 1)
                    for ft in range(2):
                        for b in range(blocks):
                            last = tr(psum[:, blocks * par, (ft * blocks + b) * P:(ft * blocks + b + 1) * P],
                                      hid[par][:, b * FF_UNIT + ft * P:b * FF_UNIT + (ft + 1) * P])
                    last.then_inc(sem("hiddenT_done"), 1)

                def down(g, par, first, last_group):
                    pe.wait_ge(sem("hidden_lo"), g + 1)
                    pe.wait_ge(sem("ffn_lo2"), g + 1)
                    w = [a.rearrange("p (k n) -> p k n", k=2) for a in ffn_split(2)]
                    hv = [rtile(2 + i)[:, par * W:par * W + 2 * blocks * P].rearrange("p (a n) -> p a n", a=2)
                          for i in range(2)]
                    for ft in range(2):
                        for b in range(blocks):
                            for half in range(2):
                                last = mm3(psum[:, 4 + 2 * b + half, :], pick(hv, slice(None), ft, slice(b * P, (b + 1) * P)),
                                           pick(w, slice(None), ft, slice(half * W, (half + 1) * W)),
                                           first and ft == 0, last_group and ft == 1)
                    last.then_inc(sem("ffn_used2"), 1)

                def group(g, par):
                    gate_up(group0 + g, par, 0)
                    first = isinstance(g, int) and g == 0
                    if not first:
                        hidden_T(group0 + g - 1, 1 - par)
                    gate_up(group0 + g, par, 1)
                    if not first:
                        down(group0 + g - 1, 1 - par, isinstance(g, int) and g == 1, False)
                    if isinstance(g, int) and g == groups - 1:
                        hidden_T(group0 + g, par)
                        down(group0 + g, par, False, True)

                ffn_loop(pe, groups, group)

            def expert(group0, n0):
                with pe.Fori(0, N_EXP) as e:
                    pe.wait_ge(sem("select_ready"), n0 + e + 1)
                    for kt in range(KT):
                        for b in range(NB):
                            last = mm(pb(2, 2)[:, kt * CAP:(kt + 1) * CAP], xn[:, b, kt * P:(kt + 1) * P],
                                      select[:, b * CAP:(b + 1) * CAP], b == 0, b == 1)
                    last.then_inc(sem("gathered"), 1)
                    pe.wait_ge(sem("x_added"), n0 + e + 1)
                    for b in range(NB):
                        last = tr(psum[:, 6, b * P:(b + 1) * P], select[:, b * CAP:(b + 1) * CAP])
                    last.then_inc(sem("selectT_done"), 1)
                    pe.wait_ge(sem("gathered_lo"), n0 + e + 1)
                    ffn(hgT, 1, EXP_GROUPS, group0 + EXP_GROUPS * e)
                    pe.wait_ge(sem("y_ready"), n0 + e + 1)
                    pe.wait_ge(sem("selectT_out"), n0 + e + 1)
                    for b in range(NB):
                        for half in range(2):
                            last = mm(psum[:, 4 + 2 * b + half, :], selectT[:, b * P:(b + 1) * P],
                                      y_tok[:, half * W:(half + 1) * W])
                    last.then_inc(sem("scattered"), 1)

            pe.wait_ge(sem("const_in"), 16)
            pe.wait_ge(sem("rows_in"), 16 * 3)
            tr(psum[:, 4, 0:4], gain_rows[0:4, 0, 0:P], 4)
            tr(psum[:, 4, P:P + 96], gain_rows[0:96, 1, 0:P], 96).then_inc(sem("gains_transposed"), 1)

            for layer in range(DEPTH):
                for s in ORDER:
                    if s in UNITS:
                        unit(layer, s)
                    elif s in NORM_NO:
                        norm(layer, s)
                    elif s == "ab":
                        hv = [a.rearrange("p (k n) -> p k n", k=KT) for a in halves(hT)]
                        for b in range(NB):
                            for k in range(KT):
                                last = mm3(psum[:, 4, b * 8:(b + 1) * 8], pick(hv, slice(None), k, slice(b * P, (b + 1) * P)),
                                           pick(w_small, slice(None), layer, k), k == 0, k == KT - 1)
                        last.then_inc(sem("ab_done"), 1)
                    elif s == "gd_tok":
                        for part in range(3):
                            pe.wait_ge(sem("conv_ready"), 3 * layer + part + 1)
                            if part == 2:
                                pe.wait_ge(sem("gd_tok_out"), 3 * layer + 1)
                            first = 6 if part == 1 else 4
                            if part == 0:
                                pe.wait_ge(sem("ab_out"), layer + 1)
                            for b in range(NB):
                                for h in range(H):
                                    last = tr(pb(first, 2)[:, b * W + h * P:b * W + (h + 1) * P],
                                              conv_out[:, part * 1024 + h * SEQ + b * P:part * 1024 + h * SEQ + (b + 1) * P])
                            last.then_inc(sem("gd_tok_done"), 1)
                    elif s == "gd_gate":
                        pe.wait_ge(sem("g_ready"), layer + 1)
                        pe.wait_ge(sem("gd_tok_out"), 3 * layer + 3)
                        mm(psum[:, 4, 0:8], c("triu"), s16[:, 0, 0:8]).then_inc(sem("gc_done"), 1)
                        for i in range(8):
                            last = mm(pb(6, 2)[:, i * P:(i + 1) * P], bc(s16[:, 0, i:i + 1], [P, P]), c("triu"))
                        last.then_inc(sem("gc_done"), 1)
                    elif s == "gd_T":
                        pe.wait_ge(sem("gd_scaled"), layer + 1)
                        blocks_T(4, kn).then_inc(sem("gd_T_done"), 1)
                        blocks_T(6, kb).then_inc(sem("gd_T_done"), 1)
                        pe.wait_ge(sem("gd_T_out"), 4 * layer + 1)
                        blocks_T(4, qn).then_inc(sem("gd_T_done"), 1)
                        pe.wait_ge(sem("qg_ready"), layer + 1)
                        pe.wait_ge(sem("gd_T_out"), 4 * layer + 2)
                        blocks_T(6, qn[:, W:], 4).then_inc(sem("gd_T_done"), 1)
                    elif s == "da_T":
                        pe.wait_ge(sem("gd_T_out"), 4 * layer + 4)
                        pe.wait_ge(sem("roped"), 2 * layer + 2)
                        heads_T(4, W0).then_inc(sem("da_T_done"), 1)
                        heads_T(6, W1).then_inc(sem("da_T_done"), 1)
                    elif s == "gd_LA":
                        pe.wait_ge(sem("da_T_out"), 2 * layer + 2)
                        for i in range(8):
                            q = slice(i * P, (i + 1) * P)
                            last = mm(pb(4, 2)[:, q], knT[:, q], kbT[:, q])
                        last.then_inc(sem("gd_LA_done"), 1)
                        for i in range(8):
                            q = slice(i * P, (i + 1) * P)
                            last = mm(pb(6, 2)[:, q], knT[:, q], qnT[:, q])
                        last.then_inc(sem("gd_LA_done"), 1)
                        pe.wait_ge(sem("lT_ready"), layer + 1)
                        blocks_T(4, lT).then_inc(sem("gd_LA_done"), 1)
                    elif s[:5] == "da_sc":
                        i = int(s[-1])
                        wd = (i + 1) * P
                        pe.wait_ge(sem("intra_ready"), layer + 1)
                        pe.wait_ge(sem("l_ready"), layer + 1)
                        if i:
                            pe.wait_ge(sem("da_o_out"), NB * layer + 1)
                        for half in range(2):
                            rows = slice(half * 64, half * 64 + 64)
                            for h in range(H):
                                last = mm(pb(4 + 2 * half, 2)[:, h * SEQ:h * SEQ + wd],
                                          da_qT[rows, h * SEQ + i * P:h * SEQ + (i + 1) * P],
                                          da_kT[rows, h * SEQ:h * SEQ + wd])
                        last.then_inc(sem("da_scores"), 1)
                    elif s[:5] == "da_pv":
                        nk = transpose_probs(layer, int(s[-1]), W23, "da", 4)
                        for h in range(H):
                            for k in range(nk):
                                last = mm(psum[:, 6, h * P:(h + 1) * P], W0[:, (h * nk + k) * P:(h * nk + k + 1) * P],
                                          da_v[:, k * W + h * P:k * W + (h + 1) * P], k == 0, k == nk - 1)
                        last.then_inc(sem("da_o_done"), 1)
                    elif s == "gd_inv":
                        pe.wait_ge(sem("da_o_out"), NB * layer + 2)
                        with pe.Fori(0, 6) as it:
                            n = 6 * layer + it
                            pe.wait_ge(sem("bT_ready"), n + 1)
                            pe.wait_ge(sem("tu_ready"), 2 * n + 2 * layer + 2)
                            for i in range(8):
                                q = slice(i * P, (i + 1) * P)
                                last = mm(pb(4, 2)[:, q], bT[:, q], t_[:, q])
                            last.then_inc(sem("m1_done"), 1)
                            pe.wait_ge(sem("m1_out"), n + 1)
                            for i in range(8):
                                q = slice(i * P, (i + 1) * P)
                                last = mm(pb(6, 2)[:, q], uT[:, q], m1[:, q])
                            last.then_inc(sem("tmu_done"), 1)
                            for i in range(8):
                                q = slice(i * P, (i + 1) * P)
                                last = mm(pb(4, 2)[:, q], m1[:, q], uT[:, q])
                            last.then_inc(sem("tmu_done"), 1)
                    elif s == "da_out":
                        pe.wait_ge(sem("da_normed"), layer + 1)
                        pe.wait_ge(sem("tu_ready"), 14 * layer + 14)
                        heads_T(4, W1).then_inc(sem("da_oT_done"), 1)
                    elif s[:5] == "sb_sc":
                        i = int(s[-1])
                        wd = (i + 1) * P
                        pe.wait_ge(sem("oaT_ready"), layer + 1)
                        if i:
                            pe.wait_ge(sem("obT_ready"), NB * layer + 1)
                        for h in range(H):
                            last = mm(pb(4, 2)[:, h * wd:(h + 1) * wd], sb_qT[:, h * SEQ + i * P:h * SEQ + (i + 1) * P],
                                      sb_kT[:, h * SEQ:h * SEQ + wd])
                        last.then_inc(sem("sb_scores"), 1)
                    elif s[:5] == "sb_pv":
                        nk = transpose_probs(layer, int(s[-1]), W2, "sb", 4)
                        for h in range(H):
                            for k in range(nk):
                                last = mm(psum[:, 6, h * P:(h + 1) * P], sb_v[:, k * W + h * P:k * W + (h + 1) * P],
                                          W0[:, (h * nk + k) * P:(h * nk + k + 1) * P], k == 0, k == nk - 1)
                        last.then_inc(sem("sb_oT_done"), 1)
                    elif s == "gd_scan":
                        pe.wait_ge(sem("kd_ready"), layer + 1)
                        pe.wait_ge(sem("obT_ready"), NB * layer + 2)
                        for h in range(H):
                            q = slice(h * P, (h + 1) * P)
                            last = mm(psum[:, 4, q], uT[:, q], vb[:, q])
                        last.then_inc(sem("scan_done"), 1)
                        for h in range(H):
                            q = slice(h * P, (h + 1) * P)
                            last = mm(psum[:, 5, q], kbg[:, q], uT[:, W + h * P:W + (h + 1) * P])
                        last.then_inc(sem("scan_done"), 1)
                        pe.wait_ge(sem("scan_out_act"), 2 * layer + 1)
                        for h in range(H):
                            q = slice(h * P, (h + 1) * P)
                            last = mm(psum[:, 6, q], kn[:, q], v_new[:, q])
                        last.then_inc(sem("scan_done"), 1)
                        for h in range(H):
                            q = slice(h * P, (h + 1) * P)
                            last = mm(psum[:, 7, q], intraT[:, q], v_new[:, q])
                        last.then_inc(sem("scan_done"), 1)
                        pe.wait_ge(sem("scan_out_dve"), 4 * layer + 2)
                        for h in range(H):
                            q, q1 = slice(h * P, (h + 1) * P), slice(W + h * P, W + (h + 1) * P)
                            mm(psum[:, 4, q], uT[:, q1], vb[:, q1], True, False)
                            last = mm(psum[:, 4, q], wT[:, q], state[:, q], False, True)
                        last.then_inc(sem("scan_done"), 1)
                        pe.wait_ge(sem("scan_out_act"), 2 * layer + 2)
                        for h in range(H):
                            q, q1 = slice(h * P, (h + 1) * P), slice(W + h * P, W + (h + 1) * P)
                            mm(psum[:, 5, q], qgT[:, q], state[:, q], True, False)
                            last = mm(psum[:, 5, q], intraT[:, q1], v_new[:, q1], False, True)
                        last.then_inc(sem("scan_done"), 1)
                    elif s == "gd_out":
                        pe.wait_ge(sem("gd_normed"), layer + 1)
                        heads_T(6, gd_o).then_inc(sem("gd_oT_done"), 1)
                    elif s[:4] == "x_sc":
                        i = int(s[-1])
                        if i == 0:
                            wait_evacuated(pe, unit_index(layer, "x_q"))
                        else:
                            pe.wait_ge(sem("oxT_ready"), NB * layer + 1)
                        for h in range(H):
                            last = mm(pb(4, 2)[:, h * SEQ:(h + 1) * SEQ], x_qT[:, h * SEQ + i * P:h * SEQ + (i + 1) * P],
                                      x_kT[:, h * SEQ:(h + 1) * SEQ])
                        last.then_inc(sem("x_scores"), 1)
                    elif s[:4] == "x_pv":
                        nk = transpose_probs(layer, int(s[-1]), W2, "x", 6)
                        for h in range(H):
                            for k in range(nk):
                                last = mm(psum[:, 4, h * P:(h + 1) * P], x_v[:, k * W + h * P:k * W + (h + 1) * P],
                                          W0[:, (h * nk + k) * P:(h * nk + k + 1) * P], k == 0, k == nk - 1)
                        last.then_inc(sem("x_oT_done"), 1)
                    elif s == "ffn":
                        pe.wait_ge(sem("norm_out"), 4 * layer + 4)
                        if layer == 0:
                            ffn(hT, NB, DENSE_GROUPS, 0)
                        else:
                            hv = [a.rearrange("p (k n) -> p k n", k=KT) for a in halves(hT_router)]
                            for b in range(NB):
                                for k in range(KT):
                                    last = mm3(psum[:, 4, b * 8:(b + 1) * 8],
                                               pick(hv, slice(None), k, slice(b * P, (b + 1) * P)),
                                               pick(w_small, slice(None), 2, k), k == 0, k == KT - 1)
                            last.then_inc(sem("router_done"), 1)
                            pe.wait_ge(sem("chosen_ready"), 1)
                            chosen = top[:, 0, :]
                            mm(psum[:, 5, 0:8], c("striu"), chosen[:, 0:8])
                            mm(psum[:, 5, 8:16], c("ones", 0, P), chosen[:, 0:8], True, False)
                            mm(psum[:, 5, 8:16], c("striu"), chosen[:, 8:16], False, True)
                            mm(psum[:, 5, 16:24], c("ones", 0, P), chosen[:, 0:8], True, False)
                            mm(psum[:, 5, 16:24], c("ones", 0, P), chosen[:, 8:16], False, True) \
                                .then_inc(sem("ranks_done"), 1)
                            expert(DENSE_GROUPS, 0)
                            pe.wait_ge(sem("overflow_known"), 1)
                            with pe.If(pe.value_load(overflow[0:1, 0:1], min_val=0, max_val=1) > 0):
                                expert(DENSE_GROUPS + EXP_GROUPS * N_EXP, N_EXP)

        POW = [(layer, s) for layer in range(DEPTH) for s in ORDER
               if s in NORM_NO or s in ("gd_scale", "da_out", "gd_out")] + [(DEPTH, "final")]

        def pow_width(s):
            return {"gd_scale": 16, "da_out": 8, "gd_out": 8}.get(s, NB)

        @block.gpsimd
        def _(pool):
            pool.wait_ge(sem("const_in"), 16)
            for i, (layer, s) in enumerate(POW):
                n = pow_width(s)
                pool.wait_ge(sem("pow_in"), i + 1)
                nc.gpsimd.tensor_tensor(pow_out[:, 0:n], pow_in[:, 0:n], c("nhalf", 0, n), ALU.pow) \
                    .then_inc(sem("pow_out"), 1)

        @block.scalar
        def _(act):
            steps = [0]

            def step(ins):
                steps[0] += 1
                ins.then_inc(sem("act_step"), 1)
                act.wait_ge(sem("act_step"), steps[0])

            def f(o, i, func, **kw):
                return nc.scalar.activation(o, i, func, **kw)

            def copy(o, i):
                return nc.scalar.activation(o, i, ACT.Copy)

            act.dma_start(gain_rows[0:2, 0, 0:P], t["da_subln"]).then_inc(sem("rows_in"), 16)
            act.dma_start(gain_rows[2:4, 0, 0:P], t["gd_norm"]).then_inc(sem("rows_in"), 16)
            act.dma_start(gain_rows[0:96, 1, 0:P], t["gd_conv"].rearrange("l j (c p) -> (l j c) p", p=P)) \
               .then_inc(sem("rows_in"), 16)
            act.dma_start(const[:, :], t["const"]).then_inc(sem("const_in"), 16)
            for i, name in enumerate(("lam_q1", "lam_k1", "lam_q2", "lam_k2")):
                act.dma_start(lam_in[:, i, :], t[name].rearrange("l d -> (l d)").partition_broadcast(P)) \
                   .then_inc(sem("small_in"), 16)
            act.dma_start(a_log[:, :], t["gd_a_log"].rearrange("l h -> (l h)").partition_broadcast(P)) \
               .then_inc(sem("small_in"), 16)
            act.dma_start(dt_bias[:, :], t["gd_dt_bias"].rearrange("l h -> (l h)").partition_broadcast(P)) \
               .then_inc(sem("small_in"), 16)
            small = w_small_in.rearrange("p (l n) -> p l n", n=8)
            act.dma_start(small[:, 0:16, :],
                          t["w_in"][:, :, AB0:AB0 + 8].rearrange("l (k p) n -> p (l k) n", p=P)).then_inc(sem("small_in"), 16)
            act.dma_start(small[:, 16:24, :], t["w_router"][0].rearrange("(k p) n -> p k n", p=P)) \
               .then_inc(sem("small_in"), 16)
            act.dma_start(GAIN_ROW, t["norm_mix"][0].partition_broadcast(P)).then_inc(sem("gain_in"), 16)
            nc.scalar.preload_act_table_set("natural_log_exp_and_others")
            act.wait_ge(sem("small_in"), 16 * 8)
            copy(w_small[0][:, :, :, :].rearrange("p l k n -> p (l k n)"), w_small_in).then_inc(sem("init_act"), 1)
            f(neg_a[:, :], a_log[:, :], ACT.Exp).then_inc(sem("init_act"), 1)
            act.wait_ge(sem("lam_dots"), 1)
            f(lam_e[:, :, :], lam_e[:, :, :], ACT.Exp).then_inc(sem("init_act"), 1)

            def norm_squares(layer, s):
                i = 4 * layer + NORM_NO.get(s, 0)
                src, junk = x, [xn[:, 0, :], xn[:, 1, :]]
                if s == "norm_mem":
                    src, junk = v3(mem_tok, NB), [W0, W1]
                    act.wait_ge(sem("mem_in"), 16 * (layer + 1))
                    act.wait_ge(sem("obT_ready"), NB * (layer + 1))
                elif s == "norm_mix":
                    if layer == 0:
                        act.wait_ge(sem("x_in"), 16)
                    else:
                        act.wait_ge(sem("ffn_added"), 1)
                elif s != "final":
                    wait_evacuated(act, unit_index(layer, "out1" if s == "norm_x" else "x_o.1"))
                for b in range(NB):
                    last = f(junk[b], src[:, b, :], ACT.Square, accum_out=ss[:, b:b + 1])
                last.then_inc(sem("squares_ready"), 1)

            def norm_high(layer, s):
                i = 4 * layer + NORM_NO[s]
                dst = halves(memT if s == "norm_mem" else hT)[0]
                for j in range(2):
                    act.wait_ge(sem("norm_transposed"), 2 * i + j + 1)
                    copy(dst[:, j * 1024:(j + 1) * 1024], pb(4 + 2 * j, 2)).then_inc(sem("norm_hi"), 1)
                name, row = {"norm_mix": ("norm_mem", layer), "norm_mem": ("norm_x", layer), "norm_x": ("norm_ffn", layer),
                             "norm_ffn": ("norm_mix", layer + 1)}[s]
                nxt = t["norm_final"] if row == DEPTH else t[name][row]
                act.wait_ge(sem("xn_ready"), i + 1)
                act.dma_start(GAIN_ROW, nxt.partition_broadcast(P)).then_inc(sem("gain_in"), 16)

            def split(layer, u):
                for q in unit_pieces(layer, u):
                    act.wait_ge(sem(f"piece_in{q % RAW}"), 16 * (q // RAW + 1))
                    if q >= SPLIT:
                        act.wait_ge(sem("piece_used"), q - SPLIT + 1)
                    copy(split_slot(q)[0], raw_slot(q)).then_inc(sem("hi_ready"), 1)

            def ffn(groups, group0, blocks, uses):
                wd = blocks * FF_UNIT

                def high(g, par, j, fresh=False):
                    n = g // 2 if isinstance(g, int) else g[1]
                    k = g if isinstance(g, int) else g[0]
                    act.wait_ge(sem(f"ffn_in{par}{j}"), (16 if j == 2 else 32) * (uses[par] + n + 1))
                    if not (isinstance(group0, int) and isinstance(k, int) and group0 + k == 0):
                        act.wait_ge(sem(f"ffn_used{j}"), group0 + k)
                    copy(ffn_split(j)[0], ffn_raw(par, j)).then_inc(sem(f"ffn_hi{j}"), 1)

                def hidden_high(g, par):
                    act.wait_ge(sem("hiddenT_done"), group0 + g + 1)
                    copy(rtile(2)[:, par * W:par * W + wd], psum[:, blocks * par, 0:wd]).then_inc(sem("hidden_hi"), 1)

                def nth(g, par, p, d):
                    if isinstance(g, int):
                        return g + d
                    return g + d, p + 1 + (par + d) // 2

                def group(g, par, p=None):
                    first = isinstance(g, int) and g == 0
                    last = isinstance(g, int) and g == groups - 1
                    if not first:
                        hidden_high(g - 1, 1 - par)
                    if not last:
                        high(nth(g, par, p, 1), 1 - par, 0)
                    act.wait_ge(sem("ffn_used1"), group0 + g + 1)
                    gate = psum[:, blocks * par:blocks * (par + 1), 0:FF_UNIT]
                    f(silu_g[par][:, 0:wd].rearrange("p (b n) -> p b n", b=blocks), gate, ACT.Silu) \
                        .then_inc(sem("silu_ready"), 1)
                    if not last:
                        high(nth(g, par, p, 1), 1 - par, 1)
                    high(nth(g, par, p, 0), par, 2)
                    if last:
                        hidden_high(g, par)

                high(0, 0, 0)
                high(0, 0, 1)
                pairs = (groups - 3) // 2
                group(0, 0)
                group(1, 1)
                with act.Fori(0, pairs) as p:
                    group(2 * p + 2, 0, p)
                    group(2 * p + 3, 1, p)
                for g in range(2 + 2 * pairs, groups):
                    group(g, g % 2)

            def expert(group0, n0, uses):
                with act.Fori(0, N_EXP) as e:
                    act.wait_ge(sem("gathered"), n0 + e + 1)
                    copy(halves(hgT)[0], pb(2, 2)).then_inc(sem("gathered_hi"), 1)
                    act.wait_ge(sem("selectT_done"), n0 + e + 1)
                    copy(selectT, psum[:, 6, 0:SEQ]).then_inc(sem("selectT_out"), 1)
                    half = EXP_GROUPS // 2
                    ffn(EXP_GROUPS, group0 + EXP_GROUPS * e, 1, [half * e + uses[0], half * e + uses[1]])
                    act.wait_ge(sem("ffn_used2"), group0 + EXP_GROUPS * e + EXP_GROUPS)
                    copy(y_tok, pb(4, 2)).then_inc(sem("y_ready"), 1)

            target = {"gd_z": z, "da_v": da_v, "sb_k": sb_kT, "sb_v": sb_v, "x_k": x_kT, "x_v": x_v}

            for layer in range(DEPTH):
                for s in ORDER:
                    if s == "norm_mix":
                        if layer:
                            for j in range(2):
                                act.wait_ge(sem(f"ffn_used{j}"), DENSE_GROUPS)
                        split(layer, "gd_q")
                    if s in UNITS:
                        for where in units_after(layer, s):
                            split(*where)
                    if s[:4] == "br_c":
                        i = int(s[-1])
                        act.wait_ge(sem("merged_sum"), 2 * layer + i + 1)
                        copy(halves(mergedT)[0][:, i * 1024:(i + 1) * 1024], merged[:, i * 1024:(i + 1) * 1024]) \
                            .then_inc(sem("merged_hi"), 1)
                    elif s in UNITS and UNITS[s][4] == "act":
                        wait_computed(act, layer, s)
                        src = pb(unit_banks(layer, s), 2)
                        done = sem("unit_out_act")
                        if s in ("gd_q", "gd_k", "gd_v"):
                            if s == "gd_q":
                                act.wait_ge(sem("pads_ready"), layer + 1)
                            part = ("gd_q", "gd_k", "gd_v").index(s)
                            f(conv_in[:, 4 * part:4 * part + 4, 3:], v3(src, 4), ACT.Copy).then_inc(done, 1)
                        elif s in ("sb_q", "x_q"):
                            f(sb_qT, src, ACT.Copy, scale=float(SB_DIM) ** -0.5).then_inc(done, 1)
                        elif s[:4] == "gate":
                            if s == "gate_a0":
                                act.wait_ge(sem("da_probsT"), NB * (layer + 1))
                            elif s == "gate_b0":
                                act.wait_ge(sem("obT_ready"), NB * (layer + 1))
                            elif s == "gate_c0":
                                wait_evacuated(act, unit_index(layer, "br_b.1"))
                                act.wait_ge(sem("merged_b"), layer + 1)
                            f(W2 if s[-1] == "0" else W3, src, ACT.Sigmoid).then_inc(done, 1)
                        else:
                            copy(target[s], src).then_inc(done, 1)
                    elif s in NORM_NO:
                        norm_squares(layer, s)
                        norm_high(layer, s)
                    elif s[:5] == "conv_":
                        part = "qkv".index(s[5])
                        n = 3 * layer + part
                        act.wait_ge(sem("conv_taps"), n + 1)
                        if part:
                            act.wait_ge(sem("conv_ready"), n)
                        f(scratch, conv_out[:, part * 1024:(part + 1) * 1024], ACT.Sigmoid).then_inc(sem("conv_sig"), 1)
                    elif s == "gd_tok":
                        for part in range(3):
                            act.wait_ge(sem("gd_tok_done"), 3 * layer + part + 1)
                            copy(tile(16 + part), pb(6 if part == 1 else 4, 2)).then_inc(sem("gd_tok_out"), 1)
                    elif s == "gd_gate":
                        act.wait_ge(sem("ab_out"), layer + 1)
                        nc.scalar.preload_act_table_set("natural_log_exp_and_others")
                        step(f(s16[:, 5, 0:8], s16[:, 4, 0:8], ACT.Exp, scale=-1.0))
                        step(f(s16[:, 2, 0:8], s16[:, 1, 0:8], ACT.Abs))
                        step(f(s16[:, 2, 0:8], s16[:, 2, 0:8], ACT.Exp, scale=-1.0))
                        f(s16[:, 3, 0:8], s16[:, 2, 0:8], ACT.Ln, bias=c("ones", 0, 1)).then_inc(sem("gates_act"), 1)
                    elif s == "gd_scale":
                        act.wait_ge(sem("decay_logs"), layer + 1)
                        f(decayT, decayT, ACT.Exp)
                        f(s16[:, 8, 8:16], s16[:, 8, 0:8], ACT.Exp)
                        f(s16[:, 9, 8:16], s16[:, 9, 0:8], ACT.Exp).then_inc(sem("decay_exp"), 1)
                    elif s == "gd_T":
                        for i, dst in enumerate((knT, kbT, qnT, qgT)):
                            act.wait_ge(sem("gd_T_done"), 4 * layer + i + 1)
                            copy(dst, pb(4 + 2 * (i % 2), 1 if i == 3 else 2)).then_inc(sem("gd_T_out"), 1)
                    elif s == "da_T":
                        for i, dst in enumerate((da_qT, da_kT)):
                            act.wait_ge(sem("da_T_done"), 2 * layer + i + 1)
                            copy(dst, pb(4 + 2 * i, 2)).then_inc(sem("da_T_out"), 1)
                    elif s == "gd_LA":
                        act.wait_ge(sem("gd_LA_done"), 3 * layer + 3)
                        copy(l_, pb(4, 2)).then_inc(sem("l_ready"), 1)
                    elif s == "gd_inv":
                        with act.Fori(0, 6) as it:
                            n = 6 * layer + it
                            act.wait_ge(sem("m1_done"), n + 1)
                            copy(m1, pb(4, 2)).then_inc(sem("m1_out"), 1)
                    elif s[:5] == "da_sc":
                        i = int(s[-1])
                        wd = (i + 1) * P
                        act.wait_ge(sem("da_max"), NB * layer + i + 1)
                        for j in range(8):
                            p = W23[:, j * wd:(j + 1) * wd]
                            last = f(p, p, ACT.Exp, bias=s16b[:, 1, j:j + 1], accum_out=s16b[:, 2, j:j + 1])
                        last.then_inc(sem("da_exp"), 1)
                    elif s[:5] == "da_pv":
                        i = int(s[-1])
                        wd = (i + 1) * P
                        act.wait_ge(sem("da_probsT"), NB * layer + i + 1)
                        copy(W0[:, 0:4 * wd], pb(4, 2)[:, 0:4 * wd]).then_inc(sem("da_probsT_out"), 1)
                    elif s == "da_out":
                        act.wait_ge(sem("da_oT_done"), layer + 1)
                        f(halves(oaT)[0], pb(4, 2), ACT.Copy, scale=gain[:, layer:layer + 1]).then_inc(sem("oaT_hi"), 1)
                    elif s[:5] == "sb_sc":
                        i = int(s[-1])
                        wd = (i + 1) * P
                        p = W2[:, 0:4 * wd]
                        act.wait_ge(sem("sb_scores"), NB * layer + i + 1)
                        wait_evacuated(act, unit_index(layer, "br_a.1"))
                        nc.scalar.preload_act_table_set("natural_log_exp_and_others")
                        step(f(p, pb(4, 2)[:, 0:4 * wd], ACT.Abs))
                        step(f(p, p, ACT.Exp, scale=-1.0))
                        f(p, p, ACT.Ln, bias=c("ones", 0, 1)).then_inc(sem("sb_ln"), 1)
                        act.wait_ge(sem("sb_log"), NB * layer + i + 1)
                        f(p, W3[:, 0:4 * wd], ACT.Exp).then_inc(sem("sb_probs"), 1)
                    elif s[:5] == "sb_pv":
                        i = int(s[-1])
                        wd = (i + 1) * P
                        act.wait_ge(sem("sb_probsT"), NB * layer + i + 1)
                        copy(W0[:, 0:4 * wd], pb(4, 2)[:, 0:4 * wd]).then_inc(sem("sb_probsT_out"), 1)
                        act.wait_ge(sem("sb_oT_done"), NB * layer + i + 1)
                        copy(v3(halves(obT)[0], 4)[:, :, i * P:(i + 1) * P], v3(psum[:, 6, :], 4)).then_inc(sem("obT_hi"), 1)
                    elif s[:4] == "x_sc":
                        i = int(s[-1])
                        act.wait_ge(sem("x_max"), NB * layer + i + 1)
                        for j in range(H):
                            last = f(W2[:, j * SEQ:(j + 1) * SEQ], pb(4, 2)[:, j * SEQ:(j + 1) * SEQ], ACT.Exp,
                                     bias=s16b[:, 4, j:j + 1], accum_out=s16b[:, 5, j:j + 1])
                        last.then_inc(sem("x_exp"), 1)
                    elif s[:4] == "x_pv":
                        i = int(s[-1])
                        act.wait_ge(sem("x_probsT"), NB * layer + i + 1)
                        copy(W0, pb(6, 2)).then_inc(sem("x_probsT_out"), 1)
                        act.wait_ge(sem("x_oT_done"), NB * layer + i + 1)
                        copy(v3(halves(oxT)[0], 4)[:, :, i * P:(i + 1) * P], v3(psum[:, 4, :], 4)).then_inc(sem("oxT_hi"), 1)
                    elif s == "gd_scan":
                        for i, n in enumerate((1, 5)):
                            act.wait_ge(sem("scan_done"), 6 * layer + n)
                            copy(v_new[:, i * W:(i + 1) * W], psum[:, 4, :]).then_inc(sem("scan_out_act"), 1)
                    elif s == "gd_out":
                        act.wait_ge(sem("tu_ready"), 14 * (layer + 1))
                        f(l_, z, ACT.Sigmoid).then_inc(sem("z_sig"), 1)
                        act.wait_ge(sem("gd_oT_done"), layer + 1)
                        f(halves(ocT)[0], pb(6, 2), ACT.Copy, scale=gain[:, 2 + layer:3 + layer]).then_inc(sem("ocT_hi"), 1)
                    elif s == "ffn":
                        act.wait_ge(sem("piece_used"), 2 * len(CHUNKS) * (layer + 1))
                        if layer == 0:
                            ffn(DENSE_GROUPS, 0, NB, [0, 0])
                        else:
                            act.wait_ge(sem("top_diff"), 1)
                            f(top[:, 11, 0:2], top[:, 10, 0:2], ACT.Exp).then_inc(sem("top_exp"), 1)
                            uses = [(DENSE_GROUPS + 1) // 2, DENSE_GROUPS // 2]
                            expert(DENSE_GROUPS, 0, uses)
                            act.wait_ge(sem("overflow_known"), 1)
                            with act.If(act.value_load(overflow[0:1, 0:1], min_val=0, max_val=1) > 0):
                                expert(DENSE_GROUPS + EXP_GROUPS * N_EXP, N_EXP,
                                       [n + EXP_GROUPS // 2 * N_EXP for n in uses])
                                act.wait_ge(sem("x_added"), 2 * N_EXP + 1)
            act.wait_ge(sem("x_added"), N_EXP + 1)
            norm_squares(DEPTH, "final")

        @block.vector
        def _(dve):
            v = nc.vector
            steps = [0]

            def step(ins):
                steps[0] += 1
                ins.then_inc(sem("dve_step"), 1)
                dve.wait_ge(sem("dve_step"), steps[0])

            def tt(o, a, b, op):
                return v.tensor_tensor(o, a, b, op)

            def power(layer, s, src, width, scale):
                i = POW.index((layer, s))
                v.tensor_scalar(pow_in[:, 0:width], src, scale, EPS, ALU.mult, ALU.add).then_inc(sem("pow_in"), 1)
                dve.wait_ge(sem("pow_out"), i + 1)

            def norm_scale(layer, s):
                i = 4 * layer + NORM_NO.get(s, 0)
                dve.wait_ge(sem("squares_ready"), i + 1)
                power(layer, s, ss[:, :], NB, 1.0 / D)
                src, dst = (v3(mem_tok, NB),) * 2 if s == "norm_mem" else (x, xn)
                dve.wait_ge(sem("gain_in"), 16 * (i + 1))
                for b in range(NB):
                    last = v.scalar_tensor_tensor(dst[:, b, :], src[:, b, :], pow_out[:, b:b + 1], GAIN_ROW, ALU.mult,
                                                  ALU.mult)
                return last

            def low(where, cols, full):
                hi = stored(where[0], where[2])[:, cols]
                return v.tensor_tensor(halves(where)[1][:, cols], full, hi, ALU.subtract)

            def norm(layer, s):
                i = 4 * layer + NORM_NO[s]
                norm_scale(layer, s).then_inc(sem("xn_ready"), 1)
                where = memT if s == "norm_mem" else hT
                if s == "norm_ffn" and layer == 1:
                    where = hT_router
                dve.wait_ge(sem("norm_hi"), 2 * i + 2)
                for j in range(2):
                    last = low(where, slice(j * 1024, (j + 1) * 1024), pb(4 + 2 * j, 2))
                last.then_inc(sem("norm_out"), 1)

            def split(layer, u):
                for q in unit_pieces(layer, u):
                    dve.wait_ge(sem("hi_ready"), q + 1)
                    tt(split_slot(q)[1], raw_slot(q), split_slot(q, False)[0], ALU.subtract).then_inc(sem("lo_ready"), 1)

            def conv(layer, part):
                n = 3 * layer + part
                wait_evacuated(dve, unit_index(layer, ("gd_q", "gd_k", "gd_v")[part]))
                for j in range(4):
                    for ch in range(4 * part, 4 * part + 4):
                        tap = gain[:, 4 + layer * 48 + j * 12 + ch:5 + layer * 48 + j * 12 + ch]
                        o = conv_out[:, ch * SEQ:(ch + 1) * SEQ]
                        src = conv_in[:, ch, j:j + SEQ]
                        if j == 0:
                            last = v.tensor_scalar(o, src, tap, None, ALU.mult)
                        else:
                            last = v.scalar_tensor_tensor(o, src, tap, o, ALU.mult, ALU.add)
                    if j < 3:
                        step(last)
                last.then_inc(sem("conv_taps"), 1)
                o = conv_out[:, part * 1024:(part + 1) * 1024]
                dve.wait_ge(sem("conv_sig"), n + 1)
                tt(o, o, scratch, ALU.mult).then_inc(sem("conv_ready"), 1)

            def rope(layer, s):
                tab = s[3]
                dst = W0 if tab == "q" else W1
                src = pb(unit_banks(layer, s), 2)
                wait_computed(dve, layer, s)
                sin = W2
                for b in range(NB):
                    cs = c("cos_" + tab, b * DA_DIM, (b + 1) * DA_DIM)
                    sn = c("sin_" + tab, b * DA_DIM, (b + 1) * DA_DIM)
                    part = src[:, b * W:(b + 1) * W]
                    tt(v3(dst[:, b * W:(b + 1) * W], 8), v3(part, 8), rep(cs, 8), ALU.mult)
                    for half in range(2):
                        o = v3(sin[:, b * W:(b + 1) * W], 8)[:, :, half * 32:half * 32 + 32]
                        i = v3(part, 8)[:, :, (1 - half) * 32:(1 - half) * 32 + 32]
                        last = tt(o, i, rep(sn[:, half * 32:half * 32 + 32], 8), ALU.mult)
                last.then_inc(sem("unit_out_dve"), 1)
                wait_evacuated(dve, unit_index(layer, s))
                tt(dst, dst, sin[:, :], ALU.add).then_inc(sem("roped"), 1)

            def ffn(groups, group0, blocks):
                wd = blocks * FF_UNIT

                def low_half(g, j):
                    dve.wait_ge(sem(f"ffn_hi{j}"), group0 + g + 1)
                    par = parity[j]
                    parity[j] = 1 - par
                    tt(ffn_split(j)[1], ffn_raw(par, j), ffn_split(j, False)[0], ALU.subtract).then_inc(sem(f"ffn_lo{j}"), 1)

                def hidden_low(g, par):
                    dve.wait_ge(sem("hidden_hi"), group0 + g + 1)
                    q = slice(par * W, par * W + wd)
                    tt(rtile(3)[:, q], psum[:, blocks * par, 0:wd], stored(2)[:, q], ALU.subtract).then_inc(sem("hidden_lo"), 1)

                def group(g, par):
                    first = isinstance(g, int) and g == 0
                    last = isinstance(g, int) and g == groups - 1
                    if not first:
                        hidden_low(g - 1, 1 - par)
                    if not last:
                        low_half(g + 1, 0)
                    dve.wait_ge(sem("silu_ready"), group0 + g + 1)
                    up = psum[:, blocks * par:blocks * (par + 1), FF_UNIT:2 * FF_UNIT]
                    tt(v3(hid[par][:, 0:wd], blocks), v3(silu_g[par][:, 0:wd], blocks), up, ALU.mult) \
                        .then_inc(sem("hidden_ready"), 1)
                    if not last:
                        low_half(g + 1, 1)
                    low_half(g, 2)
                    if last:
                        hidden_low(g, par)

                parity = [0, 0, 0]
                low_half(0, 0)
                low_half(0, 1)
                ffn_loop(dve, groups, group)

            def expert(group0, n0, ranks):
                with dve.Fori(0, N_EXP) as e:
                    for b in range(NB):
                        last = v.tensor_scalar(select[:, b * CAP:(b + 1) * CAP], c("iota"),
                                               top[:, ranks, bass.ds(b * 8 + e, 1)], None, ALU.is_equal)
                    last.then_inc(sem("select_ready"), 1)
                    dve.wait_ge(sem("gathered_hi"), n0 + e + 1)
                    low(hgT, slice(0, 1024), pb(2, 2)).then_inc(sem("gathered_lo"), 1)
                    ffn(EXP_GROUPS, group0 + EXP_GROUPS * e, 1)
                    dve.wait_ge(sem("scattered"), n0 + e + 1)
                    for b in range(NB):
                        last = v.scalar_tensor_tensor(x[:, b, :], pb(4 + 2 * b, 2), top[:, 6, bass.ds(b * 8 + e, 1)],
                                                      x[:, b, :], ALU.mult, ALU.add)
                    last.then_inc(sem("x_added"), 1)

            dve.wait_ge(sem("small_in"), 16 * 8)
            for i in range(2):
                step(tt(lam_in[:, 2 * i, :], lam_in[:, 2 * i, :], lam_in[:, 2 * i + 1, :], ALU.mult))
            v.tensor_reduce(lam_e[:, 0, :], v3(lam_in[:, 0, :], DEPTH), X, ALU.add)
            v.tensor_reduce(lam_e[:, 1, :], v3(lam_in[:, 2, :], DEPTH), X, ALU.add).then_inc(sem("lam_dots"), 1)
            dve.wait_ge(sem("init_act"), 3)
            tt(w_small[1][:, :, :, :].rearrange("p l k n -> p (l k n)"), w_small_in,
               w_small[0][:, :, :, :].rearrange("p l k n -> p (l k n)").bitcast(F32), ALU.subtract)
            v.tensor_scalar(neg_a[:, :], neg_a[:, :], -1.0, None, ALU.mult)
            step(tt(neg_lam[:, :], lam_e[:, 1, :], lam_e[:, 0, :], ALU.subtract))
            for layer in range(DEPTH):
                last = v.tensor_scalar(neg_lam[:, layer:layer + 1], neg_lam[:, layer:layer + 1], -LAM_INIT[layer], None,
                                       ALU.add)
            step(last)
            dve.wait_ge(sem("gains_transposed"), 1)
            v.tensor_copy(gain[:, 4:100], psum[:, 4, P:P + 96])
            v.tensor_copy(gain[:, 2:4], psum[:, 4, 2:4])
            for layer in range(DEPTH):
                last = v.tensor_scalar(gain[:, layer:layer + 1], psum[:, 4, layer:layer + 1], 1.0 - LAM_INIT[layer], None,
                                       ALU.mult)
            step(last)

            for layer in range(DEPTH):
                for s in ORDER:
                    if s == "norm_mix":
                        split(layer, "gd_q")
                    if s in UNITS:
                        for where in units_after(layer, s):
                            split(*where)
                    if s in ("da_q", "da_k"):
                        rope(layer, s)
                    elif s in UNITS and UNITS[s][4] == "dve":
                        g = unit_index(layer, s)
                        src = pb(unit_banks(layer, s), 2)
                        wait_computed(dve, layer, s)
                        if s[:2] == "br":
                            i = int(s[-1])
                            gate = W2 if i == 0 else W3
                            dst = merged[:, i * 1024:(i + 1) * 1024]
                            wait_evacuated(dve, unit_index(layer, f"gate_{s[3]}{i}"))
                            if s[3] == "a":
                                tt(dst, src, gate, ALU.mult).then_inc(sem("unit_out_dve"), 1)
                            else:
                                tt(gate, src, gate, ALU.mult).then_inc(sem("unit_out_dve"), 1)
                                wait_evacuated(dve, g)
                                last = tt(dst, dst, gate, ALU.add)
                                if s[3] == "c":
                                    last.then_inc(sem("merged_sum"), 1)
                                    dve.wait_ge(sem("merged_hi"), 2 * layer + i + 1)
                                    low(mergedT, slice(i * 1024, (i + 1) * 1024), dst).then_inc(sem("merged_ready"), 1)
                                elif i == 1:
                                    last.then_inc(sem("merged_b"), 1)
                        else:
                            half = int(s[-1])
                            xs = x[:, :, half * W:(half + 1) * W]
                            tt(xs, xs, v3(src, 2), ALU.add).then_inc(sem("unit_out_dve"), 1)
                    elif s in NORM_NO:
                        if s == "norm_mix":
                            v.memset(conv_in[:, :, 0:3], 0.0).then_inc(sem("pads_ready"), 1)
                        norm(layer, s)
                    elif s[:5] == "conv_":
                        conv(layer, "qkv".index(s[5]))
                    elif s == "ab":
                        dve.wait_ge(sem("ab_done"), layer + 1)
                        src = v3(psum[:, 4, 0:16], 2)
                        tt(v3(s16[:, 1, 0:8], 2), src[:, :, 0:4], rep(dt_bias[:, layer * H:(layer + 1) * H], 2), ALU.add)
                        v.tensor_copy(v3(s16[:, 4, 0:8], 2), src[:, :, 4:8]).then_inc(sem("ab_out"), 1)
                    elif s == "gd_gate":
                        dve.wait_ge(sem("gates_act"), layer + 1)
                        step(v.scalar_tensor_tensor(s16[:, 2, 0:8], s16[:, 1, 0:8], 0.0, s16[:, 3, 0:8], ALU.max, ALU.add))
                        tt(v3(s16[:, 0, 0:8], 2), v3(s16[:, 2, 0:8], 2), rep(neg_a[:, layer * H:(layer + 1) * H], 2),
                           ALU.mult).then_inc(sem("g_ready"), 1)
                        step(v.tensor_scalar(s16[:, 5, 0:8], s16[:, 5, 0:8], 1.0, None, ALU.add))
                        step(v.reciprocal(s16[:, 4, 0:8], s16[:, 5, 0:8]))
                    elif s == "gd_scale":
                        beta, eg, ekd = s16[:, 4, 0:8], s16[:, 8, 8:16], s16[:, 9, 8:16]
                        dve.wait_ge(sem("gd_tok_out"), 3 * layer + 3)
                        for i, src in enumerate((qn, kn)):
                            step(tt(scratch, src, src, ALU.mult))
                            step(v.tensor_reduce(s16[:, 6, 8 * i:8 * i + 8], v3(scratch, 8), X, ALU.add))
                        dve.wait_ge(sem("gc_done"), 2 * layer + 2)
                        spread = v3(pb(6, 2), 8)
                        step(v.tensor_copy(s16[:, 8, 0:8], psum[:, 4, 0:8]))
                        step(tt(v3(decayT, 8), spread, each(s16[:, 8, 0:8], P), ALU.subtract))
                        v.tensor_scalar(decayT, decayT, 0.0, None, ALU.min)
                        tt(s16[:, 9, 0:8], spread[:, :, P - 1], s16[:, 8, 0:8], ALU.subtract).then_inc(sem("decay_logs"), 1)
                        power(layer, s, s16[:, 6, :], 16, 1.0)
                        step(v.tensor_scalar(s16[:, 7, 0:8], pow_out[:, 0:8], float(SB_DIM) ** -0.5, None, ALU.mult))
                        tt(v3(qn, 8), v3(qn, 8), each(s16[:, 7, 0:8], P), ALU.mult)
                        step(tt(v3(kn, 8), v3(kn, 8), each(pow_out[:, 8:16], P), ALU.mult))
                        tt(v3(kb, 8), v3(kn, 8), each(beta, P), ALU.mult)
                        tt(v3(vb, 8), v3(vb, 8), each(beta, P), ALU.mult).then_inc(sem("gd_scaled"), 1)
                        dve.wait_ge(sem("decay_exp"), layer + 1)
                        dve.wait_ge(sem("gd_scaled"), layer + 1)
                        step(tt(v3(kbg, 4), v3(kb[:, W:], 4), each(eg[:, 4:8], P), ALU.mult))
                        v.tensor_scalar(kbg, kbg, -1.0, None, ALU.mult)
                        step(tt(v3(decayT, 8), v3(decayT, 8), rep(c("triu"), 8), ALU.mult))
                    elif s == "gd_T":
                        eg, ekd = s16[:, 8, 8:16], s16[:, 9, 8:16]
                        dve.wait_ge(sem("gd_T_done"), 4 * layer + 3)
                        tt(v3(qn[:, W:], 4), v3(qn[:, W:], 4), each(eg[:, 4:8], P), ALU.mult).then_inc(sem("qg_ready"), 1)
                        tt(v3(kn[:, 0:W], 4), v3(kn[:, 0:W], 4), each(ekd[:, 0:4], P), ALU.mult).then_inc(sem("kd_ready"), 1)
                    elif s == "gd_LA":
                        dve.wait_ge(sem("gd_LA_done"), 3 * layer + 1)
                        step(tt(lT, pb(4, 2), decayT, ALU.mult))
                        tt(v3(lT, 8), v3(lT, 8), rep(c("striu"), 8), ALU.mult).then_inc(sem("lT_ready"), 1)
                        dve.wait_ge(sem("gd_LA_done"), 3 * layer + 2)
                        tt(intraT, pb(6, 2), decayT, ALU.mult).then_inc(sem("intra_ready"), 1)
                        dve.wait_ge(sem("lT_ready"), layer + 1)
                        dve.wait_ge(sem("l_ready"), layer + 1)
                        tt(v3(uT, 8), v3(lT, 8), rep(c("levelT", 0, P), 8), ALU.mult)
                        step(tt(v3(t_, 8), v3(l_, 8), rep(c("level", 0, P), 8), ALU.mult))
                        for m in (uT, t_):
                            v.scalar_tensor_tensor(v3(m, 8), v3(m, 8), -1.0, rep(c("ident"), 8), ALU.mult, ALU.add) \
                                .then_inc(sem("tu_ready"), 1)
                    elif s == "gd_inv":
                        at = CONST["levelT"][0]
                        dve.wait_ge(sem("tu_ready"), 14 * layer + 2)
                        with dve.Fori(0, 6) as it:
                            n = 6 * layer + it
                            dve.wait_ge(sem("tu_ready"), 14 * layer + 2 + 2 * it)
                            tt(v3(bT, 8), v3(lT, 8), rep(const[:, bass.ds(at + P + it * P, P)], 8), ALU.mult) \
                                .then_inc(sem("bT_ready"), 1)
                            dve.wait_ge(sem("tmu_done"), 2 * n + 1)
                            tt(t_, t_, pb(6, 2), ALU.subtract).then_inc(sem("tu_ready"), 1)
                            dve.wait_ge(sem("tmu_done"), 2 * n + 2)
                            tt(uT, uT, pb(4, 2), ALU.subtract).then_inc(sem("tu_ready"), 1)
                    elif s[:5] == "da_sc":
                        i = int(s[-1])
                        wd = (i + 1) * P
                        n = NB * layer + i + 1
                        dve.wait_ge(sem("da_scores"), n)
                        for half in range(2):
                            last = tt(v3(W23[:, half * 4 * wd:(half + 1) * 4 * wd], 4), v3(pb(4 + 2 * half, 2), 4)[:, :, 0:wd],
                                      rep(c("causal", SEQ - wd, SEQ), 4), ALU.add)
                        step(last)
                        p8 = v3(W23[:, 0:8 * wd], 8)
                        step(v.tensor_reduce(s16b[:, 0, 0:8], p8, X, ALU.max))
                        v.tensor_scalar(s16b[:, 1, 0:8], s16b[:, 0, 0:8], -1.0, None, ALU.mult).then_inc(sem("da_max"), 1)
                        dve.wait_ge(sem("da_exp"), n)
                        step(v.reciprocal(s16b[:, 3, 0:8], s16b[:, 2, 0:8]))
                        step(v.tensor_scalar(s16b[:, 3, 4:8], s16b[:, 3, 4:8], neg_lam[:, layer:layer + 1], None, ALU.mult))
                        step(tt(p8, p8, each(s16b[:, 3, 0:8], wd), ALU.mult))
                        tt(W23[:, 0:4 * wd], W23[:, 0:4 * wd], W23[:, 4 * wd:8 * wd], ALU.add).then_inc(sem("da_probs"), 1)
                    elif s[:5] == "da_pv":
                        i = int(s[-1])
                        dve.wait_ge(sem("da_o_done"), NB * layer + i + 1)
                        v.tensor_copy(W1[:, i * W:(i + 1) * W], psum[:, 6, :]).then_inc(sem("da_o_out"), 1)
                    elif s == "da_out":
                        dve.wait_ge(sem("da_o_out"), NB * (layer + 1))
                        step(tt(W0, W1, W1, ALU.mult))
                        step(v.tensor_reduce(s16b[:, 6, 0:8], v3(W0, 8), X, ALU.add))
                        power(layer, s, s16b[:, 6, 0:8], 8, 1.0 / P)
                        tt(v3(W1, 8), v3(W1, 8), each(pow_out[:, 0:8], P), ALU.mult).then_inc(sem("da_normed"), 1)
                        dve.wait_ge(sem("oaT_hi"), layer + 1)
                        v.scalar_tensor_tensor(halves(oaT)[1], pb(4, 2), gain[:, layer:layer + 1], stored(oaT[0]), ALU.mult,
                                               ALU.subtract).then_inc(sem("oaT_ready"), 1)
                    elif s[:5] == "sb_sc":
                        i = int(s[-1])
                        wd = (i + 1) * P
                        n = NB * layer + i + 1
                        scores, lg = pb(4, 2)[:, 0:4 * wd], W3[:, 0:4 * wd]
                        dve.wait_ge(sem("sb_ln"), n)
                        step(v.scalar_tensor_tensor(lg, scores, 0.0, W2[:, 0:4 * wd], ALU.max, ALU.add))
                        step(tt(v3(lg, 4), v3(lg, 4), rep(c("strict01", SEQ - wd, SEQ), 4), ALU.mult))
                        for h in range(H):
                            rev = W3[:, h * wd:(h + 1) * wd][:, ::-1]
                            last = v.tensor_tensor_scan(W1[:, h * wd:(h + 1) * wd][:, ::-1], c("ones", 0, wd), rev, 0.0,
                                                        ALU.mult, ALU.add)
                        step(last)
                        step(tt(lg, scores, W1[:, 0:4 * wd], ALU.subtract))
                        tt(v3(lg, 4), v3(lg, 4), rep(c("strict_neg", SEQ - wd, SEQ), 4), ALU.add).then_inc(sem("sb_log"), 1)
                    elif s[:5] == "sb_pv":
                        i = int(s[-1])
                        q = slice(i * P, (i + 1) * P)
                        dve.wait_ge(sem("obT_hi"), NB * layer + i + 1)
                        tt(v3(halves(obT)[1], 4)[:, :, q], v3(psum[:, 6, :], 4), v3(stored(obT[0]), 4)[:, :, q],
                           ALU.subtract).then_inc(sem("obT_ready"), 1)
                    elif s[:4] == "x_sc":
                        i = int(s[-1])
                        n = NB * layer + i + 1
                        dve.wait_ge(sem("x_scores"), n)
                        step(v.tensor_reduce(s16b[:, 7, 0:4], v3(pb(4, 2), 4), X, ALU.max))
                        v.tensor_scalar(s16b[:, 4, 0:4], s16b[:, 7, 0:4], -1.0, None, ALU.mult).then_inc(sem("x_max"), 1)
                        dve.wait_ge(sem("x_exp"), n)
                        step(v.reciprocal(s16b[:, 5, 4:8], s16b[:, 5, 0:4]))
                        tt(v3(W2, 4), v3(W2, 4), each(s16b[:, 5, 4:8], SEQ), ALU.mult).then_inc(sem("x_probs"), 1)
                    elif s[:4] == "x_pv":
                        i = int(s[-1])
                        q = slice(i * P, (i + 1) * P)
                        dve.wait_ge(sem("oxT_hi"), NB * layer + i + 1)
                        tt(v3(halves(oxT)[1], 4)[:, :, q], v3(psum[:, 4, :], 4), v3(stored(oxT[0]), 4)[:, :, q],
                           ALU.subtract).then_inc(sem("oxT_ready"), 1)
                    elif s == "gd_scan":
                        for n, dst, b in ((2, wT, 5), (3, state, 6), (4, gd_o[:, 0:W], 7), (6, gd_o[:, W:], 5)):
                            dve.wait_ge(sem("scan_done"), 6 * layer + n)
                            v.tensor_copy(dst, psum[:, b, :]).then_inc(sem("scan_out_dve"), 1)
                    elif s == "gd_out":
                        dve.wait_ge(sem("scan_out_dve"), 4 * (layer + 1))
                        step(tt(lT, gd_o, gd_o, ALU.mult))
                        step(v.tensor_reduce(s16[:, 6, 0:8], v3(lT, 8), X, ALU.add))
                        power(layer, s, s16[:, 6, 0:8], 8, 1.0 / P)
                        step(tt(v3(gd_o, 8), v3(gd_o, 8), each(pow_out[:, 0:8], P), ALU.mult))
                        dve.wait_ge(sem("z_sig"), layer + 1)
                        step(tt(z, z, l_, ALU.mult))
                        tt(gd_o, gd_o, z, ALU.mult).then_inc(sem("gd_normed"), 1)
                        dve.wait_ge(sem("ocT_hi"), layer + 1)
                        v.scalar_tensor_tensor(halves(ocT)[1], pb(6, 2), gain[:, 2 + layer:3 + layer], stored(ocT[0]), ALU.mult,
                                               ALU.subtract).then_inc(sem("ocT_ready"), 1)
                    elif s == "ffn" and layer == 0:
                        ffn(DENSE_GROUPS, 0, NB)
                        dve.wait_ge(sem("ffn_used2"), DENSE_GROUPS)
                        xf = x.rearrange("p b d -> p (b d)")
                        tt(xf, xf, pb(4, 4), ALU.add).then_inc(sem("ffn_added"), 1)
                    elif s == "ffn":
                        iota8 = c("iota8")
                        dve.wait_ge(sem("router_done"), 1)
                        step(v.tensor_copy(top[:, 1, :], psum[:, 4, 0:16]))
                        for b in range(NB):
                            lg, mx = top[:, 1, b * 8:b * 8 + 8], top[:, 2, b * 8:b * 8 + 8]
                            step(v.max(mx, lg))
                            step(v.max_index(top_i[:, b, :], mx, lg))
                            step(v.tensor_copy(top[:, 9, b * 8:b * 8 + 8], top_i[:, b, :]))
                            for j in range(2):
                                step(v.tensor_scalar(top[:, 3 + j, b * 8:b * 8 + 8], iota8, top[:, 9, b * 8 + j:b * 8 + j + 1],
                                                     None, ALU.is_equal))
                        tops = v3(top[:, 2, :], 2)
                        tt(top[:, 10, 0:2], tops[:, :, 1], tops[:, :, 0], ALU.subtract).then_inc(sem("top_diff"), 1)
                        tt(top[:, 0, :], top[:, 3, :], top[:, 4, :], ALU.add).then_inc(sem("chosen_ready"), 1)
                        dve.wait_ge(sem("top_exp"), 1)
                        step(v.tensor_scalar(top[:, 12, 0:2], top[:, 11, 0:2], 1.0, None, ALU.add))
                        step(v.reciprocal(top[:, 13, 0:2], top[:, 12, 0:2]))
                        step(tt(top[:, 14, 0:2], top[:, 11, 0:2], top[:, 13, 0:2], ALU.mult))
                        for b in range(NB):
                            q = slice(b * 8, b * 8 + 8)
                            step(v.tensor_scalar(top[:, 5, q], top[:, 3, q], top[:, 13, b:b + 1], None, ALU.mult))
                            step(v.scalar_tensor_tensor(top[:, 6, q], top[:, 4, q], top[:, 14, b:b + 1], top[:, 5, q],
                                                        ALU.mult, ALU.add))
                        dve.wait_ge(sem("ranks_done"), 1)
                        step(v.scalar_tensor_tensor(top[:, 15, :], psum[:, 5, 0:16], 1.0, top[:, 0, :], ALU.add, ALU.mult))
                        step(v.tensor_scalar(top[:, 7, :], top[:, 15, :], -1.0, None, ALU.add))
                        step(v.tensor_scalar(top[:, 8, :], top[:, 7, :], -float(CAP), None, ALU.add))
                        step(v.tensor_reduce(top[:, 16, 0:1], psum[:, 5, 16:24], X, ALU.max))
                        v.tensor_scalar(overflow[:, :], top[:, 16, 0:1], float(CAP), None, ALU.is_gt) \
                            .then_inc(sem("overflow_known"), 1)
                        dve.wait_ge(sem("overflow_known"), 1)
                        v.tensor_copy(top[:, 17, 0:1], top[:, 16, 0:1]).then_inc(sem("x_added"), 1)
                        expert(DENSE_GROUPS, 0, 7)
                        with dve.If(dve.value_load(overflow[0:1, 0:1], min_val=0, max_val=1) > 0):
                            expert(DENSE_GROUPS + EXP_GROUPS * N_EXP, N_EXP, 8)
            last = norm_scale(DEPTH, "final")
            last.then_inc(sem("out_ready"), 1)


def constants():
    a = np.zeros((P, N_CONST), np.float32)

    def put(name, m):
        at, n = CONST[name]
        a[:, at:at + n] = m.reshape(P, n)

    p, j = np.arange(P)[:, None], np.arange(P)[None, :]
    k = np.arange(SEQ)[None, :]
    put("ident", (p == j).astype(np.float32))
    put("triu", (p <= j).astype(np.float32))
    put("striu", (p < j).astype(np.float32))
    put("ones", np.ones((P, SEQ), np.float32))
    put("causal", np.where(k <= p + P, 0.0, NEG).astype(np.float32))
    put("strict_neg", np.where(k < p + P, 0.0, NEG).astype(np.float32))
    put("strict01", (k < p + P).astype(np.float32))
    level = np.stack([((p // m) % 2 == 1) & (j // m == p // m - 1) for m in LEVELS], 1)
    put("level", level.astype(np.float32))
    put("levelT", np.stack([((j // m) % 2 == 1) & (p // m == j // m - 1) for m in LEVELS], 1).astype(np.float32))
    inv = (1.0 / (np.float32(10000.0) ** (np.arange(0, DA_DIM, 2, dtype=np.float32) / np.float32(DA_DIM)))).astype(np.float32)
    ang = np.arange(SEQ, dtype=np.float32)[:, None] * inv[None, :]
    cos, sin = np.cos(ang), np.sin(ang)
    for name, m in (("cos", np.concatenate([cos, cos], 1)), ("sin", np.concatenate([-sin, sin], 1))):
        m = m.reshape(NB, P, DA_DIM).transpose(1, 0, 2).astype(np.float32)
        put(name + "_k", m)
        put(name + "_q", m * np.float32(DA_DIM ** -0.5))
    put("iota", np.broadcast_to(np.arange(P, dtype=np.float32), (P, P)))
    put("nhalf", np.full((P, 16), -0.5, np.float32))
    put("iota8", np.broadcast_to(np.arange(8, dtype=np.float32), (P, 8)))
    return a


_INS = ["x", "mem", "norm_mix", "w_in", "gd_conv", "lam_q1", "lam_k1", "lam_q2", "lam_k2", "da_subln", "gd_a_log",
        "gd_dt_bias", "gd_norm", "w_br_a", "w_br_b", "w_br_c", "w_out", "norm_x", "norm_mem", "w_q_x", "w_kv_x", "w_o_x",
        "norm_ffn", "w_gate_dense", "w_up_dense", "w_down_dense", "w_router", "w_gate_exp", "w_up_exp", "w_down_exp",
        "norm_final"]


def kernel(**inputs):
    import concourse.bacc as _bacc
    from concourse.bass_utils import run_bass_kernel_spmd as _run

    nc = _bacc.Bacc("TRN2", target_bir_lowering=False, num_devices=1)
    arrays = {f"in_{name}_dram": np.ascontiguousarray(inputs[name]) for name in _INS}
    arrays["const_dram"] = constants()
    t = {}
    for name in _INS + ["const"]:
        key = "const_dram" if name == "const" else f"in_{name}_dram"
        a = arrays[key]
        t[name] = nc.dram_tensor(key, a.shape, mybir.dt.from_np(a.dtype), kind="ExternalInput").ap()
    out = nc.dram_tensor("out_0_dram", (1, SEQ, D), F32, kind="ExternalOutput").ap()
    hybrid_layers(nc, t, out)
    r = _run(nc, [arrays], core_ids=[0])
    return r.results[0]["out_0_dram"]
```

```python
from contextlib import ExitStack

import numpy as np
import concourse.bass as bass
from concourse import mybir

F32 = mybir.dt.float32
F32R = mybir.dt.float32r
I32 = mybir.dt.int32
U32 = mybir.dt.uint32
ALU = mybir.AluOpType
ACT = mybir.ActivationFunctionType
X = mybir.AxisListType.X

P = 128
D = 1024
SEQ = 256
NB = SEQ // P
KT = D // P
DEPTH = 2
H = 4
W = 512
DA_DIM = 64
SB_DIM = 128
N_EXP = 8
FF_DENSE = 2816
FF_EXP = 3584
CAP = 128
EPS = 1e-6
NEG = -1e30
RAW = 4
SPLIT = 5
GD0 = 6 * W
AB0 = 10 * W
GATE0 = 10 * W + 2 * H
LAM_INIT = [0.8 - 0.6 * float(np.exp(-0.3 * layer)) for layer in range(DEPTH)]
LEVELS = [1, 2, 4, 8, 16, 32, 64]

CONST = {}
_at = 0
for _name, _n in [("ident", P), ("triu", P), ("striu", P), ("ones", SEQ), ("causal", SEQ), ("strict_neg", SEQ),
                  ("strict01", SEQ), ("level", 7 * P), ("levelT", 7 * P), ("cos_q", 2 * DA_DIM), ("sin_q", 2 * DA_DIM),
                  ("cos_k", 2 * DA_DIM), ("sin_k", 2 * DA_DIM), ("iota", P), ("nhalf", 16), ("iota8", 8)]:
    CONST[_name] = (_at, _n)
    _at += _n
N_CONST = _at

CHUNKS = ["gd_q", "gd_k", "gd_v", "da_q", "da_k", "da_v", "sb_q", "sb_k", "sb_v", "gd_z",
          "gate_b0", "gate_a0", "gate_a1", "br_a", "gate_b1", "gate_c0", "gate_c1", "br_b", "br_c",
          "x_k", "out0", "out1", "x_v", "x_q", "x_o"]
COLUMN = {"da_q": 0, "da_k": W, "da_v": 2 * W, "sb_q": 3 * W, "sb_k": 4 * W, "sb_v": 5 * W,
          "gd_q": GD0, "gd_k": GD0 + W, "gd_v": GD0 + 2 * W, "gd_z": GD0 + 3 * W}
for _i, _g in enumerate("abc"):
    COLUMN[f"gate_{_g}0"] = GATE0 + _i * D
    COLUMN[f"gate_{_g}1"] = GATE0 + _i * D + W

UNITS = {}
for _c in CHUNKS:
    _eng = "dve" if _c in ("da_q", "da_k", "out0", "out1") or _c[:2] == "br" or _c == "x_o" else "act"
    _kind = "tok" if _c in ("gd_z", "da_q", "da_k", "da_v", "sb_v", "x_v", "out0", "out1", "x_o") else "T"
    if _c[:2] == "br" or _c == "x_o":
        UNITS[_c + ".0"] = (_c, _kind, H, 0, _eng)
        UNITS[_c + ".1"] = (_c, _kind, H, W, _eng)
    else:
        UNITS[_c] = (_c, _kind, KT, 0, _eng)
UNIT_NO = {u: i for i, u in enumerate(UNITS)}
N_UNITS = len(UNITS)

ORDER = """norm_mix gd_q#0 gd_q#1 gd_k#0 gd_k#1 conv_q gd_v#0 gd_v#1 conv_k ab da_q#0 ab_T da_q#1 conv_v da_k#0 da_k#1
da_v#0 da_v#1 gd_tok sb_q#0 gd_gate sb_q#1 gd_scale sb_k#0 sb_k#1 gd_T da_T gd_LA
da_sc0 sb_v#0 sb_v#1 da_pT0 gd_z#0 da_pv0 da_sc1 gd_z#1 gate_b0#0 da_pT1 gate_b0#1 da_pv1
gate_a0#0 gate_a0#1 da_out inv_m0 inv_t0 gate_a1#0 inv_m1 inv_t1 gate_a1#1 inv_m2 inv_t2 br_a.0#0
inv_m3 inv_t3 br_a.1#0 inv_m4 inv_t4 gate_b1#0 inv_m5 inv_t5 gate_b1#1
sb_sc0 gate_c0#0 gate_c0#1 sb_pT0 sb_pv0 sb_sc1 gate_c1#0 gate_c1#1 sb_pT1 sb_pv1
gd_scan br_b.0#0 br_b.1#0 gd_out norm_mem br_c.0#0 br_c.1#0 x_k#0 x_k#1 out0#0 out0#1 out1#0 out1#1
x_v#0 x_v#1 norm_x x_q#0 x_q#1 x_sc0 x_sc1 x_pT0 x_pT1 x_pv0 x_pv1 x_o.0#0 x_o.1#0 norm_ffn ffn""".split()
SPLIT_FIRST = ("gd_scale", "da_sc0", "da_sc1", "sb_sc0", "sb_sc1")
NORM_NO = {"norm_mix": 0, "norm_mem": 1, "norm_x": 2, "norm_ffn": 3}


def unit_pieces(layer, u):
    c, _, k, col, _ = UNITS[u]
    first = 2 * (layer * len(CHUNKS) + CHUNKS.index(c))
    return [first, first + 1] if k == KT else [first + col // W]


FF_UNIT = 256
DENSE_GROUPS = FF_DENSE // FF_UNIT
EXP_GROUPS = FF_EXP // FF_UNIT
assert FF_DENSE % FF_UNIT == 0 and FF_EXP % FF_UNIT == 0 and EXP_GROUPS % 2 == 0 and DENSE_GROUPS % 2 == 1


def hybrid_layers(nc, t, out):
    ctx = ExitStack()
    with ctx:
        def sb(name, shape, dt=F32):
            return ctx.enter_context(nc.sbuf_tensor(name, shape, dt))

        sems = {}

        def sem(name):
            if name not in sems:
                sems[name] = ctx.enter_context(nc.semaphore(name))
            return sems[name]

        const = sb("const", [P, N_CONST])
        base = (nc.sbuf_base + 31) // 32 * 32
        work = sb("work", [P, 44, 1024])
        r_views = {}
        conv_in = sb("conv_in", [P, 12, SEQ + 3])
        gain = sb("gain", [P, 4 + 96])
        gain_rows = conv_in
        w_small = [sb(f"w_small_{part}", [P, 3, KT, 8], F32R) for part in ("hi", "lo")]
        lam_e = sb("lam_e", [P, 2, DEPTH])
        neg_lam = sb("neg_lam", [P, DEPTH])
        a_log = sb("a_log", [P, DEPTH * H])
        dt_bias = sb("dt_bias", [P, DEPTH * H])
        neg_a = sb("neg_a", [P, DEPTH * H])
        ss = sb("ss", [P, NB])
        s16 = sb("s16", [P, 10, 16])
        s16b = sb("s16b", [P, 8, 8])
        pow_in = sb("pow_in", [P, 16])
        pow_out = sb("pow_out", [P, 16])
        top = sb("top", [P, 18, 16])
        top_i = sb("top_i", [P, NB, 8], U32)
        overflow = sb("overflow", [P, 1], I32)
        routing = sb("routing", [P, 3, NB, N_EXP + 1])

        def c(name, a=0, b=None):
            at, n = CONST[name]
            return const[:, at + a:at + (n if b is None else b)]

        def v3(ap, a):
            return ap.rearrange("p (a b) -> p a b", a=a)

        def tile(i, n=1):
            return work[:, i:i + n, :].rearrange("p a b -> p (a b)")

        def rtile(i, n=1):
            if (i, n) not in r_views:
                r_views[i, n] = nc.alloc_sbuf_tensor_at(f"work_r_{i}_{n}", [P, n * 1024], F32R, offset=base + 4096 * i)
            return r_views[i, n][:, :]

        def stored(i, n=1):
            return rtile(i, n).bitcast(F32)

        W0, W1, W2, W3 = (tile(i) for i in range(4))
        lam_in = v3(W0[:, 0:4 * DEPTH * DA_DIM], 4)
        w_small_in = W1[:, 0:192]
        W23 = tile(2, 2)
        small_T = W3[0:8, 0:SEQ]
        da_qT, da_kT, da_v = tile(4), tile(5), tile(6)
        merged = tile(4, 2)
        oaT = (6, 7, 1)
        sb_qT, sb_kT, sb_v = tile(8), tile(9), tile(10)
        obT = (6, 7, 1)
        gate_tiles = {"gate_b0": tile(11), "gate_b1": tile(12)}
        mergedT = (11, 8, 2)
        x_qT, x_kT, x_v, oxT = sb_qT, tile(22), sb_v, oaT
        conv_out = tile(13, 3)
        knT, kbT, qnT = tile(13), tile(14), tile(15)
        z, gd_o = tile(13), tile(14)
        m1 = qnT
        wT, state = tile(15)[:, 0:W], tile(15)[:, W:]
        memT = (13, 16, 2)
        qn, kn, vb = tile(16), tile(17), tile(18)
        mem_tok = tile(18, 2)
        kb = uT = tile(19)
        decayT = intraT = tile(20)
        ocT = (20, 21, 1)
        scratch = bT = v_new = tile(21)
        qgT, kbg = tile(22)[:, 0:W], tile(22)[:, W:]
        x = work[:, 23:25, :]
        xn = work[:, 25:27, :]
        hT = (27, 25, 2)
        hT_router = (27, 8, 2)
        RAW_AT, SPLIT_AT, GAIN_ROW = 29, 35, tile(43)
        conv_flat = conv_in[:, :, :].rearrange("p a b -> p (a b)")
        lT, l_, t_ = (conv_flat[:, 1024 * i:1024 * (i + 1)] for i in range(3))
        gate_tiles.update({"gate_a0": W2, "gate_a1": W3, "gate_c0": lT, "gate_c1": t_})
        x_probs, x_probsT = (W2, W3), (W0, W1)
        silu_g = [tile(0)[:, 0:W], tile(0)[:, W:]]
        hid = [tile(1)[:, 0:W], tile(1)[:, W:]]
        hgT = (4, 5, 1)
        y_tok, select, selectT = tile(6), tile(7)[:, 0:NB * CAP], tile(7)[:, 256:256 + SEQ]
        FFN_EARLY = 13

        def halves(where):
            hi, lo, n = where
            return rtile(hi, n), rtile(lo, n)

        def raw_slot(h):
            return tile(RAW_AT + h % RAW)

        def split_slot(h, r=True):
            at = RAW_AT + RAW + 2 * (h % SPLIT)
            return (rtile if r else stored)(at), (rtile if r else stored)(at + 1)

        def ffn_raw(par, j):
            return tile((RAW_AT if par else FFN_EARLY) + 2 * j, 2)

        def ffn_split(j, r=True):
            at = (SPLIT_AT, SPLIT_AT + 4, FFN_EARLY + 6)[j]
            return (rtile if r else stored)(at, 2), (rtile if r else stored)(at + 2, 2)

        psum = ctx.enter_context(nc.psum_tensor("psum", [P, 8, 512], F32))

        def pb(first, n=1):
            return psum[:, first:first + n, :].rearrange("p a b -> p (a b)")

        def bc(ap, shape):
            return ap.to_broadcast(shape)

        def rep(ap, n):
            return ap.unsqueeze(1).to_broadcast([P, n, ap.shape[1]])

        def each(ap, m):
            return ap.unsqueeze(2).to_broadcast([P, ap.shape[1], m])

        block = ctx.enter_context(nc.Block())

        def unit_index(layer, u):
            return layer * N_UNITS + UNIT_NO[u]

        def unit_names():
            return [(layer, u) for layer in range(DEPTH) for u in UNITS]

        def wait_evacuated(eng, g):
            eng_name = UNITS[unit_names()[g][1]][4]
            n = sum(UNITS[u][4] == eng_name for _, u in unit_names()[:g + 1])
            eng.wait_ge(sem(f"unit_out_{eng_name}"), n)

        def unit_banks(layer, u):
            return 2 * (unit_index(layer, u) % 2)

        def wait_computed(eng, layer, u):
            eng.wait_ge(sem("half_used"), 2 * (unit_pieces(layer, u)[-1] + 1))

        def piece_of(layer, s):
            u, i = s.split("#")
            pieces = unit_pieces(layer, u)
            return u, pieces[int(i)], int(i) == len(pieces) - 1

        def halves_ahead(layer, s):
            before = ORDER[ORDER.index(s) - 1]
            if "#" in s and before in SPLIT_FIRST:
                return []
            if s in SPLIT_FIRST:
                s = ORDER[ORDER.index(s) + 1]
            elif "#" not in s:
                return []
            at = 2 * piece_of(layer, s)[1]
            return [h for h in (at + 3, at + 4) if h < 4 * len(CHUNKS) * (layer + 1)]

        def ffn_loop(eng, groups, group):
            pairs = (groups - 3) // 2
            group(0, 0)
            group(1, 1)
            with eng.Fori(0, pairs) as p:
                group(2 * p + 2, 0)
                group(2 * p + 3, 1)
            for g in range(2 + 2 * pairs, groups):
                group(g, g % 2)

        @block.sync
        def _(sp):
            wi = t["w_in"]
            sp.dma_start(x, t["x"][0].rearrange("(b p) d -> p b d", p=P)).then_inc(sem("x_in"), 16)

            def rows_by_cols(dst, view, k):
                return dst.rearrange("p (k n) -> p k n", k=k), view.rearrange("(k p) n -> p k n", p=P)

            def mixer_chunk(layer, name):
                for i in range(4):
                    h = 4 * (layer * len(CHUNKS) + CHUNKS.index(name)) + i
                    if name in COLUMN:
                        w, col = wi, COLUMN[name]
                    elif name[:3] == "out":
                        w, col = t["w_out"], int(name[3]) * W
                    elif name == "x_q":
                        w, col = t["w_q_x"], 0
                    elif name in ("x_k", "x_v"):
                        w, col = t["w_kv_x"], W * int(name == "x_v")
                    else:
                        w, col = (t["w_o_x"] if name == "x_o" else t["w_br_" + name[3]]), i // 2 * W
                    row = (i % 2 if name + ".1" in UNITS else i) * 2 * P
                    if h >= RAW:
                        sp.wait_ge(sem("half_lo"), h - RAW + 1)
                    d, s = rows_by_cols(raw_slot(h), w[layer, row:row + 2 * P, col:col + W], 2)
                    sp.dma_start(d, s).then_inc(sem(f"half_in{h % RAW}"), 16)

            def ffn_stream(layer, groups, group0, gate, up, down, fresh=False):
                def gate_up(g, par, wait):
                    for j in range(2):
                        if wait:
                            sp.wait_ge(sem(f"ffn_lo{j}"), group0 + g - 1)
                        dst = ffn_raw(par, j).rearrange("p (k a n) -> p k a n", k=4, a=2)
                        for a, w in enumerate((gate(g), up(g))):
                            src = w.rearrange("(k p) n -> p k n", p=P)[:, 4 * j:4 * j + 4, :]
                            sp.dma_start(dst[:, :, a, :], src).then_inc(sem(f"ffn_in{par}{j}"), 16)

                def group(g, par):
                    static = isinstance(g, int)
                    if static and g == 0:
                        sp.wait_ge(sem("half_lo"), 4 * len(CHUNKS) * (layer + 1))
                    elif static and g == 1:
                        sp.wait_ge(sem("half_used"), 4 * len(CHUNKS) * (layer + 1))
                    if not static or g < groups - 1:
                        gate_up(g + 1, 1 - par, not (fresh and static and g == 0))
                    if not (fresh and static and g < 2):
                        sp.wait_ge(sem("ffn_lo2"), group0 + g - 1)
                    d, s = rows_by_cols(ffn_raw(par, 2), down(g), 2)
                    sp.dma_start(d, s).then_inc(sem(f"ffn_in{par}2"), 16)

                gate_up(0, 0, not fresh)
                ffn_loop(sp, groups, group)

            def experts(group0):
                def view(w, e, g):
                    return w[0, bass.ds(e, 1), :, bass.ds(g * FF_UNIT, FF_UNIT)].rearrange("e k n -> (e k) n")

                with sp.Fori(0, N_EXP) as e:
                    ffn_stream(DEPTH - 1, EXP_GROUPS, group0 + EXP_GROUPS * e, lambda g: view(t["w_gate_exp"], e, g),
                               lambda g: view(t["w_up_exp"], e, g),
                               lambda g: t["w_down_exp"][0, bass.ds(e, 1), bass.ds(g * FF_UNIT, FF_UNIT), :]
                               .rearrange("e k n -> (e k) n"))

            for layer in range(DEPTH):
                if layer:
                    for j in range(3):
                        sp.wait_ge(sem(f"ffn_lo{j}"), DENSE_GROUPS - 1)
                for name in CHUNKS:
                    mixer_chunk(layer, name)
                if layer == 0:
                    def cols(g):
                        return slice(g * FF_UNIT, (g + 1) * FF_UNIT) if isinstance(g, int) else bass.ds(g * FF_UNIT, FF_UNIT)
                    wait_computed(sp, layer, "x_v")
                    ffn_stream(layer, DENSE_GROUPS, 0, lambda g: t["w_gate_dense"][0, :, cols(g)],
                               lambda g: t["w_up_dense"][0, :, cols(g)], lambda g: t["w_down_dense"][0, cols(g), :],
                               fresh=True)
                else:
                    wait_computed(sp, layer, "x_v")
                    experts(DENSE_GROUPS)
                    sp.wait_ge(sem("overflow_known"), 1)
                    with sp.If(sp.value_load(overflow[0:1, 0:1], min_val=0, max_val=1) > 0):
                        experts(DENSE_GROUPS + EXP_GROUPS * N_EXP)
            sp.wait_ge(sem("out_ready"), 1)
            sp.dma_start(out[0].rearrange("(b p) d -> p b d", p=P), xn).then_inc(sem("out_stored"), 16)
            sp.wait_ge(sem("out_stored"), 16)

        @block.tensor
        def _(pe):
            ident = c("ident")

            def mm(o, a, b, start=True, stop=True):
                return nc.tensor.matmul(o, a, b, start=start, stop=stop)

            def tr(o, a, rows=P):
                return nc.tensor.transpose(o, a, ident[0:rows, 0:rows])

            def mm3(o, a, b, first=True, last=True, check=True):
                nc.tensor.matmul(o, a[0], b[0], start=first, stop=False, skip_group_check=not check)
                nc.tensor.matmul(o, a[0], b[1], start=False, stop=False, skip_group_check=not check)
                return nc.tensor.matmul(o, a[1], b[0], start=False, stop=last, skip_group_check=not check)

            def pick(pair, *index):
                return tuple(p[index] for p in pair)

            source = {"x_k": memT, "x_v": memT, "out0": mergedT, "out1": mergedT, "br_a": oaT, "br_b": obT,
                      "br_c": ocT, "x_o": oxT}

            def piece(layer, s):
                u, q, end = piece_of(layer, s)
                name, kind, k_tiles, _, _ = UNITS[u]
                g = unit_index(layer, u)
                i = int(s[-1])
                if i == 0 and g >= 2:
                    wait_evacuated(pe, g - 2)
                if g == 1 and i == 0:
                    pe.wait_ge(sem("gains_read"), 1)
                if s == "gd_q#0":
                    pe.wait_ge(sem("norm_out"), 4 * layer + 1)
                if s == "x_k#0":
                    pe.wait_ge(sem("norm_out"), 4 * layer + 2)
                if s == "x_q#0":
                    pe.wait_ge(sem("norm_out"), 4 * layer + 3)
                if u == "br_a.0":
                    pe.wait_ge(sem("oaT_ready"), layer + 1)
                if u == "br_b.0":
                    pe.wait_ge(sem("obT_ready"), NB * (layer + 1))
                if u == "br_c.0":
                    pe.wait_ge(sem("ocT_ready"), layer + 1)
                if s == "out0#0":
                    pe.wait_ge(sem("merged_ready"), 2 * (layer + 1))
                if u == "x_o.0":
                    pe.wait_ge(sem("oxT_ready"), NB * (layer + 1))
                x_in = [a.rearrange("p (k n) -> p k n", k=k_tiles) for a in halves(source.get(name, hT))]
                base = unit_banks(layer, u)
                for j in range(2):
                    pe.wait_ge(sem("half_lo"), 2 * q + j + 1)
                    w = [a.rearrange("p (k n) -> p k n", k=2) for a in split_slot(2 * q + j)]
                    first, done = i == 0 and j == 0, end and j == 1
                    if kind == "T":
                        for nt in range(4):
                            o = psum[:, base + nt // 2, (nt % 2) * SEQ:(nt % 2 + 1) * SEQ]
                            for k in range(2):
                                last = mm3(o, pick(w, slice(None), k, slice(nt * P, (nt + 1) * P)),
                                           pick(x_in, slice(None), 4 * i + 2 * j + k),
                                           first and k == 0 and nt % 2 == 0, done and k == 1, False)
                    else:
                        for b in range(NB):
                            for k in range(2):
                                last = mm3(psum[:, base + b, :],
                                           pick(x_in, slice(None), 4 * i + 2 * j + k, slice(b * P, (b + 1) * P)),
                                           pick(w, slice(None), k), first and k == 0, done and k == 1)
                    last.then_inc(sem("half_used"), 1)

            def norm(layer, s):
                i = 4 * layer + NORM_NO[s]
                src = v3(mem_tok, NB) if s == "norm_mem" else xn
                pe.wait_ge(sem("xn_ready"), i + 1)
                for kt in range(KT):
                    for b in range(NB):
                        last = tr(psum[:, 4 + kt // 2, (kt % 2) * SEQ + b * P:(kt % 2) * SEQ + (b + 1) * P],
                                  src[:, b, kt * P:(kt + 1) * P])
                    if kt % 4 == 3:
                        last.then_inc(sem("norm_transposed"), 1)

            def small_product(hv, which):
                for k in range(KT):
                    last = mm3(psum[0:8, 5, 0:SEQ], pick(w_small, slice(None), which, k), pick(hv, slice(None), k),
                               k == 0, k == KT - 1)
                last.then_inc(sem("small_done"), 1)

            def small_by_token(n):
                pe.wait_ge(sem("small_out"), n + 1)
                for b in range(NB):
                    last = tr(psum[:, 4, b * 8:(b + 1) * 8], small_T[:, b * P:(b + 1) * P], 8)
                return last

            def blocks_T(dst_bank, src, n=8):
                for s in range(n):
                    last = tr(pb(dst_bank, 2)[:, s * P:(s + 1) * P], src[:, s * P:(s + 1) * P])
                return last

            def heads_T(dst_bank, src):
                for h in range(H):
                    for b in range(NB):
                        last = tr(pb(dst_bank, 2)[:, h * SEQ + b * P:h * SEQ + (b + 1) * P],
                                  src[:, b * W + h * P:b * W + (h + 1) * P])
                return last

            def key_blocks(i, tag):
                return i + 1 if tag != "x" else NB

            def transpose_probs(layer, i, probs, tag, bank):
                nk = key_blocks(i, tag)
                wd = nk * P
                pe.wait_ge(sem(f"{tag}_probs"), NB * layer + i + 1)
                for h in range(H):
                    for k in range(nk):
                        last = tr(pb(bank, 2)[:, (h * nk + k) * P:(h * nk + k + 1) * P],
                                  probs[:, h * wd + k * P:h * wd + (k + 1) * P])
                last.then_inc(sem(f"{tag}_probsT"), 1)

            def ffn(where, blocks, groups, group0, beside=None):
                src = [a.rearrange("p (k n) -> p k n", k=KT) for a in halves(where)]

                def gate_up(g, par, j):
                    pe.wait_ge(sem(f"ffn_lo{j}"), g + 1)
                    w = [a.rearrange("p (k n) -> p k n", k=4) for a in ffn_split(j)]
                    for b in range(blocks):
                        for k in range(4):
                            last = mm3(psum[:, blocks * par + b, :], pick(src, slice(None), 4 * j + k, slice(b * P, (b + 1) * P)),
                                       pick(w, slice(None), k), j == 0 and k == 0, j == 1 and k == 3)
                    last.then_inc(sem(f"ffn_used{j}"), 1)

                def hidden_T(g, par):
                    pe.wait_ge(sem("hidden_ready"), g + 1)
                    for ft in range(2):
                        for b in range(blocks):
                            last = tr(psum[:, blocks * par, (ft * blocks + b) * P:(ft * blocks + b + 1) * P],
                                      hid[par][:, b * FF_UNIT + ft * P:b * FF_UNIT + (ft + 1) * P])
                    last.then_inc(sem("hiddenT_done"), 1)

                def down(g, par, first, last_group):
                    pe.wait_ge(sem("hidden_lo"), g + 1)
                    pe.wait_ge(sem("ffn_lo2"), g + 1)
                    w = [a.rearrange("p (k n) -> p k n", k=2) for a in ffn_split(2)]
                    hv = [rtile(2 + i)[:, par * W:par * W + 2 * blocks * P].rearrange("p (a n) -> p a n", a=2)
                          for i in range(2)]
                    for ft in range(2):
                        for b in range(blocks):
                            for half in range(2):
                                last = mm3(psum[:, 4 + 2 * b + half, :], pick(hv, slice(None), ft, slice(b * P, (b + 1) * P)),
                                           pick(w, slice(None), ft, slice(half * W, (half + 1) * W)),
                                           first and ft == 0, last_group and ft == 1)
                    last.then_inc(sem("ffn_used2"), 1)

                def group(g, par):
                    gate_up(group0 + g, par, 0)
                    first = isinstance(g, int) and g == 0
                    if not first:
                        hidden_T(group0 + g - 1, 1 - par)
                    if beside and isinstance(g, int) and g in (1, groups - 2):
                        beside(g)
                    gate_up(group0 + g, par, 1)
                    if not first:
                        down(group0 + g - 1, 1 - par, isinstance(g, int) and g == 1, False)
                    if isinstance(g, int) and g == groups - 1:
                        hidden_T(group0 + g, par)
                        if beside:
                            beside(g)
                        down(group0 + g, par, False, True)

                ffn_loop(pe, groups, group)

            def gather(n):
                pe.wait_ge(sem("select_ready"), n + 1)
                for kt in range(KT):
                    for b in range(NB):
                        last = mm(pb(2, 2)[:, kt * CAP:(kt + 1) * CAP], xn[:, b, kt * P:(kt + 1) * P],
                                  select[:, b * CAP:(b + 1) * CAP], b == 0, b == 1)
                last.then_inc(sem("gathered"), 1)

            def scatter(n, m):
                pe.wait_ge(sem("y_ready"), m + 1)
                pe.wait_ge(sem("selectT_out"), n + 1)
                for b in range(NB):
                    for half in range(2):
                        last = mm(psum[:, 2 + 4 * b + half, :], selectT[:, b * P:(b + 1) * P],
                                  y_tok[:, half * W:(half + 1) * W])
                last.then_inc(sem("scattered"), 1)

            def experts(group0, done):
                n0 = done // N_EXP * (N_EXP + 1)
                gather(n0)
                with pe.Fori(0, N_EXP) as e:
                    def beside(g):
                        if g == 1:
                            scatter(done + e, n0 + e)
                        elif g == EXP_GROUPS - 2:
                            pe.wait_ge(sem("x_added"), n0 + e + 1)
                            for b in range(NB):
                                last = tr(psum[:, 2, b * P:(b + 1) * P], select[:, b * CAP:(b + 1) * CAP])
                            last.then_inc(sem("selectT_done"), 1)
                        else:
                            pe.wait_ge(sem("selectT_out"), done + e + 2)
                            gather(n0 + e + 1)

                    pe.wait_ge(sem("gathered_lo"), n0 + e + 1)
                    ffn(hgT, 1, EXP_GROUPS, group0 + EXP_GROUPS * e, beside)
                pe.wait_ge(sem("gathered_lo"), n0 + N_EXP + 1)
                scatter(done + N_EXP, n0 + N_EXP)

            pe.wait_ge(sem("const_in"), 16)

            for layer in range(DEPTH):
                for s in ORDER:
                    if "#" in s:
                        piece(layer, s)
                    elif s in NORM_NO:
                        norm(layer, s)
                        if s == "norm_mix" and layer == 0:
                            pe.wait_ge(sem("rows_in"), 16 * 3)
                            tr(psum[:, 3, 0:4], gain_rows[0:4, 0, 0:P], 4)
                            tr(psum[:, 3, P:P + 96], gain_rows[0:96, 1, 0:P], 96).then_inc(sem("gains_transposed"), 1)
                    elif s == "ab":
                        hv = [a.rearrange("p (k n) -> p k n", k=KT) for a in halves(hT)]
                        small_product(hv, layer)
                    elif s == "ab_T":
                        small_by_token(layer).then_inc(sem("ab_done"), 1)
                    elif s == "gd_tok":
                        for part in range(3):
                            pe.wait_ge(sem("conv_ready"), 3 * layer + part + 1)
                            if part == 2:
                                pe.wait_ge(sem("gd_tok_out"), 3 * layer + 1)
                            first = 6 if part == 1 else 4
                            if part == 0:
                                pe.wait_ge(sem("ab_out"), layer + 1)
                            for b in range(NB):
                                for h in range(H):
                                    last = tr(pb(first, 2)[:, b * W + h * P:b * W + (h + 1) * P],
                                              conv_out[:, part * 1024 + h * SEQ + b * P:part * 1024 + h * SEQ + (b + 1) * P])
                            last.then_inc(sem("gd_tok_done"), 1)
                    elif s == "gd_gate":
                        pe.wait_ge(sem("g_ready"), layer + 1)
                        pe.wait_ge(sem("gd_tok_out"), 3 * layer + 3)
                        mm(psum[:, 4, 0:8], c("triu"), s16[:, 0, 0:8]).then_inc(sem("gc_done"), 1)
                        for i in range(8):
                            last = mm(pb(6, 2)[:, i * P:(i + 1) * P], bc(s16[:, 0, i:i + 1], [P, P]), c("triu"))
                        last.then_inc(sem("gc_done"), 1)
                    elif s == "gd_T":
                        pe.wait_ge(sem("gd_scaled"), layer + 1)
                        blocks_T(4, kn).then_inc(sem("gd_T_done"), 1)
                        blocks_T(6, kb).then_inc(sem("gd_T_done"), 1)
                        pe.wait_ge(sem("gd_T_out"), 4 * layer + 1)
                        blocks_T(4, qn).then_inc(sem("gd_T_done"), 1)
                        pe.wait_ge(sem("qg_ready"), layer + 1)
                        pe.wait_ge(sem("gd_T_out"), 4 * layer + 2)
                        blocks_T(6, qn[:, W:], 4).then_inc(sem("gd_T_done"), 1)
                    elif s == "da_T":
                        pe.wait_ge(sem("gd_T_out"), 4 * layer + 4)
                        pe.wait_ge(sem("roped"), 2 * layer + 2)
                        heads_T(4, W0).then_inc(sem("da_T_done"), 1)
                        heads_T(6, W1).then_inc(sem("da_T_done"), 1)
                    elif s == "gd_LA":
                        pe.wait_ge(sem("da_T_out"), 2 * layer + 2)
                        for i in range(8):
                            q = slice(i * P, (i + 1) * P)
                            last = mm(pb(4, 2)[:, q], knT[:, q], kbT[:, q])
                        last.then_inc(sem("gd_LA_done"), 1)
                        for i in range(8):
                            q = slice(i * P, (i + 1) * P)
                            last = mm(pb(6, 2)[:, q], knT[:, q], qnT[:, q])
                        last.then_inc(sem("gd_LA_done"), 1)
                        pe.wait_ge(sem("lT_ready"), layer + 1)
                        blocks_T(4, lT).then_inc(sem("gd_LA_done"), 1)
                    elif s[:5] == "da_sc":
                        i = int(s[-1])
                        wd = (i + 1) * P
                        pe.wait_ge(sem("intra_ready"), layer + 1)
                        pe.wait_ge(sem("l_ready"), layer + 1)
                        if i:
                            pe.wait_ge(sem("da_o_out"), NB * layer + 1)
                        for half in range(2):
                            rows = slice(half * 64, half * 64 + 64)
                            for h in range(H):
                                last = mm(pb(4 + 2 * half, 2)[:, h * SEQ:h * SEQ + wd],
                                          da_qT[rows, h * SEQ + i * P:h * SEQ + (i + 1) * P],
                                          da_kT[rows, h * SEQ:h * SEQ + wd])
                        last.then_inc(sem("da_scores"), 1)
                    elif s[:5] == "da_pT":
                        transpose_probs(layer, int(s[-1]), W23, "da", 4)
                    elif s[:5] == "da_pv":
                        i = int(s[-1])
                        nk = key_blocks(i, "da")
                        pe.wait_ge(sem("da_probsT_out"), NB * layer + i + 1)
                        for h in range(H):
                            for k in range(nk):
                                last = mm(psum[:, 6, h * P:(h + 1) * P], W0[:, (h * nk + k) * P:(h * nk + k + 1) * P],
                                          da_v[:, k * W + h * P:k * W + (h + 1) * P], k == 0, k == nk - 1)
                        last.then_inc(sem("da_o_done"), 1)
                    elif s[:5] == "inv_m":
                        it = int(s[-1])
                        n = 6 * layer + it
                        if it == 0:
                            pe.wait_ge(sem("oaT_ready"), layer + 1)
                        pe.wait_ge(sem("bT_ready"), n + 1)
                        pe.wait_ge(sem("tu_ready"), 13 * layer + 2 * it + 2)
                        for i in range(8):
                            q = slice(i * P, (i + 1) * P)
                            last = mm(pb(4, 2)[:, q], bT[:, q], t_[:, q])
                        last.then_inc(sem("m1_done"), 1)
                    elif s[:5] == "inv_t":
                        n = 6 * layer + int(s[-1])
                        pe.wait_ge(sem("m1_out"), n + 1)
                        if s != "inv_t5":
                            for i in range(8):
                                q = slice(i * P, (i + 1) * P)
                                last = mm(pb(6, 2)[:, q], uT[:, q], m1[:, q])
                            last.then_inc(sem("tmu_done"), 1)
                        for i in range(8):
                            q = slice(i * P, (i + 1) * P)
                            last = mm(pb(4, 2)[:, q], m1[:, q], uT[:, q])
                        last.then_inc(sem("tmu_done"), 1)
                    elif s == "da_out":
                        pe.wait_ge(sem("da_normed"), layer + 1)
                        heads_T(4, W1).then_inc(sem("da_oT_done"), 1)
                    elif s[:5] == "sb_sc":
                        i = int(s[-1])
                        wd = (i + 1) * P
                        pe.wait_ge(sem("tu_ready"), 13 * layer + 13)
                        if i:
                            pe.wait_ge(sem("obT_ready"), NB * layer + 1)
                        for h in range(H):
                            last = mm(pb(4, 2)[:, h * wd:(h + 1) * wd], sb_qT[:, h * SEQ + i * P:h * SEQ + (i + 1) * P],
                                      sb_kT[:, h * SEQ:h * SEQ + wd])
                        last.then_inc(sem("sb_scores"), 1)
                    elif s[:5] == "sb_pT":
                        transpose_probs(layer, int(s[-1]), W2, "sb", 4)
                    elif s[:5] == "sb_pv":
                        i = int(s[-1])
                        nk = key_blocks(i, "sb")
                        pe.wait_ge(sem("sb_probsT_out"), NB * layer + i + 1)
                        for h in range(H):
                            for k in range(nk):
                                last = mm(psum[:, 6, h * P:(h + 1) * P], sb_v[:, k * W + h * P:k * W + (h + 1) * P],
                                          W0[:, (h * nk + k) * P:(h * nk + k + 1) * P], k == 0, k == nk - 1)
                        last.then_inc(sem("sb_oT_done"), 1)
                    elif s == "gd_scan":
                        pe.wait_ge(sem("kd_ready"), layer + 1)
                        pe.wait_ge(sem("obT_ready"), NB * layer + 2)
                        for h in range(H):
                            q = slice(h * P, (h + 1) * P)
                            last = mm(psum[:, 4, q], uT[:, q], vb[:, q])
                        last.then_inc(sem("scan_done"), 1)
                        for h in range(H):
                            q = slice(h * P, (h + 1) * P)
                            last = mm(psum[:, 5, q], kbg[:, q], uT[:, W + h * P:W + (h + 1) * P])
                        last.then_inc(sem("scan_done"), 1)
                        pe.wait_ge(sem("scan_out_act"), 2 * layer + 1)
                        for h in range(H):
                            q = slice(h * P, (h + 1) * P)
                            last = mm(psum[:, 6, q], kn[:, q], v_new[:, q])
                        last.then_inc(sem("scan_done"), 1)
                        for h in range(H):
                            q = slice(h * P, (h + 1) * P)
                            last = mm(psum[:, 7, q], intraT[:, q], v_new[:, q])
                        last.then_inc(sem("scan_done"), 1)
                        pe.wait_ge(sem("scan_out_dve"), 4 * layer + 2)
                        for h in range(H):
                            q, q1 = slice(h * P, (h + 1) * P), slice(W + h * P, W + (h + 1) * P)
                            mm(psum[:, 4, q], uT[:, q1], vb[:, q1], True, False)
                            last = mm(psum[:, 4, q], wT[:, q], state[:, q], False, True)
                        last.then_inc(sem("scan_done"), 1)
                        pe.wait_ge(sem("scan_out_act"), 2 * layer + 2)
                        for h in range(H):
                            q, q1 = slice(h * P, (h + 1) * P), slice(W + h * P, W + (h + 1) * P)
                            mm(psum[:, 5, q], qgT[:, q], state[:, q], True, False)
                            last = mm(psum[:, 5, q], intraT[:, q1], v_new[:, q1], False, True)
                        last.then_inc(sem("scan_done"), 1)
                    elif s == "gd_out":
                        pe.wait_ge(sem("gd_normed"), layer + 1)
                        heads_T(6, gd_o).then_inc(sem("gd_oT_done"), 1)
                    elif s[:4] == "x_sc":
                        i = int(s[-1])
                        wait_evacuated(pe, unit_index(layer, "x_q"))
                        for h in range(H):
                            last = mm(pb(4 + 2 * i, 2)[:, h * SEQ:(h + 1) * SEQ], x_qT[:, h * SEQ + i * P:h * SEQ + (i + 1) * P],
                                      x_kT[:, h * SEQ:(h + 1) * SEQ])
                        last.then_inc(sem("x_scores"), 1)
                    elif s[:4] == "x_pT":
                        i = int(s[-1])
                        transpose_probs(layer, i, x_probs[i], "x", 2 * i)
                    elif s[:4] == "x_pv":
                        i = int(s[-1])
                        pe.wait_ge(sem("x_probsT_out"), NB * layer + i + 1)
                        for h in range(H):
                            for k in range(NB):
                                last = mm(psum[:, 4 + 2 * i, h * P:(h + 1) * P], x_v[:, k * W + h * P:k * W + (h + 1) * P],
                                          x_probsT[i][:, (h * NB + k) * P:(h * NB + k + 1) * P], k == 0, k == NB - 1)
                        last.then_inc(sem("x_oT_done"), 1)
                    elif s == "ffn":
                        pe.wait_ge(sem("norm_out"), 4 * layer + 4)
                        if layer == 0:
                            ffn(hT, NB, DENSE_GROUPS, 0)
                        else:
                            hv = [a.rearrange("p (k n) -> p k n", k=KT) for a in halves(hT_router)]
                            small_product(hv, 2)
                            small_by_token(DEPTH).then_inc(sem("router_done"), 1)
                            pe.wait_ge(sem("chosen_ready"), 1)
                            chosen = top[:, 0, :]
                            mm(psum[:, 5, 0:8], c("striu"), chosen[:, 0:8])
                            mm(psum[:, 5, 8:16], c("ones", 0, P), chosen[:, 0:8], True, False)
                            mm(psum[:, 5, 8:16], c("striu"), chosen[:, 8:16], False, True)
                            mm(psum[:, 5, 16:24], c("ones", 0, P), chosen[:, 0:8], True, False)
                            mm(psum[:, 5, 16:24], c("ones", 0, P), chosen[:, 8:16], False, True) \
                                .then_inc(sem("ranks_done"), 1)
                            experts(DENSE_GROUPS, 0)
                            pe.wait_ge(sem("overflow_known"), 1)
                            with pe.If(pe.value_load(overflow[0:1, 0:1], min_val=0, max_val=1) > 0):
                                experts(DENSE_GROUPS + EXP_GROUPS * N_EXP, N_EXP)

        POW = [(layer, s) for layer in range(DEPTH) for s in ORDER
               if s in NORM_NO or s in ("gd_scale", "da_out", "gd_out")] + [(DEPTH, "final")]

        def pow_width(s):
            return {"gd_scale": 16, "da_out": 8, "gd_out": 8}.get(s, NB)

        @block.gpsimd
        def _(pool):
            pool.wait_ge(sem("const_in"), 16)
            for i, (layer, s) in enumerate(POW):
                n = pow_width(s)
                pool.wait_ge(sem("pow_in"), i + 1)
                nc.gpsimd.tensor_tensor(pow_out[:, 0:n], pow_in[:, 0:n], c("nhalf", 0, n), ALU.pow) \
                    .then_inc(sem("pow_out"), 1)

        @block.scalar
        def _(act):
            steps = [0]

            def step(ins):
                steps[0] += 1
                ins.then_inc(sem("act_step"), 1)
                act.wait_ge(sem("act_step"), steps[0])

            def f(o, i, func, **kw):
                return nc.scalar.activation(o, i, func, **kw)

            def copy(o, i):
                return nc.scalar.activation(o, i, ACT.Copy)

            act.dma_start(const[:, :], t["const"]).then_inc(sem("const_in"), 16)
            act.dma_start(GAIN_ROW, t["norm_mix"][0].partition_broadcast(P)).then_inc(sem("gain_in"), 16)
            act.dma_start(gain_rows[0:2, 0, 0:P], t["da_subln"]).then_inc(sem("rows_in"), 16)
            act.dma_start(gain_rows[2:4, 0, 0:P], t["gd_norm"]).then_inc(sem("rows_in"), 16)
            act.dma_start(gain_rows[0:96, 1, 0:P], t["gd_conv"].rearrange("l j (c p) -> (l j c) p", p=P)) \
               .then_inc(sem("rows_in"), 16)
            for i, name in enumerate(("lam_q1", "lam_k1", "lam_q2", "lam_k2")):
                act.dma_start(lam_in[:, i, :], t[name].rearrange("l d -> (l d)").partition_broadcast(P)) \
                   .then_inc(sem("small_in"), 16)
            act.dma_start(a_log[:, :], t["gd_a_log"].rearrange("l h -> (l h)").partition_broadcast(P)) \
               .then_inc(sem("small_in"), 16)
            act.dma_start(dt_bias[:, :], t["gd_dt_bias"].rearrange("l h -> (l h)").partition_broadcast(P)) \
               .then_inc(sem("small_in"), 16)
            small = w_small_in.rearrange("p (l n) -> p l n", n=8)
            act.dma_start(small[:, 0:16, :],
                          t["w_in"][:, :, AB0:AB0 + 8].rearrange("l (k p) n -> p (l k) n", p=P)).then_inc(sem("small_in"), 16)
            act.dma_start(small[:, 16:24, :], t["w_router"][0].rearrange("(k p) n -> p k n", p=P)) \
               .then_inc(sem("small_in"), 16)
            nc.scalar.preload_act_table_set("natural_log_exp_and_others")
            def once():
                act.wait_ge(sem("small_in"), 16 * 8)
                copy(w_small[0][:, :, :, :].rearrange("p l k n -> p (l k n)"), w_small_in).then_inc(sem("init_act"), 1)
                f(neg_a[:, :], a_log[:, :], ACT.Exp).then_inc(sem("init_act"), 1)
                act.wait_ge(sem("lam_dots"), 1)
                f(lam_e[:, :, :], lam_e[:, :, :], ACT.Exp).then_inc(sem("init_act"), 1)

            def norm_squares(layer, s):
                i = 4 * layer + NORM_NO.get(s, 0)
                src, junk = x, [xn[:, 0, :], xn[:, 1, :]]
                if s == "norm_mem":
                    src, junk = v3(mem_tok, NB), [W0, W1]
                    act.wait_ge(sem("mem_in"), 16 * (layer + 1))
                    act.wait_ge(sem("obT_ready"), NB * (layer + 1))
                elif s == "norm_mix":
                    if layer == 0:
                        act.wait_ge(sem("x_in"), 16)
                    else:
                        act.wait_ge(sem("ffn_added"), 1)
                elif s != "final":
                    wait_evacuated(act, unit_index(layer, "out1" if s == "norm_x" else "x_o.1"))
                for b in range(NB):
                    last = f(junk[b], src[:, b, :], ACT.Square, accum_out=ss[:, b:b + 1])
                last.then_inc(sem("squares_ready"), 1)

            def norm_high(layer, s):
                i = 4 * layer + NORM_NO[s]
                dst = halves(memT if s == "norm_mem" else hT)[0]
                for j in range(2):
                    act.wait_ge(sem("norm_transposed"), 2 * i + j + 1)
                    copy(dst[:, j * 1024:(j + 1) * 1024], pb(4 + 2 * j, 2)).then_inc(sem("norm_hi"), 1)
                name, row = {"norm_mix": ("norm_mem", layer), "norm_mem": ("norm_x", layer), "norm_x": ("norm_ffn", layer),
                             "norm_ffn": ("norm_mix", layer + 1)}[s]
                nxt = t["norm_final"] if row == DEPTH else t[name][row]
                act.wait_ge(sem("xn_ready"), i + 1)
                act.dma_start(GAIN_ROW, nxt.partition_broadcast(P)).then_inc(sem("gain_in"), 16)

            def split(h):
                act.wait_ge(sem(f"half_in{h % RAW}"), 16 * (h // RAW + 1))
                if h >= SPLIT:
                    act.wait_ge(sem("half_used"), h - SPLIT + 1)
                copy(split_slot(h)[0], raw_slot(h)).then_inc(sem("half_hi"), 1)

            def ffn(groups, group0, blocks, uses, beside=None):
                wd = blocks * FF_UNIT

                def high(g, par, j, fresh=False):
                    n = g // 2 if isinstance(g, int) else g[1]
                    k = g if isinstance(g, int) else g[0]
                    act.wait_ge(sem(f"ffn_in{par}{j}"), (16 if j == 2 else 32) * (uses[par] + n + 1))
                    if not (isinstance(group0, int) and isinstance(k, int) and group0 + k == 0):
                        act.wait_ge(sem(f"ffn_used{j}"), group0 + k)
                    copy(ffn_split(j)[0], ffn_raw(par, j)).then_inc(sem(f"ffn_hi{j}"), 1)

                def hidden_high(g, par):
                    act.wait_ge(sem("hiddenT_done"), group0 + g + 1)
                    copy(rtile(2)[:, par * W:par * W + wd], psum[:, blocks * par, 0:wd]).then_inc(sem("hidden_hi"), 1)

                def nth(g, par, p, d):
                    if isinstance(g, int):
                        return g + d
                    return g + d, p + 1 + (par + d) // 2

                def group(g, par, p=None):
                    first = isinstance(g, int) and g == 0
                    last = isinstance(g, int) and g == groups - 1
                    if not first:
                        hidden_high(g - 1, 1 - par)
                    if not last:
                        high(nth(g, par, p, 1), 1 - par, 0)
                    act.wait_ge(sem("ffn_used1"), group0 + g + 1)
                    gate = psum[:, blocks * par:blocks * (par + 1), 0:FF_UNIT]
                    f(silu_g[par][:, 0:wd].rearrange("p (b n) -> p b n", b=blocks), gate, ACT.Silu) \
                        .then_inc(sem("silu_ready"), 1)
                    if not last:
                        high(nth(g, par, p, 1), 1 - par, 1)
                    high(nth(g, par, p, 0), par, 2)
                    if beside and isinstance(g, int) and g == groups - 2:
                        beside(g)
                    if last:
                        hidden_high(g, par)

                high(0, 0, 0)
                if beside:
                    beside(-1)
                high(0, 0, 1)
                if beside:
                    beside(0)
                pairs = (groups - 3) // 2
                group(0, 0)
                group(1, 1)
                with act.Fori(0, pairs) as p:
                    group(2 * p + 2, 0, p)
                    group(2 * p + 3, 1, p)
                for g in range(2 + 2 * pairs, groups):
                    group(g, g % 2)

            def small_out(n):
                act.wait_ge(sem("small_done"), n + 1)
                copy(small_T, psum[0:8, 5, 0:SEQ]).then_inc(sem("small_out"), 1)

            def gathered_high(n):
                act.wait_ge(sem("gathered"), n + 1)
                copy(halves(hgT)[0], pb(2, 2)).then_inc(sem("gathered_hi"), 1)

            def experts(group0, done, uses):
                n0 = done // N_EXP * (N_EXP + 1)

                def result(groups_done):
                    act.wait_ge(sem("ffn_used2"), group0 + groups_done)
                    copy(y_tok, pb(4, 2)).then_inc(sem("y_ready"), 1)

                with act.Fori(0, N_EXP) as e:
                    def beside(g):
                        if g == -1:
                            gathered_high(n0 + e)
                        elif g == 0:
                            result(EXP_GROUPS * e)
                        else:
                            act.wait_ge(sem("selectT_done"), done + e + 1)
                            copy(selectT, psum[:, 2, 0:SEQ]).then_inc(sem("selectT_out"), 1)

                    half = EXP_GROUPS // 2
                    ffn(EXP_GROUPS, group0 + EXP_GROUPS * e, 1, [half * e + uses[0], half * e + uses[1]], beside)
                gathered_high(n0 + N_EXP)
                result(EXP_GROUPS * N_EXP)

            target = {"gd_z": z, "da_v": da_v, "sb_k": sb_kT, "sb_v": sb_v, "x_k": x_kT, "x_v": x_v}

            for layer in range(DEPTH):
                for s in ORDER:
                    if s == "norm_mix":
                        if layer:
                            for j in range(2):
                                act.wait_ge(sem(f"ffn_used{j}"), DENSE_GROUPS)
                        for h in range(3):
                            split(4 * len(CHUNKS) * layer + h)
                    u, _, end = piece_of(layer, s) if "#" in s else ("", 0, False)
                    for h in halves_ahead(layer, s):
                        split(h)
                    if u[:4] == "br_c":
                        i = int(u[-1])
                        act.wait_ge(sem("merged_sum"), 2 * layer + i + 1)
                        copy(halves(mergedT)[0][:, i * 1024:(i + 1) * 1024], merged[:, i * 1024:(i + 1) * 1024]) \
                            .then_inc(sem("merged_hi"), 1)
                    elif end and UNITS[u][4] == "act":
                        wait_computed(act, layer, u)
                        src = pb(unit_banks(layer, u), 2)
                        done = sem("unit_out_act")
                        if u in ("gd_q", "gd_k", "gd_v"):
                            if u == "gd_q":
                                act.wait_ge(sem("pads_ready"), layer + 1)
                            part = ("gd_q", "gd_k", "gd_v").index(u)
                            f(conv_in[:, 4 * part:4 * part + 4, 3:], v3(src, 4), ACT.Copy).then_inc(done, 1)
                        elif u in ("sb_q", "x_q"):
                            f(sb_qT, src, ACT.Copy, scale=float(SB_DIM) ** -0.5).then_inc(done, 1)
                        elif u[:4] == "gate":
                            if u == "gate_a0":
                                act.wait_ge(sem("da_probsT"), NB * (layer + 1))
                            elif u == "gate_c0":
                                act.wait_ge(sem("tu_ready"), 13 * (layer + 1))
                            f(gate_tiles[u], src, ACT.Sigmoid).then_inc(done, 1)
                        else:
                            copy(target[u], src).then_inc(done, 1)
                    elif u:
                        pass
                    elif s in NORM_NO:
                        norm_squares(layer, s)
                        norm_high(layer, s)
                        if s == "norm_mix" and layer == 0:
                            once()
                    elif s == "ab":
                        small_out(layer)
                    elif s[:5] == "conv_":
                        part = "qkv".index(s[5])
                        n = 3 * layer + part
                        act.wait_ge(sem("conv_taps"), n + 1)
                        if part:
                            act.wait_ge(sem("conv_ready"), n)
                        f(scratch, conv_out[:, part * 1024:(part + 1) * 1024], ACT.Sigmoid).then_inc(sem("conv_sig"), 1)
                    elif s == "gd_tok":
                        for part in range(3):
                            act.wait_ge(sem("gd_tok_done"), 3 * layer + part + 1)
                            copy(tile(16 + part), pb(6 if part == 1 else 4, 2)).then_inc(sem("gd_tok_out"), 1)
                    elif s == "gd_gate":
                        act.wait_ge(sem("ab_out"), layer + 1)
                        nc.scalar.preload_act_table_set("natural_log_exp_and_others")
                        step(f(s16[:, 5, 0:8], s16[:, 4, 0:8], ACT.Exp, scale=-1.0))
                        step(f(s16[:, 2, 0:8], s16[:, 1, 0:8], ACT.Abs))
                        step(f(s16[:, 2, 0:8], s16[:, 2, 0:8], ACT.Exp, scale=-1.0))
                        f(s16[:, 3, 0:8], s16[:, 2, 0:8], ACT.Ln, bias=c("ones", 0, 1)).then_inc(sem("gates_act"), 1)
                    elif s == "gd_scale":
                        act.wait_ge(sem("decay_logs"), layer + 1)
                        f(decayT, decayT, ACT.Exp)
                        f(s16[:, 8, 8:16], s16[:, 8, 0:8], ACT.Exp)
                        f(s16[:, 9, 8:16], s16[:, 9, 0:8], ACT.Exp).then_inc(sem("decay_exp"), 1)
                    elif s == "gd_T":
                        for i, dst in enumerate((knT, kbT, qnT, qgT)):
                            act.wait_ge(sem("gd_T_done"), 4 * layer + i + 1)
                            copy(dst, pb(4 + 2 * (i % 2), 1 if i == 3 else 2)).then_inc(sem("gd_T_out"), 1)
                    elif s == "da_T":
                        for i, dst in enumerate((da_qT, da_kT)):
                            act.wait_ge(sem("da_T_done"), 2 * layer + i + 1)
                            copy(dst, pb(4 + 2 * i, 2)).then_inc(sem("da_T_out"), 1)
                    elif s == "gd_LA":
                        act.wait_ge(sem("gd_LA_done"), 3 * layer + 3)
                        copy(l_, pb(4, 2)).then_inc(sem("l_ready"), 1)
                    elif s[:5] == "inv_m":
                        act.wait_ge(sem("m1_done"), 6 * layer + int(s[-1]) + 1)
                        copy(m1, pb(4, 2)).then_inc(sem("m1_out"), 1)
                    elif s[:5] == "da_sc":
                        i = int(s[-1])
                        wd = (i + 1) * P
                        act.wait_ge(sem("da_max"), NB * layer + i + 1)
                        for j in range(8):
                            p = W23[:, j * wd:(j + 1) * wd]
                            last = f(p, p, ACT.Exp, bias=s16b[:, 1, j:j + 1], accum_out=s16b[:, 2, j:j + 1])
                        last.then_inc(sem("da_exp"), 1)
                    elif s[:5] == "da_pT":
                        i = int(s[-1])
                        wd = (i + 1) * P
                        act.wait_ge(sem("da_probsT"), NB * layer + i + 1)
                        copy(W0[:, 0:4 * wd], pb(4, 2)[:, 0:4 * wd]).then_inc(sem("da_probsT_out"), 1)
                    elif s == "da_out":
                        act.wait_ge(sem("da_oT_done"), layer + 1)
                        f(halves(oaT)[0], pb(4, 2), ACT.Copy, scale=gain[:, layer:layer + 1]).then_inc(sem("oaT_hi"), 1)
                    elif s[:5] == "sb_sc":
                        i = int(s[-1])
                        wd = (i + 1) * P
                        p = W2[:, 0:4 * wd]
                        act.wait_ge(sem("sb_scores"), NB * layer + i + 1)
                        wait_evacuated(act, unit_index(layer, "br_a.1"))
                        nc.scalar.preload_act_table_set("natural_log_exp_and_others")
                        step(f(p, pb(4, 2)[:, 0:4 * wd], ACT.Abs))
                        step(f(p, p, ACT.Exp, scale=-1.0))
                        f(p, p, ACT.Ln, bias=c("ones", 0, 1)).then_inc(sem("sb_ln"), 1)
                        act.wait_ge(sem("sb_log"), NB * layer + i + 1)
                        f(p, W3[:, 0:4 * wd], ACT.Exp).then_inc(sem("sb_probs"), 1)
                    elif s[:5] == "sb_pT":
                        i = int(s[-1])
                        wd = (i + 1) * P
                        act.wait_ge(sem("sb_probsT"), NB * layer + i + 1)
                        copy(W0[:, 0:4 * wd], pb(4, 2)[:, 0:4 * wd]).then_inc(sem("sb_probsT_out"), 1)
                        if i == NB - 1:
                            act.wait_ge(sem("tu_ready"), 13 * (layer + 1))
                            f(l_, z, ACT.Sigmoid).then_inc(sem("z_sig"), 1)
                    elif s[:5] == "sb_pv":
                        i = int(s[-1])
                        act.wait_ge(sem("sb_oT_done"), NB * layer + i + 1)
                        copy(v3(halves(obT)[0], 4)[:, :, i * P:(i + 1) * P], v3(psum[:, 6, :], 4)).then_inc(sem("obT_hi"), 1)
                    elif s[:4] == "x_sc":
                        i = int(s[-1])
                        act.wait_ge(sem("x_max"), NB * layer + i + 1)
                        for j in range(H):
                            last = f(x_probs[i][:, j * SEQ:(j + 1) * SEQ], pb(4 + 2 * i, 2)[:, j * SEQ:(j + 1) * SEQ],
                                     ACT.Exp, bias=s16b[:, 4, 4 * i + j:4 * i + j + 1],
                                     accum_out=s16b[:, 5, 4 * i + j:4 * i + j + 1])
                        last.then_inc(sem("x_exp"), 1)
                    elif s[:4] == "x_pT":
                        i = int(s[-1])
                        act.wait_ge(sem("x_probsT"), NB * layer + i + 1)
                        copy(x_probsT[i], pb(2 * i, 2)).then_inc(sem("x_probsT_out"), 1)
                    elif s[:4] == "x_pv":
                        i = int(s[-1])
                        act.wait_ge(sem("x_oT_done"), NB * layer + i + 1)
                        copy(v3(halves(oxT)[0], 4)[:, :, i * P:(i + 1) * P], v3(psum[:, 4 + 2 * i, :], 4)).then_inc(sem("oxT_hi"), 1)
                    elif s == "gd_scan":
                        for i, n in enumerate((1, 5)):
                            act.wait_ge(sem("scan_done"), 6 * layer + n)
                            copy(v_new[:, i * W:(i + 1) * W], psum[:, 4, :]).then_inc(sem("scan_out_act"), 1)
                        act.wait_ge(sem("scan_done"), 6 * (layer + 1))
                        act.dma_start(mem_tok.rearrange("p (b d) -> p b d", b=NB),
                                      t["mem"][0].rearrange("(b p) d -> p b d", p=P)).then_inc(sem("mem_in"), 16)
                    elif s == "gd_out":
                        act.wait_ge(sem("gd_oT_done"), layer + 1)
                        f(halves(ocT)[0], pb(6, 2), ACT.Copy, scale=gain[:, 2 + layer:3 + layer]).then_inc(sem("ocT_hi"), 1)
                    elif s == "ffn":
                        act.wait_ge(sem("half_used"), 4 * len(CHUNKS) * (layer + 1))
                        if layer == 0:
                            ffn(DENSE_GROUPS, 0, NB, [0, 0])
                        else:
                            small_out(DEPTH)
                            act.wait_ge(sem("top_diff"), 1)
                            f(top[:, 11, 0:2], top[:, 10, 0:2], ACT.Exp).then_inc(sem("top_exp"), 1)
                            uses = [(DENSE_GROUPS + 1) // 2, DENSE_GROUPS // 2]
                            f(selectT, c("ones"), ACT.Copy, scale=0.0).then_inc(sem("selectT_out"), 1)
                            experts(DENSE_GROUPS, 0, uses)
                            act.wait_ge(sem("overflow_known"), 1)
                            with act.If(act.value_load(overflow[0:1, 0:1], min_val=0, max_val=1) > 0):
                                experts(DENSE_GROUPS + EXP_GROUPS * N_EXP, N_EXP,
                                        [n + EXP_GROUPS // 2 * N_EXP for n in uses])
                                act.wait_ge(sem("x_added"), 2 * (N_EXP + 1))
            act.wait_ge(sem("x_added"), N_EXP + 1)
            norm_squares(DEPTH, "final")

        @block.vector
        def _(dve):
            v = nc.vector
            steps = [0]

            def step(ins):
                steps[0] += 1
                ins.then_inc(sem("dve_step"), 1)
                dve.wait_ge(sem("dve_step"), steps[0])

            def tt(o, a, b, op):
                return v.tensor_tensor(o, a, b, op)

            def power(layer, s, src, width, scale):
                i = POW.index((layer, s))
                v.tensor_scalar(pow_in[:, 0:width], src, scale, EPS, ALU.mult, ALU.add).then_inc(sem("pow_in"), 1)
                dve.wait_ge(sem("pow_out"), i + 1)

            def norm_scale(layer, s):
                i = 4 * layer + NORM_NO.get(s, 0)
                dve.wait_ge(sem("squares_ready"), i + 1)
                power(layer, s, ss[:, :], NB, 1.0 / D)
                src, dst = (v3(mem_tok, NB),) * 2 if s == "norm_mem" else (x, xn)
                dve.wait_ge(sem("gain_in"), 16 * (i + 1))
                for b in range(NB):
                    last = v.scalar_tensor_tensor(dst[:, b, :], src[:, b, :], pow_out[:, b:b + 1], GAIN_ROW, ALU.mult,
                                                  ALU.mult)
                return last

            def low(where, cols, full):
                hi = stored(where[0], where[2])[:, cols]
                return v.tensor_tensor(halves(where)[1][:, cols], full, hi, ALU.subtract)

            def norm(layer, s):
                i = 4 * layer + NORM_NO[s]
                norm_scale(layer, s).then_inc(sem("xn_ready"), 1)
                where = memT if s == "norm_mem" else hT
                if s == "norm_ffn" and layer == 1:
                    where = hT_router
                dve.wait_ge(sem("norm_hi"), 2 * i + 2)
                for j in range(2):
                    last = low(where, slice(j * 1024, (j + 1) * 1024), pb(4 + 2 * j, 2))
                last.then_inc(sem("norm_out"), 1)

            def split(h):
                dve.wait_ge(sem("half_hi"), h + 1)
                tt(split_slot(h)[1], raw_slot(h), split_slot(h, False)[0], ALU.subtract).then_inc(sem("half_lo"), 1)

            def level_T(layer, it):
                tt(v3(bT, 8), v3(lT, 8), rep(c("levelT", (it + 1) * P, (it + 2) * P), 8), ALU.mult) \
                    .then_inc(sem("bT_ready"), 1)

            def conv(layer, part):
                n = 3 * layer + part
                wait_evacuated(dve, unit_index(layer, ("gd_q", "gd_k", "gd_v")[part]))
                for j in range(4):
                    for ch in range(4 * part, 4 * part + 4):
                        tap = gain[:, 4 + layer * 48 + j * 12 + ch:5 + layer * 48 + j * 12 + ch]
                        o = conv_out[:, ch * SEQ:(ch + 1) * SEQ]
                        src = conv_in[:, ch, j:j + SEQ]
                        if j == 0:
                            last = v.tensor_scalar(o, src, tap, None, ALU.mult)
                        else:
                            last = v.scalar_tensor_tensor(o, src, tap, o, ALU.mult, ALU.add)
                    if j < 3:
                        step(last)
                last.then_inc(sem("conv_taps"), 1)
                o = conv_out[:, part * 1024:(part + 1) * 1024]
                dve.wait_ge(sem("conv_sig"), n + 1)
                tt(o, o, scratch, ALU.mult).then_inc(sem("conv_ready"), 1)

            def rope(layer, s):
                tab = s[3]
                dst = W0 if tab == "q" else W1
                src = pb(unit_banks(layer, s), 2)
                wait_computed(dve, layer, s)
                sin = W2
                for b in range(NB):
                    cs = c("cos_" + tab, b * DA_DIM, (b + 1) * DA_DIM)
                    sn = c("sin_" + tab, b * DA_DIM, (b + 1) * DA_DIM)
                    part = src[:, b * W:(b + 1) * W]
                    tt(v3(dst[:, b * W:(b + 1) * W], 8), v3(part, 8), rep(cs, 8), ALU.mult)
                    for half in range(2):
                        o = v3(sin[:, b * W:(b + 1) * W], 8)[:, :, half * 32:half * 32 + 32]
                        i = v3(part, 8)[:, :, (1 - half) * 32:(1 - half) * 32 + 32]
                        last = tt(o, i, rep(sn[:, half * 32:half * 32 + 32], 8), ALU.mult)
                last.then_inc(sem("unit_out_dve"), 1)
                wait_evacuated(dve, unit_index(layer, s))
                tt(dst, dst, sin[:, :], ALU.add).then_inc(sem("roped"), 1)

            def ffn(groups, group0, blocks, beside=None):
                wd = blocks * FF_UNIT

                def low_half(g, j):
                    dve.wait_ge(sem(f"ffn_hi{j}"), group0 + g + 1)
                    par = parity[j]
                    parity[j] = 1 - par
                    tt(ffn_split(j)[1], ffn_raw(par, j), ffn_split(j, False)[0], ALU.subtract).then_inc(sem(f"ffn_lo{j}"), 1)

                def hidden_low(g, par):
                    dve.wait_ge(sem("hidden_hi"), group0 + g + 1)
                    q = slice(par * W, par * W + wd)
                    tt(rtile(3)[:, q], psum[:, blocks * par, 0:wd], stored(2)[:, q], ALU.subtract).then_inc(sem("hidden_lo"), 1)

                def group(g, par):
                    first = isinstance(g, int) and g == 0
                    last = isinstance(g, int) and g == groups - 1
                    if not first:
                        hidden_low(g - 1, 1 - par)
                    if not last:
                        low_half(g + 1, 0)
                    dve.wait_ge(sem("silu_ready"), group0 + g + 1)
                    up = psum[:, blocks * par:blocks * (par + 1), FF_UNIT:2 * FF_UNIT]
                    tt(v3(hid[par][:, 0:wd], blocks), v3(silu_g[par][:, 0:wd], blocks), up, ALU.mult) \
                        .then_inc(sem("hidden_ready"), 1)
                    if not last:
                        low_half(g + 1, 1)
                    low_half(g, 2)
                    if beside and isinstance(g, int) and g in (1, groups - 2):
                        beside(g)
                    if last:
                        hidden_low(g, par)

                parity = [0, 0, 0]
                low_half(0, 0)
                if beside:
                    beside(-1)
                low_half(0, 1)
                ffn_loop(dve, groups, group)

            def experts(group0, done, ranks):
                n0 = done // N_EXP * (N_EXP + 1)

                def column(which, b, e):
                    return routing[:, which, b, e:e + 1] if isinstance(e, int) else routing[:, which, b, bass.ds(e, 1)]

                def choose(e):
                    for b in range(NB):
                        last = v.tensor_scalar(select[:, b * CAP:(b + 1) * CAP], c("iota"), column(ranks, b, e), None,
                                               ALU.is_equal)
                    last.then_inc(sem("select_ready"), 1)

                def gathered_low(n):
                    dve.wait_ge(sem("gathered_hi"), n + 1)
                    low(hgT, slice(0, 1024), pb(2, 2)).then_inc(sem("gathered_lo"), 1)

                def add(e):
                    dve.wait_ge(sem("scattered"), n0 + e + 1)
                    for b in range(NB):
                        last = v.scalar_tensor_tensor(x[:, b, :], pb(2 + 4 * b, 2), column(2, b, e), x[:, b, :],
                                                      ALU.mult, ALU.add)
                    last.then_inc(sem("x_added"), 1)

                choose(0)
                with dve.Fori(0, N_EXP) as e:
                    def beside(g):
                        if g == 1:
                            add(e)
                        elif g == EXP_GROUPS - 2:
                            dve.wait_ge(sem("selectT_done"), done + e + 1)
                            choose(e + 1)
                        else:
                            gathered_low(n0 + e)

                    ffn(EXP_GROUPS, group0 + EXP_GROUPS * e, 1, beside)
                gathered_low(n0 + N_EXP)
                add(N_EXP)

            def once():
                dve.wait_ge(sem("small_in"), 16 * 8)
                for i in range(2):
                    step(tt(lam_in[:, 2 * i, :], lam_in[:, 2 * i, :], lam_in[:, 2 * i + 1, :], ALU.mult))
                v.tensor_reduce(lam_e[:, 0, :], v3(lam_in[:, 0, :], DEPTH), X, ALU.add)
                v.tensor_reduce(lam_e[:, 1, :], v3(lam_in[:, 2, :], DEPTH), X, ALU.add).then_inc(sem("lam_dots"), 1)
                dve.wait_ge(sem("init_act"), 3)
                tt(w_small[1][:, :, :, :].rearrange("p l k n -> p (l k n)"), w_small_in,
                   w_small[0][:, :, :, :].rearrange("p l k n -> p (l k n)").bitcast(F32), ALU.subtract)
                v.tensor_scalar(neg_a[:, :], neg_a[:, :], -1.0, None, ALU.mult)
                step(tt(neg_lam[:, :], lam_e[:, 1, :], lam_e[:, 0, :], ALU.subtract))
                for layer in range(DEPTH):
                    last = v.tensor_scalar(neg_lam[:, layer:layer + 1], neg_lam[:, layer:layer + 1], -LAM_INIT[layer], None,
                                           ALU.add)
                step(last)
                dve.wait_ge(sem("gains_transposed"), 1)
                v.tensor_copy(gain[:, 4:100], psum[:, 3, P:P + 96])
                v.tensor_copy(gain[:, 2:4], psum[:, 3, 2:4])
                for layer in range(DEPTH):
                    last = v.tensor_scalar(gain[:, layer:layer + 1], psum[:, 3, layer:layer + 1], 1.0 - LAM_INIT[layer], None,
                                           ALU.mult)
                last.then_inc(sem("gains_read"), 1)
                dve.wait_ge(sem("gains_read"), 1)

            for layer in range(DEPTH):
                for s in ORDER:
                    if s == "norm_mix":
                        for h in range(3):
                            split(4 * len(CHUNKS) * layer + h)
                    u, _, end = piece_of(layer, s) if "#" in s else ("", 0, False)
                    for h in halves_ahead(layer, s):
                        split(h)
                    if end and u in ("da_q", "da_k"):
                        rope(layer, u)
                    elif end and UNITS[u][4] == "dve":
                        g = unit_index(layer, u)
                        src = pb(unit_banks(layer, u), 2)
                        wait_computed(dve, layer, u)
                        if u[:2] == "br":
                            i = int(u[-1])
                            gate = gate_tiles[f"gate_{u[3]}{i}"]
                            dst = merged[:, i * 1024:(i + 1) * 1024]
                            wait_evacuated(dve, unit_index(layer, f"gate_{u[3]}{i}"))
                            if u[3] == "a":
                                tt(dst, src, gate, ALU.mult).then_inc(sem("unit_out_dve"), 1)
                            else:
                                tt(gate, src, gate, ALU.mult).then_inc(sem("unit_out_dve"), 1)
                                wait_evacuated(dve, g)
                                last = tt(dst, dst, gate, ALU.add)
                                if u[3] == "c":
                                    last.then_inc(sem("merged_sum"), 1)
                                    dve.wait_ge(sem("merged_hi"), 2 * layer + i + 1)
                                    low(mergedT, slice(i * 1024, (i + 1) * 1024), dst).then_inc(sem("merged_ready"), 1)
                        else:
                            half = int(u[-1])
                            xs = x[:, :, half * W:(half + 1) * W]
                            tt(xs, xs, v3(src, 2), ALU.add).then_inc(sem("unit_out_dve"), 1)
                    elif u:
                        pass
                    elif s in NORM_NO:
                        norm(layer, s)
                        if s == "norm_mix":
                            if layer == 0:
                                once()
                            v.memset(conv_in[:, :, 0:3], 0.0).then_inc(sem("pads_ready"), 1)
                    elif s[:5] == "conv_":
                        conv(layer, "qkv".index(s[5]))
                    elif s == "ab_T":
                        dve.wait_ge(sem("ab_done"), layer + 1)
                        src = v3(psum[:, 4, 0:16], 2)
                        tt(v3(s16[:, 1, 0:8], 2), src[:, :, 0:4], rep(dt_bias[:, layer * H:(layer + 1) * H], 2), ALU.add)
                        v.tensor_copy(v3(s16[:, 4, 0:8], 2), src[:, :, 4:8]).then_inc(sem("ab_out"), 1)
                    elif s == "gd_gate":
                        dve.wait_ge(sem("gates_act"), layer + 1)
                        step(v.scalar_tensor_tensor(s16[:, 2, 0:8], s16[:, 1, 0:8], 0.0, s16[:, 3, 0:8], ALU.max, ALU.add))
                        tt(v3(s16[:, 0, 0:8], 2), v3(s16[:, 2, 0:8], 2), rep(neg_a[:, layer * H:(layer + 1) * H], 2),
                           ALU.mult).then_inc(sem("g_ready"), 1)
                        step(v.tensor_scalar(s16[:, 5, 0:8], s16[:, 5, 0:8], 1.0, None, ALU.add))
                        step(v.reciprocal(s16[:, 4, 0:8], s16[:, 5, 0:8]))
                    elif s == "gd_scale":
                        beta, eg, ekd = s16[:, 4, 0:8], s16[:, 8, 8:16], s16[:, 9, 8:16]
                        dve.wait_ge(sem("gd_tok_out"), 3 * layer + 3)
                        for i, src in enumerate((qn, kn)):
                            step(tt(scratch, src, src, ALU.mult))
                            step(v.tensor_reduce(s16[:, 6, 8 * i:8 * i + 8], v3(scratch, 8), X, ALU.add))
                        dve.wait_ge(sem("gc_done"), 2 * layer + 2)
                        spread = v3(pb(6, 2), 8)
                        step(v.tensor_copy(s16[:, 8, 0:8], psum[:, 4, 0:8]))
                        step(tt(v3(decayT, 8), spread, each(s16[:, 8, 0:8], P), ALU.subtract))
                        v.tensor_scalar(decayT, decayT, 0.0, None, ALU.min)
                        tt(s16[:, 9, 0:8], spread[:, :, P - 1], s16[:, 8, 0:8], ALU.subtract).then_inc(sem("decay_logs"), 1)
                        power(layer, s, s16[:, 6, :], 16, 1.0)
                        step(v.tensor_scalar(s16[:, 7, 0:8], pow_out[:, 0:8], float(SB_DIM) ** -0.5, None, ALU.mult))
                        tt(v3(qn, 8), v3(qn, 8), each(s16[:, 7, 0:8], P), ALU.mult)
                        step(tt(v3(kn, 8), v3(kn, 8), each(pow_out[:, 8:16], P), ALU.mult))
                        tt(v3(kb, 8), v3(kn, 8), each(beta, P), ALU.mult)
                        tt(v3(vb, 8), v3(vb, 8), each(beta, P), ALU.mult).then_inc(sem("gd_scaled"), 1)
                        dve.wait_ge(sem("decay_exp"), layer + 1)
                        dve.wait_ge(sem("gd_scaled"), layer + 1)
                        step(tt(v3(kbg, 4), v3(kb[:, W:], 4), each(eg[:, 4:8], P), ALU.mult))
                        v.tensor_scalar(kbg, kbg, -1.0, None, ALU.mult)
                        step(tt(v3(decayT, 8), v3(decayT, 8), rep(c("triu"), 8), ALU.mult))
                    elif s == "gd_T":
                        eg, ekd = s16[:, 8, 8:16], s16[:, 9, 8:16]
                        dve.wait_ge(sem("gd_T_done"), 4 * layer + 3)
                        tt(v3(qn[:, W:], 4), v3(qn[:, W:], 4), each(eg[:, 4:8], P), ALU.mult).then_inc(sem("qg_ready"), 1)
                        tt(v3(kn[:, 0:W], 4), v3(kn[:, 0:W], 4), each(ekd[:, 0:4], P), ALU.mult).then_inc(sem("kd_ready"), 1)
                    elif s == "gd_LA":
                        dve.wait_ge(sem("gd_LA_done"), 3 * layer + 1)
                        step(tt(lT, pb(4, 2), decayT, ALU.mult))
                        tt(v3(lT, 8), v3(lT, 8), rep(c("striu"), 8), ALU.mult).then_inc(sem("lT_ready"), 1)
                        dve.wait_ge(sem("gd_LA_done"), 3 * layer + 2)
                        tt(intraT, pb(6, 2), decayT, ALU.mult).then_inc(sem("intra_ready"), 1)
                        dve.wait_ge(sem("lT_ready"), layer + 1)
                        dve.wait_ge(sem("l_ready"), layer + 1)
                        tt(v3(uT, 8), v3(lT, 8), rep(c("levelT", 0, P), 8), ALU.mult)
                        step(tt(v3(t_, 8), v3(l_, 8), rep(c("level", 0, P), 8), ALU.mult))
                        for m in (uT, t_):
                            v.scalar_tensor_tensor(v3(m, 8), v3(m, 8), -1.0, rep(c("ident"), 8), ALU.mult, ALU.add) \
                                .then_inc(sem("tu_ready"), 1)
                    elif s == "inv_m0":
                        level_T(layer, 0)
                    elif s[:5] == "inv_t":
                        it = int(s[-1])
                        n = 6 * layer + it
                        if it < 5:
                            dve.wait_ge(sem("m1_done"), n + 1)
                            level_T(layer, it + 1)
                        done = 11 * layer + 2 * it + 1
                        if it < 5:
                            dve.wait_ge(sem("tmu_done"), done)
                            tt(t_, t_, pb(6, 2), ALU.subtract).then_inc(sem("tu_ready"), 1)
                            done += 1
                        dve.wait_ge(sem("tmu_done"), done)
                        tt(uT, uT, pb(4, 2), ALU.subtract).then_inc(sem("tu_ready"), 1)
                    elif s[:5] == "da_sc":
                        i = int(s[-1])
                        wd = (i + 1) * P
                        n = NB * layer + i + 1
                        dve.wait_ge(sem("da_scores"), n)
                        for half in range(2):
                            last = tt(v3(W23[:, half * 4 * wd:(half + 1) * 4 * wd], 4), v3(pb(4 + 2 * half, 2), 4)[:, :, 0:wd],
                                      rep(c("causal", SEQ - wd, SEQ), 4), ALU.add)
                        step(last)
                        p8 = v3(W23[:, 0:8 * wd], 8)
                        step(v.tensor_reduce(s16b[:, 0, 0:8], p8, X, ALU.max))
                        v.tensor_scalar(s16b[:, 1, 0:8], s16b[:, 0, 0:8], -1.0, None, ALU.mult).then_inc(sem("da_max"), 1)
                        dve.wait_ge(sem("da_exp"), n)
                        step(v.reciprocal(s16b[:, 3, 0:8], s16b[:, 2, 0:8]))
                        step(v.tensor_scalar(s16b[:, 3, 4:8], s16b[:, 3, 4:8], neg_lam[:, layer:layer + 1], None, ALU.mult))
                        step(tt(p8, p8, each(s16b[:, 3, 0:8], wd), ALU.mult))
                        tt(W23[:, 0:4 * wd], W23[:, 0:4 * wd], W23[:, 4 * wd:8 * wd], ALU.add).then_inc(sem("da_probs"), 1)
                    elif s[:5] == "da_pv":
                        i = int(s[-1])
                        dve.wait_ge(sem("da_o_done"), NB * layer + i + 1)
                        v.tensor_copy(W1[:, i * W:(i + 1) * W], psum[:, 6, :]).then_inc(sem("da_o_out"), 1)
                    elif s == "da_out":
                        dve.wait_ge(sem("da_o_out"), NB * (layer + 1))
                        step(tt(W0, W1, W1, ALU.mult))
                        step(v.tensor_reduce(s16b[:, 6, 0:8], v3(W0, 8), X, ALU.add))
                        power(layer, s, s16b[:, 6, 0:8], 8, 1.0 / P)
                        tt(v3(W1, 8), v3(W1, 8), each(pow_out[:, 0:8], P), ALU.mult).then_inc(sem("da_normed"), 1)
                        dve.wait_ge(sem("oaT_hi"), layer + 1)
                        v.scalar_tensor_tensor(halves(oaT)[1], pb(4, 2), gain[:, layer:layer + 1], stored(oaT[0]), ALU.mult,
                                               ALU.subtract).then_inc(sem("oaT_ready"), 1)
                    elif s[:5] == "sb_sc":
                        i = int(s[-1])
                        wd = (i + 1) * P
                        n = NB * layer + i + 1
                        scores, lg = pb(4, 2)[:, 0:4 * wd], W3[:, 0:4 * wd]
                        dve.wait_ge(sem("sb_ln"), n)
                        step(v.scalar_tensor_tensor(lg, scores, 0.0, W2[:, 0:4 * wd], ALU.max, ALU.add))
                        step(tt(v3(lg, 4), v3(lg, 4), rep(c("strict01", SEQ - wd, SEQ), 4), ALU.mult))
                        for h in range(H):
                            rev = W3[:, h * wd:(h + 1) * wd][:, ::-1]
                            last = v.tensor_tensor_scan(W1[:, h * wd:(h + 1) * wd][:, ::-1], c("ones", 0, wd), rev, 0.0,
                                                        ALU.mult, ALU.add)
                        step(last)
                        step(tt(lg, scores, W1[:, 0:4 * wd], ALU.subtract))
                        tt(v3(lg, 4), v3(lg, 4), rep(c("strict_neg", SEQ - wd, SEQ), 4), ALU.add).then_inc(sem("sb_log"), 1)
                    elif s[:5] == "sb_pv":
                        i = int(s[-1])
                        q = slice(i * P, (i + 1) * P)
                        if i == NB - 1:
                            dve.wait_ge(sem("z_sig"), layer + 1)
                            tt(z, z, l_, ALU.mult).then_inc(sem("z_gate"), 1)
                        dve.wait_ge(sem("obT_hi"), NB * layer + i + 1)
                        tt(v3(halves(obT)[1], 4)[:, :, q], v3(psum[:, 6, :], 4), v3(stored(obT[0]), 4)[:, :, q],
                           ALU.subtract).then_inc(sem("obT_ready"), 1)
                    elif s[:4] == "x_sc":
                        i = int(s[-1])
                        n = NB * layer + i + 1
                        dve.wait_ge(sem("x_scores"), n)
                        own = slice(4 * i, 4 * i + 4)
                        step(v.tensor_reduce(s16b[:, 7, own], v3(pb(4 + 2 * i, 2), 4), X, ALU.max))
                        v.tensor_scalar(s16b[:, 4, own], s16b[:, 7, own], -1.0, None, ALU.mult).then_inc(sem("x_max"), 1)
                    elif s[:4] == "x_pT":
                        i = int(s[-1])
                        own = slice(4 * i, 4 * i + 4)
                        dve.wait_ge(sem("x_exp"), NB * layer + i + 1)
                        step(v.reciprocal(s16b[:, 0, own], s16b[:, 5, own]))
                        tt(v3(x_probs[i], 4), v3(x_probs[i], 4), each(s16b[:, 0, own], SEQ), ALU.mult) \
                            .then_inc(sem("x_probs"), 1)
                    elif s[:4] == "x_pv":
                        i = int(s[-1])
                        q = slice(i * P, (i + 1) * P)
                        dve.wait_ge(sem("oxT_hi"), NB * layer + i + 1)
                        tt(v3(halves(oxT)[1], 4)[:, :, q], v3(psum[:, 4 + 2 * i, :], 4), v3(stored(oxT[0]), 4)[:, :, q],
                           ALU.subtract).then_inc(sem("oxT_ready"), 1)
                    elif s == "gd_scan":
                        for n, dst, b in ((2, wT, 5), (3, state, 6), (4, gd_o[:, 0:W], 7), (6, gd_o[:, W:], 5)):
                            dve.wait_ge(sem("scan_done"), 6 * layer + n)
                            v.tensor_copy(dst, psum[:, b, :]).then_inc(sem("scan_out_dve"), 1)
                    elif s == "gd_out":
                        dve.wait_ge(sem("scan_out_dve"), 4 * (layer + 1))
                        step(tt(scratch, gd_o, gd_o, ALU.mult))
                        step(v.tensor_reduce(s16[:, 6, 0:8], v3(scratch, 8), X, ALU.add))
                        power(layer, s, s16[:, 6, 0:8], 8, 1.0 / P)
                        step(tt(v3(gd_o, 8), v3(gd_o, 8), each(pow_out[:, 0:8], P), ALU.mult))
                        dve.wait_ge(sem("z_gate"), layer + 1)
                        tt(gd_o, gd_o, z, ALU.mult).then_inc(sem("gd_normed"), 1)
                        dve.wait_ge(sem("ocT_hi"), layer + 1)
                        v.scalar_tensor_tensor(halves(ocT)[1], pb(6, 2), gain[:, 2 + layer:3 + layer], stored(ocT[0]), ALU.mult,
                                               ALU.subtract).then_inc(sem("ocT_ready"), 1)
                    elif s == "ffn" and layer == 0:
                        ffn(DENSE_GROUPS, 0, NB)
                        dve.wait_ge(sem("ffn_used2"), DENSE_GROUPS)
                        xf = x.rearrange("p b d -> p (b d)")
                        tt(xf, xf, pb(4, 4), ALU.add).then_inc(sem("ffn_added"), 1)
                    elif s == "ffn":
                        iota8 = c("iota8")
                        dve.wait_ge(sem("router_done"), 1)
                        step(v.tensor_copy(top[:, 1, :], psum[:, 4, 0:16]))
                        for b in range(NB):
                            lg, mx = top[:, 1, b * 8:b * 8 + 8], top[:, 2, b * 8:b * 8 + 8]
                            step(v.max(mx, lg))
                            step(v.max_index(top_i[:, b, :], mx, lg))
                            step(v.tensor_copy(top[:, 9, b * 8:b * 8 + 8], top_i[:, b, :]))
                            for j in range(2):
                                step(v.tensor_scalar(top[:, 3 + j, b * 8:b * 8 + 8], iota8, top[:, 9, b * 8 + j:b * 8 + j + 1],
                                                     None, ALU.is_equal))
                        tops = v3(top[:, 2, :], 2)
                        tt(top[:, 10, 0:2], tops[:, :, 1], tops[:, :, 0], ALU.subtract).then_inc(sem("top_diff"), 1)
                        tt(top[:, 0, :], top[:, 3, :], top[:, 4, :], ALU.add).then_inc(sem("chosen_ready"), 1)
                        dve.wait_ge(sem("top_exp"), 1)
                        step(v.tensor_scalar(top[:, 12, 0:2], top[:, 11, 0:2], 1.0, None, ALU.add))
                        step(v.reciprocal(top[:, 13, 0:2], top[:, 12, 0:2]))
                        step(tt(top[:, 14, 0:2], top[:, 11, 0:2], top[:, 13, 0:2], ALU.mult))
                        for b in range(NB):
                            q = slice(b * 8, b * 8 + 8)
                            step(v.tensor_scalar(top[:, 5, q], top[:, 3, q], top[:, 13, b:b + 1], None, ALU.mult))
                            step(v.scalar_tensor_tensor(top[:, 6, q], top[:, 4, q], top[:, 14, b:b + 1], top[:, 5, q],
                                                        ALU.mult, ALU.add))
                        dve.wait_ge(sem("ranks_done"), 1)
                        step(v.scalar_tensor_tensor(top[:, 15, :], psum[:, 5, 0:16], 1.0, top[:, 0, :], ALU.add, ALU.mult))
                        v.memset(routing[:, 0:2, :, N_EXP:N_EXP + 1], -1.0)
                        v.memset(routing[:, 2, :, 0:1], 0.0)
                        by_block = v3(top[:, 15, :], 2)
                        v.tensor_scalar(routing[:, 0, :, 0:N_EXP], by_block, -1.0, None, ALU.add)
                        v.tensor_scalar(routing[:, 1, :, 0:N_EXP], by_block, -1.0 - CAP, None, ALU.add)
                        step(v.tensor_copy(routing[:, 2, :, 1:], v3(top[:, 6, :], 2)))
                        step(v.tensor_reduce(top[:, 16, 0:1], psum[:, 5, 16:24], X, ALU.max))
                        v.tensor_scalar(overflow[:, :], top[:, 16, 0:1], float(CAP), None, ALU.is_gt) \
                            .then_inc(sem("overflow_known"), 1)
                        dve.wait_ge(sem("overflow_known"), 1)
                        experts(DENSE_GROUPS, 0, 0)
                        with dve.If(dve.value_load(overflow[0:1, 0:1], min_val=0, max_val=1) > 0):
                            experts(DENSE_GROUPS + EXP_GROUPS * N_EXP, N_EXP, 1)
            last = norm_scale(DEPTH, "final")
            last.then_inc(sem("out_ready"), 1)


def constants():
    a = np.zeros((P, N_CONST), np.float32)

    def put(name, m):
        at, n = CONST[name]
        a[:, at:at + n] = m.reshape(P, n)

    p, j = np.arange(P)[:, None], np.arange(P)[None, :]
    k = np.arange(SEQ)[None, :]
    put("ident", (p == j).astype(np.float32))
    put("triu", (p <= j).astype(np.float32))
    put("striu", (p < j).astype(np.float32))
    put("ones", np.ones((P, SEQ), np.float32))
    put("causal", np.where(k <= p + P, 0.0, NEG).astype(np.float32))
    put("strict_neg", np.where(k < p + P, 0.0, NEG).astype(np.float32))
    put("strict01", (k < p + P).astype(np.float32))
    level = np.stack([((p // m) % 2 == 1) & (j // m == p // m - 1) for m in LEVELS], 1)
    put("level", level.astype(np.float32))
    put("levelT", np.stack([((j // m) % 2 == 1) & (p // m == j // m - 1) for m in LEVELS], 1).astype(np.float32))
    inv = (1.0 / (np.float32(10000.0) ** (np.arange(0, DA_DIM, 2, dtype=np.float32) / np.float32(DA_DIM)))).astype(np.float32)
    ang = np.arange(SEQ, dtype=np.float32)[:, None] * inv[None, :]
    cos, sin = np.cos(ang), np.sin(ang)
    for name, m in (("cos", np.concatenate([cos, cos], 1)), ("sin", np.concatenate([-sin, sin], 1))):
        m = m.reshape(NB, P, DA_DIM).transpose(1, 0, 2).astype(np.float32)
        put(name + "_k", m)
        put(name + "_q", m * np.float32(DA_DIM ** -0.5))
    put("iota", np.broadcast_to(np.arange(P, dtype=np.float32), (P, P)))
    put("nhalf", np.full((P, 16), -0.5, np.float32))
    put("iota8", np.broadcast_to(np.arange(8, dtype=np.float32), (P, 8)))
    return a


_INS = ["x", "mem", "norm_mix", "w_in", "gd_conv", "lam_q1", "lam_k1", "lam_q2", "lam_k2", "da_subln", "gd_a_log",
        "gd_dt_bias", "gd_norm", "w_br_a", "w_br_b", "w_br_c", "w_out", "norm_x", "norm_mem", "w_q_x", "w_kv_x", "w_o_x",
        "norm_ffn", "w_gate_dense", "w_up_dense", "w_down_dense", "w_router", "w_gate_exp", "w_up_exp", "w_down_exp",
        "norm_final"]


def kernel(**inputs):
    import concourse.bacc as _bacc
    from concourse.bass_utils import run_bass_kernel_spmd as _run

    nc = _bacc.Bacc("TRN2", target_bir_lowering=False, num_devices=1)
    arrays = {f"in_{name}_dram": np.ascontiguousarray(inputs[name]) for name in _INS}
    arrays["const_dram"] = constants()
    t = {}
    for name in _INS + ["const"]:
        key = "const_dram" if name == "const" else f"in_{name}_dram"
        a = arrays[key]
        t[name] = nc.dram_tensor(key, a.shape, mybir.dt.from_np(a.dtype), kind="ExternalInput").ap()
    out = nc.dram_tensor("out_0_dram", (1, SEQ, D), F32, kind="ExternalOutput").ap()
    hybrid_layers(nc, t, out)
    r = _run(nc, [arrays], core_ids=[0])
    return r.results[0]["out_0_dram"]
```
